# Optimizing a Trainium2 kernel written in Bass

```python
import jax, jax.numpy as jnp
from jax import lax
import numpy as np
import math

D_MODEL = 1024
BATCH = 1
SEQ = 512
DEPTH = 1

HEAD_DIM = 64
MIX_WIDTH = D_MODEL
ATTN_WIDTH = MIX_WIDTH // 2
ATTN_Q_HEADS = ATTN_WIDTH // HEAD_DIM
ATTN_KV_HEADS = 2
KV_WIDTH = ATTN_KV_HEADS * HEAD_DIM
WINDOW = 128
ATTN_BLOCK = 128
RWKV_WIDTH = MIX_WIDTH // 4
RWKV_HEADS = RWKV_WIDTH // HEAD_DIM
DECAY_LORA = 64
ICLR_LORA = 64
RWKV_LN_EPS = 64e-5
GLA_VAL_WIDTH = MIX_WIDTH // 4
GLA_HEADS = 4
GLA_VAL_DIM = GLA_VAL_WIDTH // GLA_HEADS
GLA_KEY_WIDTH = GLA_VAL_WIDTH // 2
GLA_KEY_DIM = GLA_KEY_WIDTH // GLA_HEADS
GLA_GATE_LORA = 16
GLA_GATE_NORMALIZER = 16.0
GLA_CHUNK = 64
IN_SPLITS = (ATTN_WIDTH, KV_WIDTH, KV_WIDTH, ATTN_WIDTH,
             3 * RWKV_WIDTH, RWKV_WIDTH,
             GLA_KEY_WIDTH, GLA_KEY_WIDTH, GLA_VAL_WIDTH, GLA_VAL_WIDTH)
IN_WIDTH = 2 * ATTN_WIDTH + 2 * KV_WIDTH + 4 * RWKV_WIDTH + 2 * GLA_KEY_WIDTH + 2 * GLA_VAL_WIDTH
NORM_EPS = 1e-6


def _rmsnorm(x, g):
    xf = x.astype(jnp.float32)
    y = xf * lax.rsqrt(jnp.mean(xf * xf, axis=-1, keepdims=True) + NORM_EPS)
    return (y * g.astype(jnp.float32)).astype(x.dtype)

def _shift(z):
    return jnp.pad(z, ((0, 0), (1, 0), (0, 0)))[:, :-1]

def _sliding_window_attention(q, k, v, sinks):
    B, T, Hq, D = q.shape
    Hkv = k.shape[2]
    G = Hq // Hkv
    nb = T // ATTN_BLOCK
    qb = q.reshape(B, nb, ATTN_BLOCK, Hkv, G, D)

    def band(z):
        zb = z.reshape(B, nb, ATTN_BLOCK, Hkv, D)
        prev = jnp.concatenate([jnp.zeros_like(zb[:, :1]), zb[:, :-1]], axis=1)
        return jnp.concatenate([prev, zb], axis=2)

    kb, vb = band(k), band(v)
    s = jnp.einsum('bnqhgd,bnkhd->bnhgqk', qb, kb,
                   preferred_element_type=jnp.float32) * (D ** -0.5)
    qi = jnp.arange(ATTN_BLOCK)[:, None]
    kj = jnp.arange(2 * ATTN_BLOCK)[None, :]
    dist = qi - kj + ATTN_BLOCK
    key_pos = jnp.arange(nb)[:, None, None] * ATTN_BLOCK + kj[None] - ATTN_BLOCK
    valid = (dist >= 0) & (dist < WINDOW) & (key_pos >= 0)
    slopes = 2.0 ** (-8.0 * jnp.arange(1, Hq + 1, dtype=jnp.float32) / Hq)
    s = s - slopes.reshape(Hkv, G)[:, :, None, None] * dist.astype(jnp.float32)
    s = jnp.where(valid[None, :, None, None], s, -jnp.inf)
    sink = jnp.broadcast_to(sinks.astype(jnp.float32).reshape(Hkv, G)[:, :, None, None],
                            s.shape[:-1] + (1,))
    p = jax.nn.softmax(jnp.concatenate([s, sink], axis=-1), axis=-1)[..., :-1]
    o = jnp.einsum('bnhgqk,bnkhd->bnqhgd', p.astype(v.dtype), vb)
    return o.reshape(B, T, Hq * D)

def _rwkv7_mixer(h, r, k, v, mu_w, mu_a, w0, w1, w2, a0, a1, a2, k_k, k_a, r_k, ln_w, ln_b):
    B, T, _ = h.shape
    f32 = jnp.float32
    h_prev = _shift(h)
    xw = h + (h_prev - h) * mu_w
    xa = h + (h_prev - h) * mu_a
    w = -jax.nn.softplus(-(w0 + jnp.tanh(xw @ w1) @ w2).astype(f32)) - 0.5
    decay = jnp.exp(-jnp.exp(w))
    a = jax.nn.sigmoid((a0 + (xa @ a1) @ a2).astype(f32))
    r, k, v = r.astype(f32), k.astype(f32), v.astype(f32)
    heads = lambda z: z.reshape(B, T, RWKV_HEADS, HEAD_DIM)
    kk = heads(k * k_k.astype(f32))
    kk = kk / jnp.maximum(jnp.linalg.norm(kk, axis=-1, keepdims=True), 1e-12)
    k = k * (1.0 + (a - 1.0) * k_a.astype(f32))

    def step(S, inp):
        r_t, w_t, k_t, v_t, kk_t, a_t = inp
        sa = jnp.einsum('bhvk,bhk->bhv', S, -kk_t)
        S = (S * w_t[:, :, None, :] + sa[..., None] * (kk_t * a_t)[:, :, None, :]
             + v_t[..., None] * k_t[:, :, None, :])
        return S, jnp.einsum('bhvk,bhk->bhv', S, r_t)

    tm = lambda z: jnp.moveaxis(z, 1, 0)
    S0 = jnp.zeros((B, RWKV_HEADS, HEAD_DIM, HEAD_DIM), f32)
    _, y = lax.scan(step, S0, (tm(heads(r)), tm(heads(decay)), tm(heads(k)), tm(heads(v)),
                               tm(kk), tm(heads(a))))
    y = jnp.moveaxis(y, 0, 1)
    mean = jnp.mean(y, axis=-1, keepdims=True)
    var = jnp.mean(jnp.square(y - mean), axis=-1, keepdims=True)
    y = ((y - mean) * lax.rsqrt(var + RWKV_LN_EPS)).reshape(B, T, RWKV_WIDTH)
    y = y * ln_w.astype(f32) + ln_b.astype(f32)
    bonus = jnp.sum(heads(r) * heads(k) * r_k.astype(f32), axis=-1, keepdims=True) * heads(v)
    return (y + bonus.reshape(B, T, RWKV_WIDTH)).astype(h.dtype)

def _gla_mixer(h, q, k, v, gk1, gk2, gk_b, norm_w):
    B, T, _ = h.shape
    f32 = jnp.float32
    n = T // GLA_CHUNK
    gk = jax.nn.log_sigmoid(((h @ gk1) @ gk2 + gk_b).astype(f32)) / GLA_GATE_NORMALIZER

    def chunks(z, d):
        return z.reshape(B, n, GLA_CHUNK, GLA_HEADS, d).transpose(1, 0, 3, 2, 4).astype(f32)

    qc = chunks(q, GLA_KEY_DIM) * (GLA_KEY_DIM ** -0.5)
    kc = chunks(k, GLA_KEY_DIM)
    vc = chunks(v, GLA_VAL_DIM)
    gc = chunks(gk, GLA_KEY_DIM)
    causal = jnp.tril(jnp.ones((GLA_CHUNK, GLA_CHUNK), bool))

    def step(S, inp):
        q_c, k_c, v_c, g_c = inp
        b = jnp.cumsum(g_c, axis=2)
        diff = b[:, :, :, None, :] - b[:, :, None, :, :]
        diff = jnp.where(causal[:, :, None], diff, -jnp.inf)
        A = jnp.einsum('bhid,bhjd,bhijd->bhij', q_c, k_c, jnp.exp(diff))
        o = A @ v_c + jnp.einsum('bhid,bhdv->bhiv', q_c * jnp.exp(b), S)
        b_last = b[:, :, -1:, :]
        S = (jnp.exp(b_last[:, :, 0, :])[..., None] * S
             + jnp.einsum('bhjd,bhjv->bhdv', k_c * jnp.exp(b_last - b), v_c))
        return S, o

    S0 = jnp.zeros((B, GLA_HEADS, GLA_KEY_DIM, GLA_VAL_DIM), f32)
    _, o = lax.scan(step, S0, (qc, kc, vc, gc))
    o = o.transpose(1, 0, 3, 2, 4).reshape(B, T, GLA_HEADS, GLA_VAL_DIM)
    o = o * lax.rsqrt(jnp.mean(o * o, axis=-1, keepdims=True) + 1e-5) * norm_w.astype(f32)
    return o.reshape(B, T, GLA_VAL_WIDTH).astype(h.dtype)

def _hybrid_layer(x, c_act, ada_w, ada_b, g_pre, g_post, w_in, w_out, sinks,
                  mu_rkv, mu_w, mu_a, w0, w1, w2, a0, a1, a2, k_k, k_a, r_k, ln_w, ln_b,
                  gk1, gk2, gk_b, gla_norm_w):
    B, T, _ = x.shape
    shift, scale, gate = jnp.split(c_act @ ada_w + ada_b, 3, axis=-1)
    h = _rmsnorm(x, g_pre) * (1.0 + scale[:, None]) + shift[:, None]
    proj = h @ w_in
    aq, ak, av, ag, rkv, rg, gq, gkk, gv, gg = jnp.split(proj, list(np.cumsum(IN_SPLITS)[:-1]), axis=-1)
    attn = _sliding_window_attention(aq.reshape(B, T, ATTN_Q_HEADS, HEAD_DIM),
                                     ak.reshape(B, T, ATTN_KV_HEADS, HEAD_DIM),
                                     av.reshape(B, T, ATTN_KV_HEADS, HEAD_DIM), sinks)
    attn = attn * jax.nn.silu(ag)
    rkv = rkv + (_shift(rkv) - rkv) * mu_rkv
    rr, rk, rv = jnp.split(rkv, 3, axis=-1)
    rwkv = _rwkv7_mixer(h, rr, rk, rv, mu_w, mu_a, w0, w1, w2, a0, a1, a2, k_k, k_a, r_k, ln_w, ln_b)
    rwkv = rwkv * jax.nn.silu(rg)
    gla = _gla_mixer(h, gq, gkk, gv, gk1, gk2, gk_b, gla_norm_w) * jax.nn.silu(gg)
    y = jnp.concatenate([attn, rwkv, gla], axis=-1) @ w_out
    return x + gate[:, None] * _rmsnorm(y, g_post)

def first_inputs(seed: int = 0) -> dict:
    key = jax.random.key(seed)
    ks = jax.random.split(key, 32)
    nrm = lambda k, shape, s: s * jax.random.normal(k, shape, jnp.float32)
    uni = lambda k, shape, lo, hi: jax.random.uniform(k, shape, jnp.float32, lo, hi)
    D, L = D_MODEL, DEPTH
    return {
        "x": nrm(ks[0], (BATCH, SEQ, D), 1.0),
        "c": nrm(ks[1], (BATCH, D), 1.0),
        "ada_w": nrm(ks[2], (L, D, 3 * D), 0.5 * D ** -0.5),
        "ada_b": nrm(ks[3], (L, 3 * D), 0.02),
        "norm_pre": 1.0 + nrm(ks[4], (L, D), 0.05),
        "norm_post": 1.0 + nrm(ks[5], (L, D), 0.05),
        "w_in": nrm(ks[6], (L, D, IN_WIDTH), D ** -0.5),
        "w_out": nrm(ks[7], (L, MIX_WIDTH, D), MIX_WIDTH ** -0.5),
        "attn_sinks": nrm(ks[8], (L, ATTN_Q_HEADS), 0.5),
        "rwkv_mu_rkv": uni(ks[9], (L, 3 * RWKV_WIDTH), 0.0, 1.0),
        "rwkv_mu_w": uni(ks[10], (L, D), 0.0, 1.0),
        "rwkv_mu_a": uni(ks[11], (L, D), 0.0, 1.0),
        "rwkv_w0": uni(ks[12], (L, RWKV_WIDTH), -4.0, 1.0),
        "rwkv_w1": nrm(ks[13], (L, D, DECAY_LORA), D ** -0.5),
        "rwkv_w2": nrm(ks[14], (L, DECAY_LORA, RWKV_WIDTH), 0.5 * DECAY_LORA ** -0.5),
        "rwkv_a0": nrm(ks[15], (L, RWKV_WIDTH), 0.1),
        "rwkv_a1": nrm(ks[16], (L, D, ICLR_LORA), D ** -0.5),
        "rwkv_a2": nrm(ks[17], (L, ICLR_LORA, RWKV_WIDTH), 0.5 * ICLR_LORA ** -0.5),
        "rwkv_k_k": 0.85 + nrm(ks[18], (L, RWKV_WIDTH), 0.05),
        "rwkv_k_a": 1.0 + nrm(ks[19], (L, RWKV_WIDTH), 0.05),
        "rwkv_r_k": nrm(ks[20], (L, RWKV_HEADS, HEAD_DIM), 0.1),
        "rwkv_ln_w": 1.0 + nrm(ks[21], (L, RWKV_WIDTH), 0.05),
        "rwkv_ln_b": nrm(ks[22], (L, RWKV_WIDTH), 0.02),
        "gla_gk1": nrm(ks[23], (L, D, GLA_GATE_LORA), D ** -0.5),
        "gla_gk2": nrm(ks[24], (L, GLA_GATE_LORA, GLA_KEY_WIDTH), GLA_GATE_LORA ** -0.5),
        "gla_gk_b": nrm(ks[25], (L, GLA_KEY_WIDTH), 0.1),
        "gla_norm_w": 1.0 + nrm(ks[26], (L, GLA_VAL_DIM), 0.05),
    }

def first_block(x, c, ada_w, ada_b, norm_pre, norm_post, w_in, w_out, attn_sinks,
              rwkv_mu_rkv, rwkv_mu_w, rwkv_mu_a, rwkv_w0, rwkv_w1, rwkv_w2,
              rwkv_a0, rwkv_a1, rwkv_a2, rwkv_k_k, rwkv_k_a, rwkv_r_k, rwkv_ln_w, rwkv_ln_b,
              gla_gk1, gla_gk2, gla_gk_b, gla_norm_w):
    c_act = jax.nn.silu(c)
    for l in range(DEPTH):
        x = _hybrid_layer(x, c_act, ada_w[l], ada_b[l], norm_pre[l], norm_post[l], w_in[l], w_out[l],
                          attn_sinks[l], rwkv_mu_rkv[l], rwkv_mu_w[l], rwkv_mu_a[l],
                          rwkv_w0[l], rwkv_w1[l], rwkv_w2[l], rwkv_a0[l], rwkv_a1[l], rwkv_a2[l],
                          rwkv_k_k[l], rwkv_k_a[l], rwkv_r_k[l], rwkv_ln_w[l], rwkv_ln_b[l],
                          gla_gk1[l], gla_gk2[l], gla_gk_b[l], gla_norm_w[l])
    return x


DEPTH_2 = 2

N_META = 16
BLOCK_Q = 128
ROPE_THETA = 10000.0
RMS_EPS = 1e-6
DA_HEADS = 8
DA_HEAD_DIM = 64
DSA_HEADS = 16
DSA_HEAD_DIM = 64
IDX_HEADS = 8
IDX_DIM = 64
TOPK_MAX = 256
DSA_QKV = DSA_HEADS * DSA_HEAD_DIM
DSA_SPLITS = [DSA_QKV, 2 * DSA_QKV, 3 * DSA_QKV,
              3 * DSA_QKV + IDX_HEADS * IDX_DIM,
              3 * DSA_QKV + IDX_HEADS * IDX_DIM + IDX_DIM]
DSA_IN_WIDTH = DSA_SPLITS[-1] + IDX_HEADS
ROPE_DIM = 64
BIG_SCORE = 1e30
FFN_HIDDEN = 2816
CONV_WIDTH = 3


def rms_norm(x, g):
    xf = x.astype(jnp.float32)
    y = xf * lax.rsqrt(jnp.mean(xf * xf, axis=-1, keepdims=True) + RMS_EPS)
    return (y * g.astype(jnp.float32)).astype(x.dtype)

def rope_tables(T, dim):
    inv = ROPE_THETA ** (-jnp.arange(0, dim, 2, dtype=jnp.float32) / dim)
    ang = jnp.arange(T, dtype=jnp.float32)[:, None] * inv[None, :]
    return jnp.cos(ang), jnp.sin(ang)

def apply_rope(x, cos, sin):
    shape = (1, cos.shape[0]) + (1,) * (x.ndim - 3) + (cos.shape[1],)
    c = cos.reshape(shape)
    s = sin.reshape(shape)
    x1, x2 = jnp.split(x.astype(jnp.float32), 2, axis=-1)
    return jnp.concatenate([x1 * c - x2 * s, x2 * c + x1 * s], axis=-1).astype(x.dtype)

def sweep_blocks(fn, T):
    out = lax.map(fn, jnp.arange(T // BLOCK_Q) * BLOCK_Q)
    out = jnp.moveaxis(out, 0, 1)
    return out.reshape((out.shape[0], T) + out.shape[3:])

def diff_attention(h, w_qkv, lq1, lk1, lq2, lk2, subln, w_o, cos, sin, lambda_init):
    B, T, _ = h.shape
    q, k, v = jnp.split(h @ w_qkv, 3, axis=-1)
    q = apply_rope(q.reshape(B, T, DA_HEADS, 2, DA_HEAD_DIM), cos, sin) * (DA_HEAD_DIM ** -0.5)
    k = apply_rope(k.reshape(B, T, DA_HEADS, 2, DA_HEAD_DIM), cos, sin)
    v = v.reshape(B, T, DA_HEADS, 2 * DA_HEAD_DIM)
    f32 = jnp.float32
    lam = (jnp.exp(jnp.sum(lq1.astype(f32) * lk1.astype(f32)))
           - jnp.exp(jnp.sum(lq2.astype(f32) * lk2.astype(f32))) + lambda_init)
    k_pos = jnp.arange(T)

    def block(start):
        q_pos = start + jnp.arange(BLOCK_Q)
        qb = lax.dynamic_slice_in_dim(q, start, BLOCK_Q, axis=1)
        s = jnp.einsum('bqhcd,bkhcd->bhcqk', qb, k).astype(f32)
        s = jnp.where(k_pos[None, :] <= q_pos[:, None], s, -jnp.inf)
        p = jax.nn.softmax(s, axis=-1)
        a = p[:, :, 0] - lam * p[:, :, 1]
        return jnp.einsum('bhqk,bkhe->bqhe', a.astype(v.dtype), v)

    o = sweep_blocks(block, T)
    o = rms_norm(o, subln) * (1.0 - lambda_init)
    return o.reshape(B, T, DA_HEADS * 2 * DA_HEAD_DIM) @ w_o

def dsa_attention(h, w_in, idx_k_norm, w_o, cos, sin, n_keys):
    B, T, _ = h.shape
    q, k, v, qi, ki, wi = jnp.split(h @ w_in, DSA_SPLITS, axis=-1)
    q = apply_rope(q.reshape(B, T, DSA_HEADS, DSA_HEAD_DIM), cos, sin) * (DSA_HEAD_DIM ** -0.5)
    k = apply_rope(k.reshape(B, T, DSA_HEADS, DSA_HEAD_DIM), cos, sin)
    v = v.reshape(B, T, DSA_HEADS, DSA_HEAD_DIM)
    qi = apply_rope(qi.reshape(B, T, IDX_HEADS, IDX_DIM), cos, sin)
    ki = apply_rope(rms_norm(ki, idx_k_norm), cos, sin)
    wi = wi * (IDX_HEADS ** -0.5)
    topk = min(TOPK_MAX, n_keys // 4)
    k_pos = jnp.arange(T)
    f32 = jnp.float32
    gather = jax.vmap(lambda arr, idx: arr[idx])

    def block(start):
        q_pos = start + jnp.arange(BLOCK_Q)
        qb = lax.dynamic_slice_in_dim(q, start, BLOCK_Q, axis=1)
        qib = lax.dynamic_slice_in_dim(qi, start, BLOCK_Q, axis=1)
        wb = lax.dynamic_slice_in_dim(wi, start, BLOCK_Q, axis=1)
        raw = jnp.einsum('bqhd,bkd->bqhk', qib, ki).astype(f32) * (IDX_DIM ** -0.5)
        score = jnp.einsum('bqhk,bqh->bqk', jax.nn.relu(raw), wb.astype(f32))
        causal = k_pos[None, :] <= q_pos[:, None]
        score = jnp.where(causal & (k_pos < N_META)[None, :], BIG_SCORE, score)
        score = jnp.where(causal, score, -jnp.inf)
        top_val, top_idx = lax.top_k(score, topk)
        valid = top_val > -jnp.inf
        ks = gather(k, top_idx)
        vs = gather(v, top_idx)
        s = jnp.einsum('bqhd,bqjhd->bhqj', qb, ks).astype(f32)
        s = jnp.where(valid[:, None], s, -jnp.inf)
        p = jax.nn.softmax(s, axis=-1)
        return jnp.einsum('bhqj,bqjhd->bqhd', p.astype(vs.dtype), vs)

    o = sweep_blocks(block, T)
    return o.reshape(B, T, DSA_QKV) @ w_o

def conv_ffn(h, w_up, conv_w, conv_b, w_down):
    u = h @ w_up
    T = u.shape[1]
    up = jnp.pad(u, ((0, 0), (CONV_WIDTH - 1, 0), (0, 0)))
    c = conv_b + sum(conv_w[j] * up[:, j:j + T] for j in range(CONV_WIDTH))
    g, val = jnp.split(c, 2, axis=-1)
    return (jax.nn.silu(g) * val) @ w_down

def second_inputs(seed: int = 0) -> dict:
    key = jax.random.key(seed)
    ks = iter(jax.random.split(key, 32))
    n_a = (DEPTH_2 + 1) // 2
    n_b = DEPTH_2 // 2
    D, F = D_MODEL, FFN_HIDDEN

    def nrm(shape, scale):
        return jax.random.normal(next(ks), shape, jnp.float32) * scale

    def gain(shape):
        return 1.0 + nrm(shape, 0.02)

    return {
        "x": nrm((BATCH, SEQ, D), 1.0),
        "meta_tokens": nrm((N_META, D), 1.0),
        "da_norm": gain((n_a, D)),
        "da_w_qkv": nrm((n_a, D, 3 * D), D ** -0.5),
        "da_lambda_q1": nrm((n_a, DA_HEAD_DIM), 0.1),
        "da_lambda_k1": nrm((n_a, DA_HEAD_DIM), 0.1),
        "da_lambda_q2": nrm((n_a, DA_HEAD_DIM), 0.1),
        "da_lambda_k2": nrm((n_a, DA_HEAD_DIM), 0.1),
        "da_subln": gain((n_a, 2 * DA_HEAD_DIM)),
        "da_w_o": nrm((n_a, DA_HEADS * 2 * DA_HEAD_DIM, D), D ** -0.5),
        "dsa_norm": gain((n_b, D)),
        "dsa_w_in": nrm((n_b, D, DSA_IN_WIDTH), D ** -0.5),
        "dsa_idx_k_norm": gain((n_b, IDX_DIM)),
        "dsa_w_o": nrm((n_b, DSA_QKV, D), DSA_QKV ** -0.5),
        "ffn_norm": gain((DEPTH_2, D)),
        "ffn_w_up": nrm((DEPTH_2, D, 2 * F), D ** -0.5),
        "ffn_conv_w": nrm((DEPTH_2, CONV_WIDTH, 2 * F), CONV_WIDTH ** -0.5),
        "ffn_conv_b": nrm((DEPTH_2, 2 * F), 0.02),
        "ffn_w_down": nrm((DEPTH_2, F, D), F ** -0.5),
        "final_norm": gain((D,)),
    }

def second_block(x, meta_tokens, da_norm, da_w_qkv, da_lambda_q1, da_lambda_k1,
              da_lambda_q2, da_lambda_k2, da_subln, da_w_o, dsa_norm, dsa_w_in,
              dsa_idx_k_norm, dsa_w_o, ffn_norm, ffn_w_up, ffn_conv_w, ffn_conv_b,
              ffn_w_down, final_norm):
    B, L, D = x.shape
    T = L + N_META
    T_pad = ((T + BLOCK_Q - 1) // BLOCK_Q) * BLOCK_Q
    meta = jnp.broadcast_to(meta_tokens[None].astype(x.dtype), (B, N_META, D))
    h = jnp.concatenate([meta, x], axis=1)
    h = jnp.pad(h, ((0, 0), (0, T_pad - T), (0, 0)))
    cos, sin = rope_tables(T_pad, ROPE_DIM)
    for i in range(DEPTH_2):
        j = i // 2
        if i % 2 == 0:
            lambda_init = 0.8 - 0.6 * math.exp(-0.3 * i)
            h = h + diff_attention(rms_norm(h, da_norm[j]), da_w_qkv[j],
                                   da_lambda_q1[j], da_lambda_k1[j],
                                   da_lambda_q2[j], da_lambda_k2[j],
                                   da_subln[j], da_w_o[j], cos, sin, lambda_init)
        else:
            h = h + dsa_attention(rms_norm(h, dsa_norm[j]), dsa_w_in[j],
                                  dsa_idx_k_norm[j], dsa_w_o[j], cos, sin, L)
        h = h + conv_ffn(rms_norm(h, ffn_norm[i]), ffn_w_up[i], ffn_conv_w[i],
                         ffn_conv_b[i], ffn_w_down[i])
    h = rms_norm(h, final_norm)
    return h[:, N_META:N_META + L]


def setup_inputs(seed=0):
    out = dict(first_inputs(seed))
    for name, value in second_inputs(seed + 1).items():
        if name != "x":
            out[name + "_2"] = value
    return out


def reference(
    x, c, ada_w, ada_b, norm_pre, norm_post, w_in, w_out, attn_sinks, rwkv_mu_rkv, rwkv_mu_w,
    rwkv_mu_a, rwkv_w0, rwkv_w1, rwkv_w2, rwkv_a0, rwkv_a1, rwkv_a2, rwkv_k_k, rwkv_k_a,
    rwkv_r_k, rwkv_ln_w, rwkv_ln_b, gla_gk1, gla_gk2, gla_gk_b, gla_norm_w, meta_tokens_2,
    da_norm_2, da_w_qkv_2, da_lambda_q1_2, da_lambda_k1_2, da_lambda_q2_2, da_lambda_k2_2,
    da_subln_2, da_w_o_2, dsa_norm_2, dsa_w_in_2, dsa_idx_k_norm_2, dsa_w_o_2, ffn_norm_2,
    ffn_w_up_2, ffn_conv_w_2, ffn_conv_b_2, ffn_w_down_2, final_norm_2,
):
    x = first_block(
        x, c, ada_w, ada_b, norm_pre, norm_post, w_in, w_out, attn_sinks, rwkv_mu_rkv,
        rwkv_mu_w, rwkv_mu_a, rwkv_w0, rwkv_w1, rwkv_w2, rwkv_a0, rwkv_a1, rwkv_a2, rwkv_k_k,
        rwkv_k_a, rwkv_r_k, rwkv_ln_w, rwkv_ln_b, gla_gk1, gla_gk2, gla_gk_b, gla_norm_w,
    )
    return second_block(
        x, meta_tokens_2, da_norm_2, da_w_qkv_2, da_lambda_q1_2, da_lambda_k1_2, da_lambda_q2_2,
        da_lambda_k2_2, da_subln_2, da_w_o_2, dsa_norm_2, dsa_w_in_2, dsa_idx_k_norm_2,
        dsa_w_o_2, ffn_norm_2, ffn_w_up_2, ffn_conv_w_2, ffn_conv_b_2, ffn_w_down_2,
        final_norm_2,
    )


_drawn_inputs = setup_inputs


def setup_inputs(seed=0):
    import zlib

    import numpy as np

    out = dict(_drawn_inputs(seed))
    spreads = {}
    factors = {'attn_sinks': 4.357,
     'rwkv_mu_w': 8.0,
     'rwkv_a0': 4.001,
     'rwkv_k_k': 5.165,
     'rwkv_k_a': 2.887,
     'rwkv_ln_w': 3.394,
     'rwkv_ln_b': 4.687,
     'gla_gk_b': 3.448,
     'gla_norm_w': 3.373,
     'da_lambda_q1_2': 8.0,
     'da_subln_2': 3.265,
     'dsa_norm_2': 4.327,
     'dsa_idx_k_norm_2': 5.623,
     'ffn_norm_2': 2.877,
     'ffn_conv_b_2': 2.923}
    for name, (base, spread) in spreads.items():
        noise = np.random.default_rng([zlib.crc32(name.encode()), seed]).standard_normal(out[name].shape)
        drawn = base * np.exp(spread * noise) if base else spread * noise
        out[name] = __import__('jax').numpy.asarray(drawn.astype(out[name].dtype))
    for name, factor in factors.items():
        out[name] = (out[name] * factor).astype(out[name].dtype)
    return out
```

```python
import math
from contextlib import ExitStack

import numpy as np

from concourse import mybir

P = 128
D = 1024
KT = D // P
T1 = 512
META = 16
T2 = T1 + META
HALF = T2 // 2
FFN = 2816
FT = FFN // P
RING = 8
BIG = 1e30
LAMBDA_INIT = 0.8 - 0.6 * math.exp(0.0)

COLUMNS = [
    ("c", 8), ("ada_b", 24), ("norm_pre", 8), ("norm_post", 8), ("mu_rkv", 6), ("mu_w", 8), ("mu_a", 8),
    ("w0", 2), ("a0", 2), ("k_k", 2), ("k_a", 2), ("r_k", 2), ("ln_w", 2), ("ln_b", 2), ("gk_b", 1),
    ("gla_norm", 1), ("da_norm", 8), ("subln", 1), ("dsa_norm", 8), ("ffn_norm", 16), ("final_norm", 8),
    ("conv_w", 6 * FT * 2), ("conv_b", 2 * FT * 2), ("lam_q", 2), ("lam_k", 2), ("idx_norm", 2), ("sinks", 8),
]
COL = {}
_at = 0
for _name, _n in COLUMNS:
    COL[_name] = (_at, _n)
    _at += _n
NCOL = _at

N_ADA = 24
N_IN1 = 26
N_OUT = 8
N_DA = 24
N_DSA = 31
N_UP = 2 * FT
N_DOWN = 3 * KT
S_IN1 = N_ADA
S_OUT1 = S_IN1 + N_IN1
S_DA = S_OUT1 + N_OUT
S_DAO = S_DA + N_DA
S_UP0 = S_DAO + N_OUT
S_DOWN0 = S_UP0 + N_UP
S_DSA = S_DOWN0 + N_DOWN
S_DSAO = S_DSA + N_DSA
S_UP1 = S_DSAO + N_OUT
S_DOWN1 = S_UP1 + N_UP
N_SLOTS = S_DOWN1 + N_DOWN


def build(nc, ins, out_t):
    F32 = mybir.dt.float32
    BF16 = mybir.dt.bfloat16
    U8 = mybir.dt.uint8
    ALU = mybir.AluOpType
    ACT = mybir.ActivationFunctionType
    AX = mybir.AxisListType

    ctx = ExitStack()

    def sb(name, shape, dt=F32):
        return ctx.enter_context(nc.sbuf_tensor(name, shape, dt))

    def sem(name):
        return ctx.enter_context(nc.semaphore(name))

    class Steps:

        def __init__(self, eng, counter):
            self.eng, self.counter, self.n = eng, counter, 0

        def did(self, ins):
            ins.then_inc(self.counter, 1)
            self.n += 1
            return ins

        def settle(self):
            self.eng.wait_ge(self.counter, self.n)

        def link(self, ins):
            self.did(ins)
            self.settle()

    psum = ctx.enter_context(nc.psum_tensor("banks", [P, 8, 512], F32))
    h = sb("h", [P, KT, T2])
    hn_raw = sb("hn_raw", [P, KT * (T2 + 1)])
    hn = hn_raw[:, 0:KT * T2].rearrange("p (k t) -> p k t", k=KT)
    h1 = hn_raw[:, 0:KT * (T1 + 1)].rearrange("p (k t) -> p k t", k=KT)
    ring = sb("ring", [P, RING, KT * P])
    cols = sb("cols", [P, NCOL])
    ident = sb("ident", [P, P])
    ones = sb("ones", [P, P])
    identb = sb("identb", [P, P], BF16)
    causalb = sb("causalb", [P, P], BF16)
    rs = sb("rs", [P, T2])
    ada = sb("ada", [P, 24])
    small = sb("small", [P, 64])
    ARENA = 30500
    arena = sb("arena", [P, ARENA])
    norm_tmp = sb("norm_tmp", [P, T2])

    class Carve:

        def __init__(self, base, size):
            self.base, self.size, self.at = base, size, 0

        def take(self, *dims):
            n = int(np.prod(dims))
            v = self.base[:, self.at:self.at + n]
            self.at += n
            assert self.at <= self.size, (self.at, self.size)
            names = "abcd"[:len(dims)]
            if len(dims) == 1:
                return v
            return v.rearrange("p (" + " ".join(names) + ") -> p " + " ".join(names), **dict(zip(names[:-1], dims[:-1])))

    def col(name, i=0, n=1):
        a = COL[name][0] + i
        return cols[:, a:a + n]

    c1 = Carve(arena, ARENA)
    bones = c1.take(P)
    agate = c1.take(4, T1)
    rgate = c1.take(2, T1)
    ggate = c1.take(2, T1)
    mix = c1.take(8, T1)
    zb = c1.take(6, T1 + 1)
    sg = c1.take(2, T1)
    asig = c1.take(2, T1)
    front = c1.at
    gq = c1.take(T1)
    gk = c1.take(T1)
    gv = c1.take(2, T1)
    gz = c1.take(T1)
    low = c1.take(T1)
    glow = c1.take(T1)
    att_at = c1.at
    qz1 = c1.take(4, 2, T1)
    k1 = c1.take(T1)
    v1 = c1.take(T1)
    tail_at = c1.at
    alibi = c1.take(8, 256)
    loraW = c1.take(KT, P)
    lora2 = c1.take(5, P)
    dmix = c1.take(T1)
    mask_in = c1.take(8, P)
    ca = Carve(hn_raw, KT * (T2 + 1))
    p1 = ca.take(2, 2, 256)
    pt1 = ca.take(2, 4 * P)
    v1tok = ca.take(4, P)
    cg = Carve(arena[:, att_at:ARENA], ARENA - att_at)
    g_b = cg.take(T1)
    g_d = cg.take(2, T1)
    g_ql = cg.take(2, T1)
    g_kl = cg.take(2, T1)
    g_vz = cg.take(4, 4, P)
    g_vt = cg.take(4, 256)
    g_kt = cg.take(4, P)
    g_qe = cg.take(T1)
    g_es = cg.take(2, T1)
    ch = Carve(hn_raw, KT * (T2 + 1))
    g_at = ch.take(4, T1)
    g_kd = ch.take(T1)
    g_s = ch.take(2, 256)
    g_o = ch.take(2, T1)
    cr = Carve(arena[:, front:ARENA], ARENA - front)
    r_kk = cr.take(T1)
    r_b = cr.take(T1)
    r_e = cr.take(3, T1)
    r_rho = cr.take(T1)
    r_lt = cr.take(8, P)
    r_akt = cr.take(8, P)
    r_rbt = cr.take(8, 64)
    r_rkt = cr.take(8, 64)
    r_x = cr.take(8, 2, P)
    r_t = cr.take(8, P)
    r_n = cr.take(8, P)
    r_tok = cr.take(8, 4, P)
    r_wt = cr.take(8, P)
    r_t1 = cr.take(8, P)
    r_s = cr.take(2, P)
    r_se = cr.take(P)
    r_u = cr.take(2, P)
    ck = Carve(hn_raw, KT * (T2 + 1))
    r_z = ck.take(4, 8, P)
    y1_buf = Carve(arena[:, front:ARENA], ARENA - front).take(KT, T1)
    cb = Carve(arena, ARENA)
    cosT = cb.take(T2)
    sinT = cb.take(T2)
    low_at = cb.at
    kz = cb.take(8, T2)
    rope_buf = cb.take(2, 4, T2)
    oT = rope_buf.rearrange("p a b t -> p (a b) t")
    vch = cb.take(2, T2)
    prob_buf = cb.take(4, 2, T2)
    prob_flat = prob_buf.rearrange("p a b t -> p (a b) t")
    sel = prob_flat[:, 4:8, :]
    pt = cb.take(2, 4 * P)
    ki2 = cb.take(T2)
    wch = cb.take(T2)
    cb.at = low_at
    act_t = cb.take(FT, T2)
    u_in = cb.take(4, T2 + 2)
    u_c = cb.take(4, T2)
    cb.at = ARENA - 8 * 2 * T2 - 5 * 1024
    assert cb.at >= low_at + FT * T2 + 4 * (T2 + 2) + 4 * T2
    vtok = cb.take(5, 1024)
    qz = cb.take(8, 2, T2)
    qiz = vtok.rearrange("p a b -> p (a b)")[:, 0:8 * T2].rearrange("p (a b t) -> p a b t", a=4, b=2)
    stat = sb("stat", [P, 4, 8])
    stat2 = sb("stat2", [P, 8])
    nlam = stat2[:, 4:5]
    wtok = sb("wtok", [P, 4, 8])
    top8 = sb("top8", [P, 8])
    causalf = sb("causalf", [P, P])

    def rope_t(i, j):
        return rope_buf[:, i % 2, j, :]

    def prob(u, c, maps=2):
        return prob_buf[:, u % 4, c, :] if maps == 2 else prob_flat[:, u % 4, :]

    def prob1(j):
        return prob_flat[:, j, :]

    rmask = sb("rmask", [P, 2 * P + 128])
    lvlmask = sb("lvlmask", [P, 6, P])
    glamask = sb("glamask", [P, 8, P], U8)
    gblock = sb("gblock", [P, 256])
    reset64 = sb("reset64", [P, T1])
    reset128 = sb("reset128", [P, T1])
    w_loaded = [sem(f"w_loaded{r}") for r in range(RING)]
    names = """slot_used params_in x_in consts_in meta_in out_stored dve_step act_step pool_step
        c_exp c_silu ada_done norm_sq norm_sum norm_var norm_std hn_ready shift_diff lora_scaled
        lora_low lora_done in1_evac qz1_zeroed zero_cols mixed
        s1_scores s1_soft s1_sinkd s1_exp s1_prob s1_trans s1_pt s1_pv s1_out v1_trans v1_tok
        g_absz g_ln g_cum g_diff g_exp g_lvl g_score g_taken g_zero g_tr g_trc g_qk g_sc g_sd g_ops g_ost g_osq g_osum g_ovar g_ostd g_done
        r_zero r_kkraw r_kksq r_kksum r_kkstd r_decay r_exps r_ready r_bon r_bonsum r_prod r_masked r_tokps r_toksb
        r_nready r_tps r_tsb r_xps r_wps r_t1sb r_wsb r_ups r_usb r_sps r_ssb r_yps r_ysb
        r_mean r_cent r_ysq r_ysum r_yvar r_ystd r_done x_upd x1_done
            rope_in qz_zero lam_prod lam_sum lam_exp rope_read rope_done v_ch v_tr v_tok a_sc a_max a_exp a_prob a_tr a_pt a_pv a_o
            hd_sq hd_sum hd_var hd_std hd_done res_done u_zero u_evac conv_done silu_done a_ready
            ki_sq ki_sum ki_var ki_std ki_normed ki_done wi_ch wi_tr i_sc i_relu i_acc""".split()
    scattered = [sem(f"scattered{i}") for i in range(2)]
    S = {n: sem(n) for n in names}
    block = ctx.enter_context(nc.Block())

    def bank(b, n=T1):
        return psum[:, b, 0:n]

    def pair(g, parts=P):
        return psum[0:parts, 2 * (g % 3):2 * (g % 3) + 2, 0:HALF]

    def halves(v):
        return v.rearrange("p (a b) -> p a b", a=2)

    ITEMS = 31

    def zb_d(k):
        return mix[:, k, :]

    def rz(q, u):
        return r_z[:, q, u, :]

    def rz_half(q, s):
        return r_z[64 * s:64 * s + 64, q, :, 64 * s:64 * s + 64]

    def g_e(lv):
        return g_es[:, lv % 2, :]

    def y1(g):
        return y1_buf[:, g, :]

    def g_o_sq(j):
        return g_ql[:, j, :]

    TILES = [(n, min(P, T2 - n * P)) for n in range(5)]
    EPS = 1e-6
    SELECTED = float(np.float32(-3e38))
    TOPK = 128
    LA_PE, LA_DVE, LA_ACT = 3, 2, 2

    def keys(n):
        return min((n + 1) * P, T2)

    def banks_of(b, n):
        if n < 4:
            return psum[:, b, 0:keys(n)]
        return psum[0:16, b:b + 2, 0:HALF]

    def idx_bank(i, n):
        return banks_of(2 * (i % 3), n)

    def sc_bank(maps, n, c):
        if maps == 1:
            return banks_of(n, n)
        return banks_of(2 * (n % 3) + c if n < 4 else 2 + 2 * c, n)

    def sc_sb(v, n):
        return v[:, 0:keys(n)] if n < 4 else halves(v[0:16, :])

    def hn_base(v):
        return KT * (v - 1)

    def tensor_block2(pe):
        mm = nc.tensor.matmul

        def slot(n):
            pe.wait_ge(w_loaded[n % RING], 16 * (n // RING + 1))
            return ring[:, n % RING, :].rearrange("p (k m) -> p k m", k=KT)

        def both(g, w, rhs, first, last):
            for a in range(2):
                ins_ = mm(psum[:, 2 * (g % 3) + a, 0:HALF], w, rhs[:, a * HALF:(a + 1) * HALF], start=first, stop=last)
            return ins_

        def sums(v):
            for k in range(KT):
                pe.wait_ge(S["norm_sq"], KT * v + k + 1)
                for a in range(2):
                    last = mm(psum[:, 6 + a, 0:HALF], ones[:, :], hn[:, k, a * HALF:(a + 1) * HALF], start=k == 0, stop=k == KT - 1)
            last.then_inc(S["norm_sum"], 1)

        def project(s0, groups, v, free, after=None):
            for g in groups:
                w = slot(s0 + g)
                if g >= 3:
                    free(g - 3)
                for k in range(KT):
                    if g == 0:
                        pe.wait_ge(S["hn_ready"], hn_base(v) + k + 1)
                    last = both(g, w[:, k, :], hn[:, k, :], k == 0, k == KT - 1)
                last.then_inc(S["slot_used"], 1)
                if after:
                    after(g)

        def v_transpose(j, base):
            pe.wait_ge(S["v_ch"], base + j + 1)
            if j >= 1:
                pe.wait_ge(S["v_tok"], base + j)
            for n, w in TILES:
                dst = psum[:, 6, n * P:(n + 1) * P] if n < 4 else psum[0:16, 7, 0:P]
                last = nc.tensor.transpose(dst, vch[:, j % 2, n * P:n * P + w], ident[:, :])
            last.then_inc(S["v_tr"], 1)

        def attention(maps, heads, base_u, base_sc):
            units = [(hd, n, w) for hd in range(heads) for n, w in TILES]

            def free_scores(u, c):
                hd, n, w = units[u]
                if maps == 1:
                    if hd:
                        pe.wait_ge(S["a_max"], base_u + u - 4)
                elif n < 3:
                    if hd:
                        pe.wait_ge(S["a_exp"], base_sc + (2 * u - 2, 2 * u - 3, 2 * u - 4)[n])
                elif n == 3:
                    pe.wait_ge(S["a_exp"], base_sc + 2 * u - 4)
                else:
                    pe.wait_ge(S["a_exp"], base_sc + 2 * u - 4 + 2 * c)

            def scores(u):
                hd, n, w = units[u]
                for c in range(maps):
                    free_scores(u, c)
                    m = hd * maps + c
                    q = qz[:, m // 2, m % 2, n * P:n * P + w]
                    o = sc_bank(maps, n, c)
                    masked = maps == 2
                    if n < 4:
                        last = mm(o, q, kz[:, m // 2, 0:keys(n)], start=True, stop=not masked)
                        if masked:
                            last = mm(o[:, n * P:(n + 1) * P], identb[:, :], causalb[:, :], start=False, stop=True)
                    else:
                        mm(o[:, 0, :], q, kz[:, m // 2, 0:HALF], start=True, stop=True)
                        last = mm(o[:, 1, :], q, kz[:, m // 2, HALF:T2], start=True, stop=not masked)
                        if masked:
                            last = mm(o[:, 1, 4 * P - HALF:HALF], identb[:, 0:16], causalb[:, 0:16], start=False, stop=True)
                    last.then_inc(S["a_sc"], 1)

            def transposes(u):
                hd, n, w = units[u]
                pe.wait_ge(S["a_prob"], base_u + u + 1)
                if u >= 1:
                    pe.wait_ge(S["a_pt"], base_u + u)
                for j in range(n + 1):
                    kj = TILES[j][1]
                    last = nc.tensor.transpose(psum[0:kj, 6, j * w:(j + 1) * w], prob(u, 0, maps)[0:w, j * P:j * P + kj], ident[0:w, 0:w])
                last.then_inc(S["a_tr"], 1)

            def values(u):
                hd, n, w = units[u]
                pe.wait_ge(S["a_pt"], base_u + u + 1)
                if u >= 1:
                    pe.wait_ge(S["a_o"], base_u + u)
                e = (hd * maps // 2) * P
                for j in range(n + 1):
                    kj = TILES[j][1]
                    last = mm(psum[:, 7, 0:w], vtok[0:kj, j, e:e + P], pt[0:kj, u % 2, j * w:(j + 1) * w], start=j == 0, stop=j == n)
                last.then_inc(S["a_pv"], 1)

            for u in range(LA_PE):
                scores(u)
            for u in range(len(units)):
                if u + LA_PE < len(units):
                    scores(u + LA_PE)
                transposes(u)
                if u:
                    values(u - 1)
            values(len(units) - 1)

        def residual(s0, base, first_free, rhs, rhs_ready):
            for g in range(KT):
                w = slot(s0 + g)
                if g >= 3:
                    pe.wait_ge(S["res_done"], base + g - 2)
                else:
                    first_free(g)
                for k in range(KT):
                    if g == 0:
                        rhs_ready(k)
                    last = both(g, w[:, k, :], rhs[:, k, :], k == 0, k == KT - 1)
                last.then_inc(S["slot_used"], 1)

        def ffn(i, v, s_up, s_down, base):
            def free(g):
                pe.wait_ge(S["u_evac"], N_UP * i + g + 1)
            project(s_up, range(N_UP), v, free)
            n = s_down
            for g in range(KT):
                if g >= 3:
                    pe.wait_ge(S["res_done"], base + g - 2)
                else:
                    pe.wait_ge(S["u_evac"], N_UP * (i + 1))
                for part in range(3):
                    w = slot(n)
                    for k in range(8 * part, min(8 * part + 8, FT)):
                        if g == 0:
                            pe.wait_ge(S["a_ready"], FT * i + k + 1)
                        last = both(g, w[:, k % 8, :], act_t[:, k, :], k == 0, k == FT - 1)
                    last.then_inc(S["slot_used"], 1)
                    n += 1

        sums(2)
        pe.wait_ge(S["lam_prod"], 1)
        mm(psum[:, 0, 0:2], ones[:, :], stat2[:, 0:2], start=True, stop=True).then_inc(S["lam_sum"], 1)
        pe.wait_ge(S["lam_exp"], 1)

        def da_free(g):
            if g < 16:
                pe.wait_ge(S["rope_read"], g // 2 + 1)
            else:
                pe.wait_ge(S["v_ch"], g - 16 + 1)

        def da_after(g):
            if g > 16:
                v_transpose(g - 17, 0)
        project(S_DA, range(N_DA), 2, da_free, da_after)
        v_transpose(7, 0)
        for b in range(2):
            pe.wait_ge(scattered[b], 128 * 4)
        pe.wait_ge(S["v_tok"], 8)
        attention(2, 8, 0, 0)
        for hd in range(8):
            pe.wait_ge(S["hd_sq"], hd + 1)
            if hd >= 3:
                pe.wait_ge(S["hd_var"], hd - 2)
            both(hd, ones[:, :], prob(hd, 1), True, True).then_inc(S["hd_sum"], 1)

        def da_o_free(g):
            pe.wait_ge(S["hd_var"], 8)
        residual(S_DAO, 0, da_o_free, oT, lambda k: pe.wait_ge(S["hd_done"], k + 1))
        sums(3)
        ffn(0, 3, S_UP0, S_DOWN0, 8)

        sums(4)

        def dsa_free(g):
            if g < 4:
                pe.wait_ge(S["rope_read"], 8 + g // 2 + 1)
            elif g < 6:
                pe.wait_ge(S["ki_normed"], 1)
            elif g == 6:
                pe.wait_ge(S["wi_ch"], 1)
            elif g < 23:
                pe.wait_ge(S["rope_read"], 10 + (g - 7) // 2 + 1)
            else:
                pe.wait_ge(S["v_ch"], 8 + g - 23 + 1)

        project(S_DSA, range(7), 4, dsa_free)
        pe.wait_ge(S["ki_sq"], 1)
        for j in range(2):
            for a in range(2):
                last = mm(psum[:, 6 + a, 0:HALF], ones[:, :], prob1(j)[:, a * HALF:(a + 1) * HALF], start=j == 0, stop=j == 1)
        last.then_inc(S["ki_sum"], 1)
        pe.wait_ge(S["ki_var"], 1)
        pe.wait_ge(S["wi_ch"], 1)
        for n, w in TILES[1:]:
            last = nc.tensor.transpose(psum[0:w, 6, (n - 1) * P:n * P], wch[:, n * P:n * P + w], ident[:, :])
        last.then_inc(S["wi_tr"], 1)
        for b in range(2):
            pe.wait_ge(scattered[b], 128 * 5)
        pe.wait_ge(S["ki_done"], 1)
        pe.wait_ge(S["wi_ch"], 1)
        for i, (n, hd) in enumerate([(n, hd) for n in range(1, 5) for hd in range(8)]):
            w = TILES[n][1]
            if i >= 3:
                pe.wait_ge(S["i_relu"], i - 2)
            q = qiz[:, hd // 2, hd % 2, n * P:n * P + w]
            if n < 4:
                last = mm(psum[:, 2 * (i % 3), 0:keys(n)], q, ki2[:, 0:keys(n)], start=True, stop=True)
            else:
                for a in range(2):
                    last = mm(psum[0:16, 2 * (i % 3) + a, 0:HALF], q, ki2[:, a * HALF:(a + 1) * HALF], start=True, stop=True)
            last.then_inc(S["i_sc"], 1)
        pe.wait_ge(S["i_relu"], 32)

        def dsa_free2(g):
            if g >= 7:
                dsa_free(g)

        def dsa_after(g):
            if g > 23:
                v_transpose(g - 24, 8)
        project(S_DSA, range(7, N_DSA), 4, dsa_free2, dsa_after)
        v_transpose(7, 8)
        for b in range(2):
            pe.wait_ge(scattered[b], 128 * 9)
        pe.wait_ge(S["v_tok"], 16)
        attention(1, 16, 40, 80)

        def dsa_o_free(g):
            pe.wait_ge(S["a_max"], 120)
        residual(S_DSAO, 16, dsa_o_free, oT, lambda k: pe.wait_ge(S["a_o"], 120))
        sums(5)
        ffn(1, 5, S_UP1, S_DOWN1, 24)
        sums(6)

    def pool_block2(pool):
        g = nc.gpsimd
        pool.wait_ge(S["x1_done"], KT)
        g.memset(qz, 0.0).then_inc(S["qz_zero"], 1)
        pool.wait_ge(S["a_pv"], 40)
        g.memset(qiz, 0.0).then_inc(S["qz_zero"], 1)

    def act_block2(act):
        A = nc.scalar.activation
        st = Steps(act, S["act_step"])
        st.n = 1

        act.wait_ge(S["x1_done"], KT)
        act.dma_start(cosT, ins["cosT"]).then_inc(S["rope_in"], 16)
        act.dma_start(sinT, ins["sinT"]).then_inc(S["rope_in"], 16)

        def squares(v, ready):
            for k in range(KT):
                ready(k)
                A(hn[:, k, :], h[:, k, :], ACT.Square).then_inc(S["norm_sq"], 1)
            act.wait_ge(S["norm_var"], v + 1)
            A(rs[:, :], rs[:, :], ACT.Sqrt).then_inc(S["norm_std"], 1)

        def scatter(i, p, dst):
            act.wait_ge(S["rope_done"], i + 1)
            for r in range(4):
                m = 4 * p + r
                for half, src in enumerate((rope_t(i, 0), rope_t(i, 3))):
                    at = 64 * (m % 2) + 32 * half
                    act.dma_start(dst(m)[at:at + 32], src[32 * r:32 * r + 32, :]).then_inc(scattered[i % 2], 16)

        def values(s0, g0, base):
            for j in range(8):
                act.wait_ge(S["slot_used"], s0 + g0 + j + 1)
                if j >= 2:
                    act.wait_ge(S["v_tr"], base + j - 1)
                A(halves(vch[:, j % 2, :]), pair(g0 + j), ACT.Copy).then_inc(S["v_ch"], 1)

        def attention(maps, heads, base_u, base_sc):
            units = [(hd, n, w) for hd in range(heads) for n, w in TILES]

            def exps(u):
                hd, n, w = units[u]
                act.wait_ge(S["a_max"], base_u + u + 1)
                if u >= 4:
                    act.wait_ge(S["a_tr"], base_u + u - 3)
                s = stat[0:w, u % 4, :]
                for c in range(maps):
                    p = sc_sb(prob(u, c, maps), n)
                    A(p, sc_bank(maps, n, c) if maps == 2 else p, ACT.Exp, bias=s[:, 2 + c:3 + c], scale=0.125 if maps == 2 else 1.0,
                      accum_out=s[:, 4 + c:5 + c]).then_inc(S["a_exp"], 1)

            def copy_pt(u):
                hd, n, w = units[u]
                act.wait_ge(S["a_tr"], base_u + u + 1)
                if u >= 2:
                    act.wait_ge(S["a_pv"], base_u + u - 1)
                if n < 4:
                    A(pt[:, u % 2, 0:w * (n + 1)], psum[:, 6, 0:w * (n + 1)], ACT.Copy).then_inc(S["a_pt"], 1)
                else:
                    A(pt[:, u % 2, 0:64], psum[:, 6, 0:64], ACT.Copy)
                    A(pt[0:16, u % 2, 64:80], psum[0:16, 6, 64:80], ACT.Copy).then_inc(S["a_pt"], 1)

            def out(u):
                hd, n, w = units[u]
                act.wait_ge(S["a_pv"], base_u + u + 1)
                r = slice(0, P) if maps == 2 else slice(64 * (hd % 2), 64 * (hd % 2) + 64)
                A(oT[r, hd * maps // 2, n * P:n * P + w], psum[r, 7, 0:w], ACT.Copy).then_inc(S["a_o"], 1)

            for u in range(LA_ACT):
                exps(u)
            for u in range(len(units)):
                if u + LA_ACT < len(units):
                    exps(u + LA_ACT)
                copy_pt(u)
                if u:
                    out(u - 1)
            out(len(units) - 1)

        def ffn(i, v, s_up, base):
            for g in range(N_UP):
                act.wait_ge(S["slot_used"], s_up + g + 1)
                if g == 0:
                    act.wait_ge(S["u_zero"], i + 1)
                if g >= 4:
                    act.wait_ge(S["conv_done"], N_UP * i + g - 3)
                A(halves(u_in[:, g % 4, 2:T2 + 2]), pair(g), ACT.Copy).then_inc(S["u_evac"], 1)
                if g % 2:
                    act.wait_ge(S["conv_done"], N_UP * i + g)
                    A(u_c[:, (g - 1) % 4, :], u_c[:, (g - 1) % 4, :], ACT.Silu).then_inc(S["silu_done"], 1)

        def x1_ready(k):
            act.wait_ge(S["x1_done"], k + 1)
            act.wait_ge(S["meta_in"], 16)

        squares(2, x1_ready)
        act.wait_ge(S["lam_sum"], 1)
        A(stat2[:, 2:4], psum[:, 0, 0:2], ACT.Exp).then_inc(S["lam_exp"], 1)
        act.wait_ge(S["qz_zero"], 1)
        for i in range(8):
            if i < 4:
                scatter(i, i, lambda m: qz[:, m // 2, m % 2, :])
            else:
                scatter(i, i - 4, lambda m: kz[:, m // 2, :])
        values(S_DA, 16, 0)
        attention(2, 8, 0, 0)
        act.wait_ge(S["a_prob"], 40)
        for hd in range(8):
            if hd >= 2:
                act.wait_ge(S["hd_sum"], hd - 1)
            A(prob(hd, 1), oT[:, hd, :], ACT.Square).then_inc(S["hd_sq"], 1)
            if hd:
                act.wait_ge(S["hd_var"], hd)
                A(prob(hd - 1, 0), prob(hd - 1, 0), ACT.Sqrt).then_inc(S["hd_std"], 1)
        act.wait_ge(S["hd_var"], 8)
        A(prob(7, 0), prob(7, 0), ACT.Sqrt).then_inc(S["hd_std"], 1)
        squares(3, lambda k: act.wait_ge(S["res_done"], k + 1))
        ffn(0, 3, S_UP0, 8)
        squares(4, lambda k: act.wait_ge(S["res_done"], 8 + k + 1))
        act.wait_ge(S["qz_zero"], 2)
        for i in range(8, 10):
            scatter(i, i - 8, lambda m: qiz[:, m // 2, m % 2, :])
        act.wait_ge(S["slot_used"], S_DSA + 6)
        A(halves(prob1(0)), pair(4), ACT.Square)
        A(halves(prob1(1)), pair(5), ACT.Square).then_inc(S["ki_sq"], 1)
        act.wait_ge(S["slot_used"], S_DSA + 7)
        A(halves(wch), pair(6), ACT.Copy).then_inc(S["wi_ch"], 1)
        act.wait_ge(S["ki_var"], 1)
        A(rope_t(1, 0), rope_t(1, 0), ACT.Sqrt).then_inc(S["ki_std"], 1)
        for i, (n, hd) in enumerate([(n, hd) for n in range(1, 5) for hd in range(8)]):
            act.wait_ge(S["i_sc"], i + 1)
            if i >= 2:
                act.wait_ge(S["i_acc"], i - 1)
            A(sc_sb(prob1(i % 2), n), idx_bank(i, n), ACT.Relu, scale=0.125).then_inc(S["i_relu"], 1)
        for i in range(10, 18):
            if i < 14:
                scatter(i, i - 10, lambda m: qz[:, m // 2, m % 2, :])
            else:
                scatter(i, i - 14, lambda m: kz[:, m // 2, :])
        values(S_DSA, 23, 8)
        attention(1, 16, 40, 80)
        squares(5, lambda k: act.wait_ge(S["res_done"], 16 + k + 1))
        ffn(1, 5, S_UP1, 24)
        squares(6, lambda k: act.wait_ge(S["res_done"], 24 + k + 1))

    def vector_block2(ve, st):
        V = nc.vector

        def norm(v, gain):
            ve.wait_ge(S["norm_sum"], v + 1)
            V.tensor_scalar(halves(rs[:, :]), psum[:, 6:8, 0:HALF], 1.0 / D, EPS, ALU.mult, ALU.add).then_inc(S["norm_var"], 1)
            ve.wait_ge(S["norm_std"], v + 1)
            st.link(V.reciprocal(rs[:, :], rs[:, :]))
            for k in range(KT):
                V.scalar_tensor_tensor(out=hn[:, k, :], in0=h[:, k, :], scalar=gain(k), in1=rs[:, :], op0=ALU.mult, op1=ALU.mult).then_inc(S["hn_ready"], 1)

        cos2, sin2 = halves(cosT), halves(sinT)

        def rope(i, s0, g):
            ve.wait_ge(S["slot_used"], s0 + g + 2)
            if i >= 2:
                ve.wait_ge(scattered[i % 2], 128 * (i // 2))
            a, b = pair(g), pair(g + 1)
            V.tensor_tensor(halves(rope_t(i, 0)), a, cos2, ALU.mult)
            V.tensor_tensor(halves(rope_t(i, 1)), b, sin2, ALU.mult)
            V.tensor_tensor(halves(rope_t(i, 2)), a, sin2, ALU.mult)
            V.tensor_tensor(halves(rope_t(i, 3)), b, cos2, ALU.mult).then_inc(S["rope_read"], 1)
            ve.wait_ge(S["rope_read"], i + 1)
            V.tensor_tensor(rope_t(i, 0), rope_t(i, 0), rope_t(i, 1), ALU.subtract)
            V.tensor_tensor(rope_t(i, 3), rope_t(i, 3), rope_t(i, 2), ALU.add).then_inc(S["rope_done"], 1)

        def values(base):
            for j in range(8):
                ve.wait_ge(S["v_tr"], base + j + 1)
                V.tensor_copy(vtok[:, 0:4, j * P:(j + 1) * P], psum[:, 6, :].rearrange("p (n m) -> p n m", n=4))
                V.tensor_copy(vtok[0:16, 4, j * P:(j + 1) * P], psum[0:16, 7, 0:P]).then_inc(S["v_tok"], 1)

        def attention(maps, heads, base_u, base_sc):
            units = [(hd, n, w) for hd in range(heads) for n, w in TILES]

            def soft(u):
                hd, n, w = units[u]
                s = stat[0:w, u % 4, :]
                for c in range(maps):
                    ve.wait_ge(S["a_sc"], base_sc + u * maps + c + 1)
                    if maps == 2:
                        axis = AX.X if n < 4 else AX.XY
                        st.did(V.tensor_reduce(s[:, c:c + 1], sc_bank(2, n, c), axis, ALU.max))
                    else:
                        if u >= 4:
                            ve.wait_ge(S["a_tr"], base_u + u - 3)
                        bias = sc_sb(sel[:, n - 1, :], n) if n else causalf[:, :]
                        st.did(V.tensor_tensor_reduce(out=sc_sb(prob(u, 0, 1), n), in0=sc_bank(1, n, 0), in1=bias, scale=0.125, scalar=-BIG,
                                                      op0=ALU.add, op1=ALU.max, accum_out=s[:, c:c + 1]))
                st.settle()
                V.tensor_scalar(s[:, 2:2 + maps], s[:, 0:maps], -0.125 if maps == 2 else -1.0, None, ALU.mult).then_inc(S["a_max"], 1)

            def normalise(u):
                hd, n, w = units[u]
                s = stat[0:w, u % 4, :]
                ve.wait_ge(S["a_exp"], base_sc + (u + 1) * maps)
                st.link(V.reciprocal(s[:, 6:6 + maps], s[:, 4:4 + maps]))
                p0 = prob(u, 0, maps)[0:w, 0:keys(n)]
                if maps == 2:
                    st.did(V.tensor_scalar(s[:, 7:8], s[:, 7:8], nlam[0:w], None, ALU.mult))
                    st.link(V.tensor_scalar(p0, p0, s[:, 6:7], None, ALU.mult))
                    V.scalar_tensor_tensor(out=p0, in0=prob(u, 1)[0:w, 0:keys(n)], scalar=s[:, 7:8], in1=p0, op0=ALU.mult, op1=ALU.add).then_inc(S["a_prob"], 1)
                else:
                    V.tensor_scalar(p0, p0, s[:, 6:7], None, ALU.mult).then_inc(S["a_prob"], 1)

            for u in range(LA_DVE):
                soft(u)
            for u in range(len(units)):
                if u + LA_DVE < len(units):
                    soft(u + LA_DVE)
                normalise(u)

        def residual(ready, base):
            for g in range(KT):
                ve.wait_ge(S["slot_used"], ready(g))
                V.tensor_tensor(halves(h[:, g, :]), halves(h[:, g, :]), pair(g), ALU.add).then_inc(S["res_done"], 1)

        def ffn(i, s_up, s_down, base):
            V.memset(u_in[:, :, 0:2], 0.0).then_inc(S["u_zero"], 1)
            for g in range(N_UP):
                n = N_UP * i + g
                ve.wait_ge(S["u_evac"], n + 1)
                w = [col("conv_w", 3 * N_UP * i + N_UP * j + g) for j in range(3)]
                c = u_c[:, g % 4, :]
                u = u_in[:, g % 4, :]
                st.link(V.tensor_scalar(c, u[:, 2:T2 + 2], w[2], col("conv_b", n), ALU.mult, ALU.add))
                st.link(V.scalar_tensor_tensor(out=c, in0=u[:, 1:T2 + 1], scalar=w[1], in1=c, op0=ALU.mult, op1=ALU.add))
                V.scalar_tensor_tensor(out=c, in0=u[:, 0:T2], scalar=w[0], in1=c, op0=ALU.mult, op1=ALU.add).then_inc(S["conv_done"], 1)
                if g % 2:
                    ve.wait_ge(S["silu_done"], (n + 1) // 2)
                    ve.wait_ge(S["conv_done"], n + 1)
                    V.tensor_tensor(act_t[:, g // 2, :], u_c[:, (g - 1) % 4, :], c, ALU.mult).then_inc(S["a_ready"], 1)
                    ve.wait_ge(S["a_ready"], (n + 1) // 2)
            residual(lambda g: s_down + 3 * (g + 1), base)

        V.tensor_tensor(stat2[:, 0:2], col("lam_q", 0, 2), col("lam_k", 0, 2), ALU.mult).then_inc(S["lam_prod"], 1)
        norm(2, lambda k: col("da_norm", k))
        ve.wait_ge(S["lam_exp"], 1)
        st.link(V.tensor_tensor(stat2[:, 4:5], stat2[:, 3:4], stat2[:, 2:3], ALU.subtract))
        st.did(V.tensor_scalar(stat2[:, 4:5], stat2[:, 4:5], -LAMBDA_INIT, None, ALU.add))
        st.link(V.tensor_scalar(stat2[:, 5:6], col("subln"), 1.0 - LAMBDA_INIT, None, ALU.mult))
        ve.wait_ge(S["rope_in"], 32)
        for i in range(8):
            rope(i, S_DA, 2 * i)
        values(0)
        attention(2, 8, 0, 0)
        for hd in range(8):
            ve.wait_ge(S["hd_sum"], hd + 1)
            V.tensor_scalar(halves(prob(hd, 0)), pair(hd), 1.0 / P, EPS, ALU.mult, ALU.add).then_inc(S["hd_var"], 1)
            ve.wait_ge(S["hd_std"], hd + 1)
            st.link(V.reciprocal(prob(hd, 0), prob(hd, 0)))
            V.scalar_tensor_tensor(out=oT[:, hd, :], in0=oT[:, hd, :], scalar=stat2[:, 5:6], in1=prob(hd, 0), op0=ALU.mult, op1=ALU.mult).then_inc(S["hd_done"], 1)
            ve.wait_ge(S["hd_done"], hd + 1)
        residual(lambda g: S_DAO + g + 1, 0)
        norm(3, lambda k: col("ffn_norm", k))
        ffn(0, S_UP0, S_DOWN0, 8)

        norm(4, lambda k: col("dsa_norm", k))
        for i in range(2):
            rope(8 + i, S_DSA, 2 * i)
        ve.wait_ge(S["ki_sum"], 1)
        ve.wait_ge(scattered[1], 128 * 5)
        V.tensor_scalar(halves(rope_t(1, 0)), psum[:, 6:8, 0:HALF], 1.0 / 256, EPS, ALU.mult, ALU.add).then_inc(S["ki_var"], 1)
        ve.wait_ge(S["ki_std"], 1)
        st.link(V.reciprocal(rope_t(1, 0), rope_t(1, 0)))
        ve.wait_ge(S["wi_ch"], 1)
        ve.wait_ge(scattered[0], 128 * 5)
        for j in range(2):
            V.scalar_tensor_tensor(out=halves(rope_t(1, 2 + j)), in0=pair(4 + j), scalar=col("idx_norm", j), in1=halves(rope_t(1, 0)),
                                   op0=ALU.mult, op1=ALU.mult).then_inc(S["ki_normed"], 1)
        ve.wait_ge(S["ki_normed"], 2)
        ka, kb = rope_t(1, 2), rope_t(1, 3)
        for q in range(4):
            r = slice(32 * q, 32 * q + 32)
            own, other = (ka, kb) if q % 2 == 0 else (kb, ka)
            st.did(V.tensor_tensor(rope_t(0, 0)[r], own[r], cosT[r], ALU.mult))
            st.did(V.tensor_tensor(rope_t(0, 1)[r], other[r], sinT[r], ALU.mult))
        st.settle()
        for q in range(4):
            r = slice(32 * q, 32 * q + 32)
            last = V.tensor_tensor(ki2[r], rope_t(0, 0)[r], rope_t(0, 1)[r], ALU.subtract if q % 2 == 0 else ALU.add)
        last.then_inc(S["ki_done"], 1)
        ve.wait_ge(S["wi_tr"], 1)
        for n, w in TILES[1:]:
            st.did(V.tensor_scalar(wtok[0:w, n - 1, :], psum[0:w, 6, (n - 1) * P:(n - 1) * P + 8], 8.0 ** -0.5, None, ALU.mult))
        st.settle()
        for i, (n, hd) in enumerate([(n, hd) for n in range(1, 5) for hd in range(8)]):
            w = TILES[n][1]
            ve.wait_ge(S["i_relu"], i + 1)
            s = sel[0:w, n - 1, 0:keys(n)]
            r = prob1(i % 2)[0:w, 0:keys(n)]
            if hd == 0:
                V.tensor_scalar(s, r, wtok[0:w, n - 1, 0:1], None, ALU.mult).then_inc(S["i_acc"], 1)
            else:
                V.scalar_tensor_tensor(out=s, in0=r, scalar=wtok[0:w, n - 1, hd:hd + 1], in1=s, op0=ALU.mult, op1=ALU.add).then_inc(S["i_acc"], 1)
            ve.wait_ge(S["i_acc"], i + 1)
            if hd == 7:
                d = sel[0:w, n - 1, n * P:n * P + w]
                st.did(V.tensor_tensor(d, d, causalf[0:w, 0:w], ALU.add))
                st.link(V.memset(sel[0:w, n - 1, 0:META], BIG))

        def take_eight(r):
            n, w = TILES[1 + r // 16]
            s = sel[0:w, n - 1, 0:keys(n)]
            st.link(V.max(top8[0:w, :], s))
            st.link(V.match_replace(out=s, in_to_replace=top8[0:w, :], in_values=s, imm_value=SELECTED))
            if r % 16 == 15:
                st.link(V.tensor_scalar(s, s, SELECTED, -BIG, ALU.not_equal, ALU.mult))

        for i in range(8):
            rope(10 + i, S_DSA, 7 + 2 * i)
            for r in range(8):
                take_eight(8 * i + r)
        values(8)
        attention(1, 16, 40, 80)
        residual(lambda g: S_DSAO + g + 1, 16)
        norm(5, lambda k: col("ffn_norm", 8 + k))
        ffn(1, S_UP1, S_DOWN1, 24)
        norm(6, lambda k: col("final_norm", k))

    @block.sync
    def _(sp):
        sp.dma_start(cols[:, :], ins["columns"]).then_inc(S["params_in"], 16)
        for k in range(2):
            sp.dma_start(h[:, 4 * k:4 * k + 4, META:T2], ins["xT"][:, 4 * k:4 * k + 4, :]).then_inc(S["x_in"], 16)
        sp.dma_start(h[:, :, 0:META], ins["metaT"]).then_inc(S["meta_in"], 16)
        for dst, name in ((loraW, "lora1"), (lora2, "lora2"), (ident[:, :], "ident"), (bones, "bones"), 
                          (causalf[:, :], "causalf"), (alibi, "alibi"), (rmask[:, :], "rmask"),
                          (lvlmask[:, :, :], "lvlmask"), (mask_in, "glamask"), (gblock[:, :], "gblock"),
                          (reset64[:, :], "reset64"), (reset128[:, :], "reset128")):
            sp.dma_start(dst, ins[name]).then_inc(S["consts_in"], 16)
        for r in range(RING):
            sp.dma_start(ring[:, r, :], ins["weights"][r]).then_inc(w_loaded[r], 16)
        turns = N_SLOTS // RING
        turns = N_SLOTS // RING
        with sp.Fori(1, turns) as turn:
            for r in range(RING):
                sp.wait_ge(S["slot_used"], turn * RING + (r - RING + 1))
                sp.dma_start(ring[:, r, :], ins["weights"][turn * RING + r]).then_inc(w_loaded[r], 16)
        for n in range(turns * RING, N_SLOTS):
            sp.wait_ge(S["slot_used"], n - RING + 1)
            sp.dma_start(ring[:, n % RING, :], ins["weights"][n]).then_inc(w_loaded[n % RING], 16)
        sp.wait_ge(S["hn_ready"], KT * 6)
        sp.dma_start(out_t, hn[:, :, META:T2]).then_inc(S["out_stored"], 16)
        sp.wait_ge(S["out_stored"], 16)

    @block.tensor
    def _(pe):
        mm = nc.tensor.matmul

        def slot(n):
            pe.wait_ge(w_loaded[n % RING], 16 * (n // RING + 1))
            return ring[:, n % RING, :].rearrange("p (k m) -> p k m", k=KT)

        def norm_sums1(v):
            for k in range(KT):
                pe.wait_ge(S["norm_sq"], KT * v + k + 1)
                last = mm(bank(1), ones[:, :], hn[:, k, 0:T1], start=k == 0, stop=k == KT - 1)
            last.then_inc(S["norm_sum"], 1)

        pe.wait_ge(S["zero_cols"], 1)
        norm_sums1(0)
        pe.wait_ge(S["c_silu"], 1)
        for m in range(N_ADA):
            w = slot(m)
            for k in range(KT):
                last = mm(psum[:, 0, m:m + 1], w[:, k, :], small[:, k:k + 1], start=k == 0, stop=k == KT - 1)
            last.then_inc(S["slot_used"], 1)

        def free_bank(n):
            if n >= 8:
                pe.wait_ge(S["in1_evac"], n - 7)

        def in1(item, g, rhs=lambda k: h1[:, k, 1:T1 + 1]):
            w = slot(S_IN1 + g)
            free_bank(item)
            for k in range(KT):
                if g == 0:
                    pe.wait_ge(S["hn_ready"], k + 1)
                last = mm(bank(item % 8), w[:, k, :], rhs(k), start=k == 0, stop=k == KT - 1 and g > 0)
            last.then_inc(S["slot_used"], 1)

        in1(0, 0)
        pe.wait_ge(S["shift_diff"], KT)
        pe.wait_ge(S["lora_scaled"], KT)
        for k in range(KT):
            last = mm(bank(0), loraW[:, k, :], zb_d(k), start=False, stop=k == KT - 1)
        last.then_inc(S["lora_done"], 1)
        for g in range(1, 8):
            in1(g, g)
        pe.wait_ge(S["in1_evac"], 2)
        for j in range(5):
            free_bank(8 + j)
            mm(bank((8 + j) % 8), lora2[:, j, :], (low if j < 4 else glow), start=True, stop=True).then_inc(S["lora_done"], 1)
        for g in range(8, N_IN1):
            in1(g + 5, g)

        def v1_transposes():
            pe.wait_ge(S["in1_evac"], ITEMS)
            for t in range(4):
                last = nc.tensor.transpose(psum[:, 7, t * P:(t + 1) * P], v1[:, t * P:(t + 1) * P], ident[:, :])
            last.then_inc(S["v1_trans"], 1)

        v1_transposes()
        units = [(n, g) for n in range(4) for g in range(4)]

        def s1_scores(u):
            n, g = units[u]
            lo = max(0, n - 1) * P
            w = (n + 1) * P - lo
            if u >= 3:
                pe.wait_ge(S["s1_soft"], u - 2)
            for s in range(2):
                last = mm(psum[:, u % 3, s * w:(s + 1) * w], qz1[:, g, s, n * P:(n + 1) * P], k1[:, lo:lo + w], start=True, stop=True)
            last.then_inc(S["s1_scores"], 1)

        def s1_transposes(u):
            n, g = units[u]
            blocks = 2 if n else 1
            pe.wait_ge(S["s1_prob"], u + 1)
            if u >= 1:
                pe.wait_ge(S["s1_pt"], u)
            for s in range(2):
                for b in range(blocks):
                    j = s * blocks + b
                    last = nc.tensor.transpose(psum[:, 6, j * P:(j + 1) * P], p1[:, u % 2, s, b * P:(b + 1) * P], ident[:, :])
            last.then_inc(S["s1_trans"], 1)

        def s1_values(u):
            n, g = units[u]
            blocks = 2 if n else 1
            pe.wait_ge(S["s1_pt"], u + 1)
            if u == 0:
                pe.wait_ge(S["v1_tok"], 1)
            if u >= 1:
                pe.wait_ge(S["s1_out"], u)
            for s in range(2):
                for b in range(blocks):
                    last = mm(psum[:, 7, s * P:(s + 1) * P], v1tok[:, max(0, n - 1) + b, :],
                              pt1[:, u % 2, (s * blocks + b) * P:(s * blocks + b + 1) * P], start=b == 0, stop=b == blocks - 1)
            last.then_inc(S["s1_pv"], 1)

        s1_scores(0)
        for u in range(16):
            if u + 1 < 16:
                s1_scores(u + 1)
            s1_transposes(u)
            if u >= 1:
                s1_values(u - 1)
        s1_values(15)

        for lv in range(8):
            if lv < 7:
                pe.wait_ge(S["g_lvl"], lv + 1)
            if lv == 0:
                pe.wait_ge(S["s1_out"], 16)
            else:
                pe.wait_ge(S["g_taken"], 4 * lv)
            for hd in range(4):
                r = slice(32 * hd, 32 * hd + 32)
                for c in range(4):
                    t = slice(c * P, (c + 1) * P)
                    kl, ql = (g_kl[r, lv % 2, t], g_ql[r, lv % 2, t]) if lv < 7 else (gk[r, t], gq[r, t])
                    last = mm(psum[:, hd, c * P:(c + 1) * P], kl, ql, start=True, stop=True)
                last.then_inc(S["g_score"], 1)
        for j in range(2):
            for c in range(4):
                last = nc.tensor.transpose(psum[:, 4 + j, c * P:(c + 1) * P], gv[:, j, c * P:(c + 1) * P], ident[:, :])
            last.then_inc(S["g_tr"], 1)
        pe.wait_ge(S["g_qk"], 1)
        for c in range(4):
            last = nc.tensor.transpose(psum[:, 6, c * P:(c + 1) * P], g_kd[:, c * P:(c + 1) * P], ident[:, :])
        last.then_inc(S["g_tr"], 1)
        pe.wait_ge(S["g_trc"], 7)
        pe.wait_ge(S["g_taken"], 32)
        for c in range(4):
            t = slice(c * P, (c + 1) * P)
            if c >= 1:
                pe.wait_ge(S["g_sc"], c)
            for j in range(2):
                o = psum[:, j, t]
                if c >= 1:
                    mm(o, g_s[:, c % 2, j * P:(j + 1) * P], g_qe[:, t], start=True, stop=False)
                for s in range(2):
                    last = mm(o, g_vz[:, c, 2 * j + s, :], g_at[:, 2 * j + s, t], start=c == 0 and s == 0, stop=s == 1)
            last.then_inc(S["g_ops"], 1)
            if c < 3:
                mm(psum[:, 7, 0:256], g_kt[:, c, :], g_vt[:, c, :], start=True, stop=True).then_inc(S["g_sd"], 1)
        for j in range(2):
            pe.wait_ge(S["g_osq"], j + 1)
            mm(bank(2 + j), bones, g_o_sq(j), start=True, stop=True).then_inc(S["g_osum"], 1)

        for i in range(2):
            pe.wait_ge(S["r_kksq"], i + 1)
            mm(bank(0), bones, r_e[:, 0, :], start=True, stop=True).then_inc(S["r_kksum"], 1)
            pe.wait_ge(S["r_bon"], i + 1)
            mm(bank(1), bones, r_rho, start=True, stop=True).then_inc(S["r_bonsum"], 1)
            pe.wait_ge(S["r_ready"], i + 1)
            for u in range(8):
                if u >= 4:
                    pe.wait_ge(S["r_masked"], 8 * i + u - 3)
                t = slice(u * 64, (u + 1) * 64)
                b = u % 4
                mm(psum[:, b, 0:P], rz(1, u), rz(0, u), start=True, stop=True)
                mm(psum[:, b, P:2 * P], rz(2, u), rz(0, u), start=True, stop=True)
                mm(psum[:, b, 2 * P:2 * P + 64], rz(1, u), r_rho[:, t], start=True, stop=True)
                mm(psum[:, b, 2 * P + 64:3 * P], rz(2, u), r_rho[:, t], start=True, stop=True).then_inc(S["r_prod"], 1)
                if u >= 2:
                    pe.wait_ge(S["r_toksb"], 8 * i + u - 1)
                for q in range(4):
                    last = nc.tensor.transpose(psum[:, 6 + u % 2, q * P:(q + 1) * P], rz(q, u), ident[:, :])
                last.then_inc(S["r_tokps"], 1)
            for lv in range(6):
                for u in range(8):
                    if u % 2 == 0:
                        pe.wait_ge(S["r_nready"], 24 * i + 4 * lv + u // 2 + 1)
                    last = mm(psum[:, 4 + u // 4, (u % 4) * P:(u % 4 + 1) * P], r_n[:, u, :], r_x[:, u, 0, :], start=True, stop=True)
                    if u % 4 == 3:
                        last.then_inc(S["r_tps"], 1)
                for u in range(8):
                    if u % 4 == 0:
                        pe.wait_ge(S["r_tsb"], 12 * i + 2 * lv + u // 4 + 1)
                    o = (u % 2) * 256
                    mm(psum[:, u // 2, o:o + P], r_x[:, u, 1, :], r_t[:, u, :], start=True, stop=True)
                    last = mm(psum[:, u // 2, o + P:o + 2 * P], r_t[:, u, :], r_x[:, u, 1, :], start=True, stop=True)
                    if u % 2:
                        last.then_inc(S["r_xps"], 1)
            pe.wait_ge(S["r_toksb"], 8 * (i + 1))
            pe.wait_ge(S["x_upd"], 4 * (i + 1))
            for u in range(8):
                o = (u % 4) * P
                mm(psum[:, 4 + u // 4, o:o + P], r_akt[:, u, :], r_tok[:, u, 3, :], start=True, stop=True)
                mm(psum[:, u // 4, o:o + P], r_tok[:, u, 0, :], r_x[:, u, 1, :], start=True, stop=True).then_inc(S["r_wps"], 1)
            pe.wait_ge(S["r_t1sb"], i + 1)
            pe.wait_ge(S["r_wsb"], i + 1)
            for c in range(8):
                n = 8 * i + c
                if c >= 1:
                    pe.wait_ge(S["r_ssb"], 7 * i + c)
                last = mm(psum[:, 6 + c % 2, 0:P], r_x[:, c, 1, :], r_t1[:, c, :], start=True, stop=c == 0)
                if c:
                    last = mm(psum[:, 6 + c % 2, 0:P], r_wt[:, c, :], r_s[:, c % 2, :], start=False, stop=True)
                last.then_inc(S["r_ups"], 1)
                pe.wait_ge(S["r_usb"], n + 1)
                if c < 7:
                    mm(psum[:, 2 + c % 2, 0:P], r_tok[:, c, 1, :], r_u[:, c % 2, :], start=True, stop=False)
                    mm(psum[:, 2 + c % 2, 0:P], r_tok[:, c, 2, :], r_tok[:, c, 3, :], start=False, stop=True).then_inc(S["r_sps"], 1)
                t = slice(c * 64, (c + 1) * 64)
                if c >= 2:
                    pe.wait_ge(S["r_ysb"], n - 1)
                y = psum[:, 4 + c % 2, 0:64]
                if c:
                    mm(y, r_s[:, c % 2, :], r_rho[:, t], start=True, stop=False)
                mm(y, r_u[:, c % 2, :], r_rbt[:, c, :], start=c == 0, stop=False)
                mm(y, r_tok[:, c, 3, :], r_rkt[:, c, :], start=False, stop=True).then_inc(S["r_yps"], 1)
            pe.wait_ge(S["r_ysb"], 8 * (i + 1))
            mm(bank(0), bones, sg[:, i, :], start=True, stop=True).then_inc(S["r_mean"], 1)
            pe.wait_ge(S["r_ysq"], i + 1)
            mm(bank(1), bones, r_e[:, 0, :], start=True, stop=True).then_inc(S["r_ysum"], 1)

        pe.wait_ge(S["r_done"], 2)
        pe.wait_ge(S["g_done"], 2)
        pe.wait_ge(S["s1_out"], 16)
        for g in range(N_OUT):
            w = slot(S_OUT1 + g)
            for k in range(KT):
                last = mm(bank(g), w[:, k, :], mix[:, k, :], start=k == 0, stop=k == KT - 1)
            last.then_inc(S["slot_used"], 1)
        pe.wait_ge(S["norm_sq"], KT + 2)
        norm_sums1(1)
        tensor_block2(pe)

    @block.gpsimd
    def _(pool):
        g = nc.gpsimd
        st = Steps(pool, S["pool_step"])
        g.memset(zb[:, :, 0:1], 0.0).then_inc(S["qz1_zeroed"], 1)
        g.memset(qz1, 0.0).then_inc(S["qz1_zeroed"], 1)
        pool.wait_ge(S["s1_out"], 16)
        pool.wait_ge(S["s1_pv"], 16)
        g.memset(g_at, 0.0).then_inc(S["g_zero"], 1)
        g.memset(g_vz, 0.0).then_inc(S["g_zero"], 1)
        pool.wait_ge(S["g_done"], 2)
        g.memset(r_z, 0.0).then_inc(S["r_zero"], 1)
        pool_block2(pool)

    @block.scalar
    def _(act):
        A = nc.scalar.activation
        st = Steps(act, S["act_step"])
        act.wait_ge(S["params_in"], 16)
        A(small[:, 0:8], col("c", 0, 8), ACT.Silu).then_inc(S["c_silu"], 1)
        act.wait_ge(S["x_in"], 32)
        for k in range(KT):
            A(hn[:, k, 0:T1], h[:, k, META:T2], ACT.Square).then_inc(S["norm_sq"], 1)
        act.wait_ge(S["norm_var"], 1)
        A(rs[:, 0:T1], rs[:, 0:T1], ACT.Sqrt).then_inc(S["norm_std"], 1)

        def take(item):
            if item < 8 and item != 0:
                act.wait_ge(S["slot_used"], S_IN1 + item + 1)
            elif item == 0:
                act.wait_ge(S["lora_done"], 1)
            elif item < 13:
                act.wait_ge(S["lora_done"], 2 + item - 8)
            else:
                act.wait_ge(S["slot_used"], S_IN1 + item - 5 + 1)
            return bank(item % 8)

        def evac(dst, item, func=ACT.Copy, part=slice(0, P), **kw):
            return A(dst, psum[part, item % 8, 0:T1], func, **kw)

        done = S["in1_evac"]
        take(0)
        evac(low[0:64, :], 0, ACT.Tanh, slice(0, 64))
        evac(low[64:P, :], 0, part=slice(64, P)).then_inc(done, 1)
        take(1)
        evac(glow, 1).then_inc(done, 1)
        for j in range(6):
            take(2 + j)
            evac(zb[:, j, 1:T1 + 1], 2 + j).then_inc(done, 1)
        for j in range(2):
            take(8 + j)
            evac(sg[:, j, :], 8 + j, ACT.Sigmoid, bias=col("w0", j)).then_inc(done, 1)
        for j in range(2):
            take(10 + j)
            evac(asig[:, j, :], 10 + j, ACT.Sigmoid, bias=col("a0", j)).then_inc(done, 1)
        take(12)
        evac(gz, 12, ACT.Identity, bias=col("gk_b")).then_inc(done, 1)
        take(13)
        evac(gq, 13, scale=32.0 ** -0.5).then_inc(done, 1)
        take(14)
        evac(gk, 14).then_inc(done, 1)
        for j in range(2):
            take(15 + j)
            evac(gv[:, j, :], 15 + j).then_inc(done, 1)
        act.wait_ge(S["qz1_zeroed"], 2)
        for j in range(4):
            take(17 + j)
            evac(qz1[0:64, j, 0, :], 17 + j, part=slice(0, 64))
            evac(qz1[64:P, j, 1, :], 17 + j, part=slice(64, P)).then_inc(done, 1)
        take(21)
        evac(k1, 21).then_inc(done, 1)
        take(22)
        evac(v1, 22).then_inc(done, 1)
        for j in range(4):
            take(23 + j)
            evac(agate[:, j, :], 23 + j, ACT.Silu).then_inc(done, 1)
        for j in range(2):
            take(27 + j)
            evac(rgate[:, j, :], 27 + j, ACT.Silu).then_inc(done, 1)
        for j in range(2):
            take(29 + j)
            evac(ggate[:, j, :], 29 + j, ACT.Silu).then_inc(done, 1)

        act.wait_ge(S["g_absz"], 1)
        st.link(A(norm_tmp[:, 0:T1], norm_tmp[:, 0:T1], ACT.Exp))
        A(norm_tmp[:, 0:T1], norm_tmp[:, 0:T1], ACT.Ln, bias=1.0).then_inc(S["g_ln"], 1)

        act.wait_ge(S["v1_trans"], 1)
        A(v1tok, psum[:, 7, 0:512].rearrange("p (a b) -> p a b", a=4), ACT.Copy).then_inc(S["v1_tok"], 1)

        def s1_exp(u):
            n, g = divmod(u, 4)
            w = 256 if n else P
            act.wait_ge(S["s1_soft"], u + 1)
            o = 24 + 8 * (u % 2)
            for s in range(2):
                A(p1[:, u % 2, s, 0:w], p1[:, u % 2, s, 0:w], ACT.Exp, bias=small[:, o + 2 + s:o + 3 + s],
                  accum_out=small[:, o + 4 + s:o + 5 + s])
            A(small[:, o + 6:o + 8], small[:, o + 6:o + 8], ACT.Exp).then_inc(S["s1_exp"], 1)

        def s1_copy(u):
            n, g = divmod(u, 4)
            w = 4 * P if n else 2 * P
            act.wait_ge(S["s1_trans"], u + 1)
            if u >= 2:
                act.wait_ge(S["s1_pv"], u - 1)
            A(pt1[:, u % 2, 0:w], psum[:, 6, 0:w], ACT.Copy).then_inc(S["s1_pt"], 1)

        s1_exp(0)
        for u in range(16):
            if u + 1 < 16:
                s1_exp(u + 1)
            s1_copy(u)

        act.wait_ge(S["g_cum"], 1)
        A(g_d[:, 0, :], g_b, ACT.Exp, scale=1.0 / 16).then_inc(S["g_exp"], 1)
        A(g_d[:, 1, :], g_d[:, 1, :], ACT.Exp, scale=1.0 / 16).then_inc(S["g_exp"], 1)
        for lv in range(7):
            act.wait_ge(S["g_diff"], lv + 1)
            A(g_e(lv), g_e(lv), ACT.Exp, scale=1.0 / 16).then_inc(S["g_exp"], 1)
        act.wait_ge(S["g_zero"], 2)
        for j in range(2):
            act.wait_ge(S["g_tr"], j + 1)
            src = psum[:, 4 + j, 0:512].rearrange("p (c m) -> p c m", c=4)
            A(g_vt[:, :, j * P:(j + 1) * P], src, ACT.Copy).then_inc(S["g_trc"], 1)
            for s in range(2):
                A(g_vz[:, :, 2 * j + s, 64 * s:64 * s + 64], src[:, :, 64 * s:64 * s + 64], ACT.Copy).then_inc(S["g_trc"], 1)
        act.wait_ge(S["g_tr"], 3)
        A(g_kt, psum[:, 6, 0:512].rearrange("p (c m) -> p c m", c=4), ACT.Copy).then_inc(S["g_trc"], 1)
        act.wait_ge(S["g_ost"], 4)
        for j in range(2):
            A(g_o_sq(j), g_o[:, j, :], ACT.Square).then_inc(S["g_osq"], 1)
        for j in range(2):
            act.wait_ge(S["g_ovar"], j + 1)
            A(g_kl[:, j, :], g_kl[:, j, :], ACT.Sqrt).then_inc(S["g_ostd"], 1)

        for i in range(2):
            act.wait_ge(S["r_kkraw"], i + 1)
            A(r_e[:, 0, :], r_kk, ACT.Square).then_inc(S["r_kksq"], 1)
            act.wait_ge(S["r_kksum"], i + 1)
            A(norm_tmp[:, 0:T1], bank(0), ACT.Sqrt).then_inc(S["r_kkstd"], 1)
            act.wait_ge(S["r_decay"], i + 1)
            A(r_e[:, 0, :], r_e[:, 0, :], ACT.Exp)
            A(r_e[:, 1, :], r_b, ACT.Exp, scale=-1.0)
            A(r_e[:, 2, :], r_b, ACT.Exp).then_inc(S["r_exps"], 1)
            for u in range(8):
                act.wait_ge(S["r_tokps"], 8 * i + u + 1)
                A(r_tok[:, u, :, :], psum[:, 6 + u % 2, 0:512].rearrange("p (q m) -> p q m", q=4), ACT.Copy).then_inc(S["r_toksb"], 1)
            for lv in range(6):
                for q in range(2):
                    act.wait_ge(S["r_tps"], 12 * i + 2 * lv + q + 1)
                    A(r_t[:, 4 * q:4 * q + 4, :], psum[:, 4 + q, :].rearrange("p (u m) -> p u m", u=4), ACT.Copy).then_inc(S["r_tsb"], 1)
            act.wait_ge(S["r_wps"], 8 * (i + 1))
            A(r_t1[:, 0:4, :], psum[:, 4, :].rearrange("p (u m) -> p u m", u=4), ACT.Copy)
            A(r_t1[:, 4:8, :], psum[:, 5, :].rearrange("p (u m) -> p u m", u=4), ACT.Copy).then_inc(S["r_t1sb"], 1)
            for c in range(8):
                n = 8 * i + c
                act.wait_ge(S["r_ups"], n + 1)
                if c >= 2:
                    act.wait_ge(S["r_yps"], n - 1)
                A(r_u[:, c % 2, :], psum[:, 6 + c % 2, 0:P], ACT.Copy).then_inc(S["r_usb"], 1)
                act.wait_ge(S["r_yps"], n + 1)
                A(sg[:, i, c * 64:(c + 1) * 64], psum[:, 4 + c % 2, 0:64], ACT.Copy).then_inc(S["r_ysb"], 1)
            act.wait_ge(S["r_cent"], i + 1)
            A(r_e[:, 0, :], sg[:, i, :], ACT.Square).then_inc(S["r_ysq"], 1)
            act.wait_ge(S["r_yvar"], i + 1)
            A(r_e[:, 1, :], r_e[:, 1, :], ACT.Sqrt).then_inc(S["r_ystd"], 1)

        for g in range(N_OUT):
            act.wait_ge(S["slot_used"], S_OUT1 + g + 1)
            A(y1(g), bank(g), ACT.Copy)
            A(hn[:, g, 0:T1], bank(g), ACT.Square).then_inc(S["norm_sq"], 1)
        act.wait_ge(S["norm_var"], 2)
        A(rs[:, 0:T1], rs[:, 0:T1], ACT.Sqrt).then_inc(S["norm_std"], 1)
        act_block2(act)

    @block.vector
    def _(ve):
        V = nc.vector
        st = Steps(ve, S["dve_step"])
        V.memset(ones[:, :], 1.0).then_inc(S["zero_cols"], 1)
        ve.wait_ge(S["params_in"], 16)
        ve.wait_ge(S["consts_in"], 16 * 12)
        V.tensor_copy(identb[:, :], ident[:, :])
        V.tensor_copy(causalb[:, :], causalf[:, :])
        V.tensor_copy(glamask[:, :, :], mask_in)
        ve.wait_ge(S["norm_sum"], 1)
        V.tensor_scalar(rs[:, 0:T1], bank(1), 1.0 / D, 1e-6, ALU.mult, ALU.add).then_inc(S["norm_var"], 1)
        ve.wait_ge(S["norm_std"], 1)
        V.memset(h1[:, :, 0:1], 0.0)
        st.link(V.reciprocal(rs[:, 0:T1], rs[:, 0:T1]))
        ve.wait_ge(S["slot_used"], N_ADA)
        st.link(V.tensor_tensor(ada[:, :], psum[:, 0, 0:24], col("ada_b", 0, 24), ALU.add))
        V.scalar_tensor_tensor(out=small[:, 8:16], in0=ada[:, 8:16], scalar=1.0, in1=col("norm_pre", 0, 8), op0=ALU.add, op1=ALU.mult)
        st.link(V.tensor_tensor(small[:, 16:24], ada[:, 16:24], col("norm_post", 0, 8), ALU.mult))
        for k in range(KT):
            st.did(V.scalar_tensor_tensor(out=h1[:, k, 1:T1 + 1], in0=h[:, k, META:T2], scalar=small[:, 8 + k:9 + k],
                                          in1=rs[:, 0:T1], op0=ALU.mult, op1=ALU.mult))
        st.settle()
        for k in range(KT):
            V.tensor_scalar(h1[:, k, 1:T1 + 1], h1[:, k, 1:T1 + 1], ada[:, k:k + 1], None, ALU.add).then_inc(S["hn_ready"], 1)
        for k in range(KT):
            ve.wait_ge(S["hn_ready"], k + 1)
            V.tensor_tensor(zb_d(k), h1[:, k, 0:T1], h1[:, k, 1:T1 + 1], ALU.subtract).then_inc(S["shift_diff"], 1)
            V.tensor_scalar(loraW[:, k, 0:64], loraW[:, k, 0:64], col("mu_w", k), None, ALU.mult)
            V.tensor_scalar(loraW[:, k, 64:P], loraW[:, k, 64:P], col("mu_a", k), None, ALU.mult).then_inc(S["lora_scaled"], 1)
        ve.wait_ge(S["qz1_zeroed"], 1)
        for j in range(6):
            ve.wait_ge(S["in1_evac"], 3 + j)
            st.link(V.tensor_tensor(dmix, zb[:, j, 0:T1], zb[:, j, 1:T1 + 1], ALU.subtract))
            st.link(V.scalar_tensor_tensor(out=zb[:, j, 1:T1 + 1], in0=dmix, scalar=col("mu_rkv", j), in1=zb[:, j, 1:T1 + 1],
                                           op0=ALU.mult, op1=ALU.add))
        ve.wait_ge(S["in1_evac"], 13)
        V.scalar_tensor_tensor(out=norm_tmp[:, 0:T1], in0=gz, scalar=-1.0, in1=gz, op0=ALU.mult, op1=ALU.min).then_inc(S["g_absz"], 1)
        ve.wait_ge(S["g_ln"], 1)
        st.link(V.scalar_tensor_tensor(out=gz, in0=gz, scalar=0.0, in1=norm_tmp[:, 0:T1], op0=ALU.min, op1=ALU.subtract))

        ve.wait_ge(S["in1_evac"], ITEMS)

        def s1_max(u):
            n, g = divmod(u, 4)
            w = 256 if n else P
            o = 24 + 8 * (u % 2)
            ve.wait_ge(S["s1_scores"], u + 1)
            if u >= 2:
                ve.wait_ge(S["s1_trans"], u - 1)
            for s in range(2):
                st.did(V.tensor_tensor_reduce(out=p1[:, u % 2, s, 0:w], in0=psum[:, u % 3, s * w:(s + 1) * w],
                                              in1=alibi[:, g + 4 * s, 256 - w:256], scale=0.125, scalar=-BIG, op0=ALU.add, op1=ALU.max,
                                              accum_out=small[:, o + s:o + s + 1]))
            st.settle()
            sinks = cols[:, COL["sinks"][0] + g:COL["sinks"][0] + g + 5:4]
            st.link(V.tensor_tensor(small[:, o:o + 2], small[:, o:o + 2], sinks, ALU.max))
            V.tensor_tensor(small[:, o + 6:o + 8], sinks, small[:, o:o + 2], ALU.subtract)
            V.tensor_scalar(small[:, o + 2:o + 4], small[:, o:o + 2], -1.0, None, ALU.mult).then_inc(S["s1_soft"], 1)

        def s1_normalise(u):
            n, g = divmod(u, 4)
            w = 256 if n else P
            o = 24 + 8 * (u % 2)
            ve.wait_ge(S["s1_exp"], u + 1)
            st.link(V.tensor_tensor(small[:, o + 4:o + 6], small[:, o + 4:o + 6], small[:, o + 6:o + 8], ALU.add))
            st.link(V.reciprocal(small[:, o + 4:o + 6], small[:, o + 4:o + 6]))
            V.tensor_scalar(p1[:, u % 2, 0, 0:w], p1[:, u % 2, 0, 0:w], small[:, o + 4:o + 5], None, ALU.mult)
            V.tensor_scalar(p1[:, u % 2, 1, 0:w], p1[:, u % 2, 1, 0:w], small[:, o + 5:o + 6], None, ALU.mult).then_inc(S["s1_prob"], 1)

        def s1_gate(u):
            n, g = divmod(u, 4)
            t = slice(n * P, (n + 1) * P)
            ve.wait_ge(S["s1_pv"], u + 1)
            V.tensor_tensor(mix[0:64, g, t], psum[0:64, 7, 0:P], agate[0:64, g, t], ALU.mult)
            V.tensor_tensor(mix[64:P, g, t], psum[64:P, 7, P:2 * P], agate[64:P, g, t], ALU.mult).then_inc(S["s1_out"], 1)

        s1_max(0)
        for u in range(16):
            if u + 1 < 16:
                s1_max(u + 1)
            s1_normalise(u)
            if u >= 1:
                s1_gate(u - 1)
        s1_gate(15)

        ve.wait_ge(S["s1_out"], 16)
        st.link(V.tensor_tensor_scan(g_b, reset128[:, :], gz, 0.0, ALU.mult, ALU.add))
        b128 = g_b.rearrange("p (n w) -> p n w", w=P)
        V.tensor_tensor(g_d[:, 1, :].rearrange("p (n w) -> p n w", w=P), b128[:, :, P - 1:P].to_broadcast([P, 4, P]), b128, ALU.subtract).then_inc(S["g_cum"], 1)
        ve.wait_ge(S["g_exp"], 2)
        V.tensor_tensor(g_qe, gq, g_d[:, 0, :], ALU.mult)
        V.tensor_tensor(g_kd, gk, g_d[:, 1, :], ALU.mult).then_inc(S["g_qk"], 1)

        def g_distance(lv):
            s = 1 << lv
            bb = g_b.rearrange("p (n w) -> p n w", w=2 * s)
            e = g_e(lv)
            st.link(V.tensor_tensor(e.rearrange("p (n w) -> p n w", w=2 * s), bb, bb[:, :, s - 1:s].to_broadcast([P, T1 // (2 * s), 2 * s]), ALU.subtract))
            V.scalar_tensor_tensor(out=e, in0=e, scalar=-1.0, in1=e, op0=ALU.mult, op1=ALU.min).then_inc(S["g_diff"], 1)

        def g_take(lv):
            if lv == 0:
                ve.wait_ge(S["g_zero"], 1)
            for hd in range(4):
                ve.wait_ge(S["g_score"], 4 * lv + hd + 1)
                V.copy_predicated(g_at[:, hd, :].rearrange("p (c m) -> p c m", c=4),
                                  glamask[:, lv:lv + 1, :].to_broadcast([P, 4, P]),
                                  psum[:, hd, :].rearrange("p (c m) -> p c m", c=4)).then_inc(S["g_taken"], 1)

        for lv in range(7):
            g_distance(lv)
            if lv >= 1:
                g_take(lv - 1)
            ve.wait_ge(S["g_exp"], 2 + lv + 1)
            V.tensor_tensor(g_ql[:, lv % 2, :], gq, g_e(lv), ALU.mult)
            V.tensor_tensor(g_kl[:, lv % 2, :], gk, g_e(lv), ALU.mult).then_inc(S["g_lvl"], 1)
        g_take(6)
        g_take(7)
        for c in range(4):
            t = slice(c * P, (c + 1) * P)
            ve.wait_ge(S["g_ops"], c + 1)
            V.tensor_copy(g_o[:, 0:2, t], psum[:, 0:2, t]).then_inc(S["g_ost"], 1)
            if c < 3:
                ve.wait_ge(S["g_sd"], c + 1)
                nxt = g_s[:, (c + 1) % 2, :]
                if c == 0:
                    V.tensor_tensor(nxt, psum[:, 7, 0:256], gblock[:, :], ALU.mult).then_inc(S["g_sc"], 1)
                else:
                    st.link(V.tensor_tensor(nxt, psum[:, 7, 0:256], gblock[:, :], ALU.mult))
                    V.scalar_tensor_tensor(out=nxt, in0=g_s[:, c % 2, :], scalar=g_d[:, 0, (c + 1) * P - 1:(c + 1) * P], in1=nxt,
                                           op0=ALU.mult, op1=ALU.add).then_inc(S["g_sc"], 1)
        for j in range(2):
            ve.wait_ge(S["g_osum"], j + 1)
            V.tensor_scalar(g_kl[:, j, :], bank(2 + j), 1.0 / 64, 1e-5, ALU.mult, ALU.add).then_inc(S["g_ovar"], 1)
        for j in range(2):
            ve.wait_ge(S["g_ostd"], j + 1)
            st.link(V.reciprocal(g_kl[:, j, :], g_kl[:, j, :]))
            st.link(V.scalar_tensor_tensor(out=g_kl[:, j, :], in0=g_kl[:, j, :], scalar=col("gla_norm"), in1=g_o[:, j, :], op0=ALU.mult, op1=ALU.mult))
            V.tensor_tensor(mix[:, 6 + j, :], g_kl[:, j, :], ggate[:, j, :], ALU.mult).then_inc(S["g_done"], 1)

        ve.wait_ge(S["r_zero"], 1)
        for i in range(2):
            if i:
                ve.wait_ge(S["r_done"], i)
            zr, zk, zv = (zb[:, 2 * q + i, 1:T1 + 1] for q in range(3))
            V.tensor_scalar(r_kk, zk, col("k_k", i), None, ALU.mult).then_inc(S["r_kkraw"], 1)
            st.link(V.tensor_scalar(r_e[:, 1, :], sg[:, i, :], -math.exp(-0.5), None, ALU.mult))
            st.link(V.tensor_tensor_scan(r_b, reset64[:, :], r_e[:, 1, :], 0.0, ALU.mult, ALU.add))
            st.link(V.tensor_scalar(small[:, 40:41], col("k_a", i), -1.0, 1.0, ALU.mult, ALU.add))
            st.link(V.tensor_scalar(r_rho, asig[:, i, :], col("k_a", i), small[:, 40:41], ALU.mult, ALU.add))
            st.link(V.tensor_tensor(zk, zk, r_rho, ALU.mult))
            V.scalar_tensor_tensor(out=r_rho, in0=zr, scalar=col("r_k", i), in1=zk, op0=ALU.mult, op1=ALU.mult).then_inc(S["r_bon"], 1)
            ve.wait_ge(S["r_kkstd"], i + 1)
            V.tensor_tensor(r_e[:, 0, :], r_b, r_e[:, 1, :], ALU.subtract).then_inc(S["r_decay"], 1)
            st.link(V.tensor_scalar(norm_tmp[:, 0:T1], norm_tmp[:, 0:T1], 1e-12, None, ALU.max))
            st.link(V.reciprocal(norm_tmp[:, 0:T1], norm_tmp[:, 0:T1]))
            st.link(V.tensor_tensor(r_kk, r_kk, norm_tmp[:, 0:T1], ALU.mult))
            ve.wait_ge(S["r_bonsum"], i + 1)
            V.tensor_tensor(mix[:, 4 + i, :], bank(1), zv, ALU.mult)
            ve.wait_ge(S["r_exps"], i + 1)

            def chunks(v, s):
                return v[64 * s:64 * s + 64].rearrange("p (c t) -> p c t", c=8)

            for s in range(2):
                st.did(V.tensor_tensor(rz_half(0, s), chunks(r_kk, s), chunks(r_e[:, 0, :], s), ALU.mult))
                st.did(V.tensor_tensor(rz_half(2, s), chunks(zk, s), chunks(r_e[:, 1, :], s), ALU.mult))
                st.did(V.tensor_copy(rz_half(3, s), chunks(zv, s)))
            st.did(V.tensor_tensor(r_rho, zr, r_e[:, 2, :], ALU.mult))
            st.settle()
            st.link(V.tensor_tensor(r_kk, r_kk, asig[:, i, :], ALU.mult))
            V.tensor_tensor(rz_half(1, 0), chunks(r_kk, 0), chunks(r_e[:, 1, :], 0), ALU.mult)
            V.tensor_tensor(rz_half(1, 1), chunks(r_kk, 1), chunks(r_e[:, 1, :], 1), ALU.mult).then_inc(S["r_ready"], 1)
            for u in range(8):
                ve.wait_ge(S["r_prod"], 8 * i + u + 1)
                b = u % 4
                V.tensor_tensor(r_lt[:, u, :], psum[:, b, 0:P], rmask[:, 0:P], ALU.mult)
                V.tensor_tensor(r_akt[:, u, :], psum[:, b, P:2 * P], rmask[:, P:2 * P], ALU.mult)
                V.tensor_tensor(r_rbt[:, u, :], psum[:, b, 2 * P:2 * P + 64], rmask[:, 2 * P:2 * P + 64], ALU.mult)
                V.tensor_tensor(r_rkt[:, u, :], psum[:, b, 2 * P + 64:3 * P], rmask[:, 2 * P + 64:3 * P], ALU.mult).then_inc(S["r_masked"], 1)
                st.did(V.tensor_copy(r_x[:, u, :, :], ident[:, :].rearrange("p (a m) -> p a m", a=1).to_broadcast([P, 2, P])))
            st.settle()
            ve.wait_ge(S["r_masked"], 8 * (i + 1))
            for q in range(4):
                two = slice(2 * q, 2 * q + 2)
                V.tensor_tensor(r_n[:, two, :], r_lt[:, two, :], lvlmask[:, 0:1, :].to_broadcast([P, 2, P]), ALU.mult).then_inc(S["r_nready"], 1)
            for lv in range(6):
                for q in range(4):
                    two = slice(2 * q, 2 * q + 2)
                    ve.wait_ge(S["r_xps"], 24 * i + 4 * lv + q + 1)
                    upd = V.tensor_tensor(r_x[:, two, :, :], r_x[:, two, :, :], psum[:, q, :].rearrange("p (u a m) -> p u a m", u=2, a=2), ALU.add)
                    if lv < 5:
                        V.tensor_tensor(r_n[:, two, :], r_lt[:, two, :], lvlmask[:, lv + 1:lv + 2, :].to_broadcast([P, 2, P]), ALU.mult).then_inc(S["r_nready"], 1)
                    else:
                        upd.then_inc(S["x_upd"], 1)
            ve.wait_ge(S["r_wps"], 8 * (i + 1))
            V.tensor_scalar(r_wt[:, 0:4, :], psum[:, 0, :].rearrange("p (u m) -> p u m", u=4), -1.0, None, ALU.mult)
            V.tensor_scalar(r_wt[:, 4:8, :], psum[:, 1, :].rearrange("p (u m) -> p u m", u=4), -1.0, None, ALU.mult).then_inc(S["r_wsb"], 1)
            for c in range(7):
                nxt = r_s[:, (c + 1) % 2, :]
                e = r_e[:, 2, 64 * c + 63:64 * c + 64]
                if c:
                    st.link(V.tensor_scalar(r_se, r_s[:, c % 2, :], e, None, ALU.mult))
                ve.wait_ge(S["r_sps"], 7 * i + c + 1)
                if c >= 1:
                    ve.wait_ge(S["r_yps"], 8 * i + c)
                if c:
                    V.scalar_tensor_tensor(out=nxt, in0=psum[:, 2 + c % 2, 0:P], scalar=e, in1=r_se, op0=ALU.mult, op1=ALU.add).then_inc(S["r_ssb"], 1)
                else:
                    V.tensor_scalar(nxt, psum[:, 2 + c % 2, 0:P], e, None, ALU.mult).then_inc(S["r_ssb"], 1)
                ve.wait_ge(S["r_ssb"], 7 * i + c + 1)
            ve.wait_ge(S["r_mean"], i + 1)
            V.scalar_tensor_tensor(out=sg[:, i, :], in0=bank(0), scalar=-1.0 / 64, in1=sg[:, i, :], op0=ALU.mult, op1=ALU.add).then_inc(S["r_cent"], 1)
            ve.wait_ge(S["r_ysum"], i + 1)
            V.tensor_scalar(r_e[:, 1, :], bank(1), 1.0 / 64, 64e-5, ALU.mult, ALU.add).then_inc(S["r_yvar"], 1)
            ve.wait_ge(S["r_ystd"], i + 1)
            st.link(V.reciprocal(r_e[:, 1, :], r_e[:, 1, :]))
            st.link(V.scalar_tensor_tensor(out=r_e[:, 1, :], in0=sg[:, i, :], scalar=col("ln_w", i), in1=r_e[:, 1, :], op0=ALU.mult, op1=ALU.mult))
            st.link(V.scalar_tensor_tensor(out=r_e[:, 1, :], in0=r_e[:, 1, :], scalar=col("ln_b", i), in1=mix[:, 4 + i, :], op0=ALU.add, op1=ALU.add))
            V.tensor_tensor(mix[:, 4 + i, :], r_e[:, 1, :], rgate[:, i, :], ALU.mult).then_inc(S["r_done"], 1)

        ve.wait_ge(S["norm_sum"], 2)
        V.tensor_scalar(rs[:, 0:T1], bank(1), 1.0 / D, 1e-6, ALU.mult, ALU.add).then_inc(S["norm_var"], 1)
        ve.wait_ge(S["norm_std"], 2)
        st.link(V.reciprocal(rs[:, 0:T1], rs[:, 0:T1]))
        for g in range(KT):
            st.did(V.scalar_tensor_tensor(out=y1(g), in0=y1(g), scalar=small[:, 16 + g:17 + g], in1=rs[:, 0:T1], op0=ALU.mult, op1=ALU.mult))
        st.settle()
        for g in range(KT):
            V.tensor_tensor(h[:, g, META:T2], h[:, g, META:T2], y1(g), ALU.add).then_inc(S["x1_done"], 1)
        vector_block2(ve, st)
    ctx.close()


def _groups(w):
    k, m = w.shape
    return w.reshape(k // P, P, m // P, P).transpose(2, 1, 0, 3).reshape(m // P, P, k)


def _down(w):
    g = _groups(w)
    out = np.zeros((g.shape[0], 3, P, KT * P), w.dtype)
    for j in range(3):
        n = min(KT * P, FFN - j * KT * P)
        out[:, j, :, :n] = g[:, :, j * KT * P:j * KT * P + n]
    return out.reshape(-1, P, KT * P)


def _pad_cols(w, n):
    return np.concatenate([w, np.zeros((w.shape[0], n - w.shape[1]), w.dtype)], axis=1)


def _rope_split(w, heads):
    k = w.shape[0]
    return w.reshape(k, heads // 4, 4, 2, 32).transpose(0, 1, 3, 2, 4).reshape(k, heads * 64)


def _vec(v):
    return v.reshape(-1, P).T


def _layout(a):
    f = {k: np.asarray(v) for k, v in a.items()}
    one = {k: (v[0] if v.ndim and v.shape[0] == 1 else v) for k, v in f.items()}
    w_in = one["w_in"]
    cut = np.cumsum([512, 128, 128, 512, 768, 256, 128, 128, 256, 256])
    aq, ak, av, ag, rkv, rg, gq, gk, gv, gg = np.split(w_in, cut[:-1], axis=1)
    pairs = np.arange(8).reshape(2, 4).T.reshape(-1)

    def by_pair(w):
        return w.reshape(w.shape[0], 8, 64)[:, pairs].reshape(w.shape[0], 512)

    lora1 = np.concatenate([one["rwkv_w1"], one["rwkv_a1"]], axis=1)
    w_out = one["w_out"]
    w_out = np.concatenate([w_out[:512].reshape(8, 64, D)[pairs].reshape(512, D), w_out[512:]], axis=0)
    dsa = one["dsa_w_in_2"]
    dq, dk, dv, qi, ki, wi = np.split(dsa, np.cumsum([1024, 1024, 1024, 512, 64]), axis=1)
    qkv = one["da_w_qkv_2"]
    up, down = f["ffn_w_up_2"], f["ffn_w_down_2"]

    def mixed_up(w):
        return w.reshape(D, 2, FT, P).transpose(0, 2, 1, 3).reshape(D, 2 * FFN)

    streams = [
        _groups(one["ada_w"]),
        _groups(lora1), _groups(_pad_cols(one["gla_gk1"], P)), _groups(rkv), _groups(gq), _groups(gk), _groups(gv),
        _groups(by_pair(aq)), _groups(ak), _groups(av), _groups(by_pair(ag)), _groups(rg), _groups(gg),
        _groups(w_out),
        _groups(_rope_split(qkv[:, :1024], 16)), _groups(_rope_split(qkv[:, 1024:2048], 16)), _groups(qkv[:, 2048:]),
        _groups(one["da_w_o_2"]),
        _groups(mixed_up(up[0])), _down(down[0]),
        _groups(_rope_split(qi, 8)), _groups(np.tile(ki[:, :32], (1, 4))), _groups(np.tile(ki[:, 32:], (1, 4))),
        _groups(_pad_cols(wi, P)),
        _groups(_rope_split(dq, 16)), _groups(_rope_split(dk, 16)), _groups(dv),
        _groups(one["dsa_w_o_2"]),
        _groups(mixed_up(up[1])), _down(down[1]),
    ]
    weights = np.concatenate(streams, axis=0)
    assert weights.shape[0] == N_SLOTS, (weights.shape, N_SLOTS)

    def block_cols(v):
        return v.reshape(2, FT, P).transpose(1, 0, 2).reshape(-1, P).T

    zero64 = np.zeros((64,), w_in.dtype)
    w2, a2, gk2 = one["rwkv_w2"], one["rwkv_a2"], one["gla_gk2"]
    lora2 = np.zeros((P, 5, P), w_in.dtype)
    for j in range(2):
        lora2[0:64, j] = w2[:, j * P:(j + 1) * P]
        lora2[64:P, 2 + j] = a2[:, j * P:(j + 1) * P]
    lora2[0:16, 4] = gk2
    parts = {
        "c": _vec(f["c"][0]), "ada_b": _vec(one["ada_b"]), "norm_pre": _vec(one["norm_pre"]), "norm_post": _vec(one["norm_post"]),
        "mu_rkv": _vec(one["rwkv_mu_rkv"]), "mu_w": _vec(one["rwkv_mu_w"]), "mu_a": _vec(one["rwkv_mu_a"]),
        "w0": _vec(one["rwkv_w0"]), "a0": _vec(one["rwkv_a0"]), "k_k": _vec(one["rwkv_k_k"]), "k_a": _vec(one["rwkv_k_a"]),
        "r_k": _vec(one["rwkv_r_k"].reshape(-1)), "ln_w": _vec(one["rwkv_ln_w"]), "ln_b": _vec(one["rwkv_ln_b"]),
        "gk_b": _vec(one["gla_gk_b"]), "gla_norm": _vec(np.tile(one["gla_norm_w"], 2)),
        "da_norm": _vec(one["da_norm_2"]), "subln": _vec(one["da_subln_2"]), "dsa_norm": _vec(one["dsa_norm_2"]),
        "ffn_norm": np.concatenate([_vec(v) for v in f["ffn_norm_2"]], axis=1), "final_norm": _vec(f["final_norm_2"]),
        "conv_w": np.concatenate([block_cols(f["ffn_conv_w_2"][i, j]) for i in range(2) for j in range(3)], axis=1),
        "conv_b": np.concatenate([block_cols(f["ffn_conv_b_2"][i]) for i in range(2)], axis=1),
        "lam_q": np.stack([np.concatenate([one[f"da_lambda_q{i}_2"], zero64]) for i in (1, 2)], axis=1),
        "lam_k": np.stack([np.concatenate([one[f"da_lambda_k{i}_2"], zero64]) for i in (1, 2)], axis=1),
        "idx_norm": np.stack([np.tile(one["dsa_idx_k_norm_2"][:32], 4), np.tile(one["dsa_idx_k_norm_2"][32:], 4)], axis=1),
        "sinks": np.broadcast_to(one["attn_sinks"][None, :], (P, 8)),
    }
    columns = np.concatenate([parts[n] for n, _ in COLUMNS], axis=1)

    def tokens_last(x):
        return np.ascontiguousarray(x.T.reshape(KT, P, -1).transpose(1, 0, 2))

    return {
        "weights": weights, "columns": np.ascontiguousarray(columns), "xT": tokens_last(f["x"][0]), "metaT": tokens_last(f["meta_tokens_2"]),
        "lora1": np.ascontiguousarray(lora1.reshape(KT, P, P).transpose(1, 0, 2)), "lora2": lora2,
        **_constants(),
    }


def _constants():
    f32 = np.float32
    i = np.arange(P)
    eye = np.eye(P, dtype=f32)
    same64 = i[:, None] // 64 == i[None, :] // 64
    causal = np.where(i[None, :] <= i[:, None], 0.0, -BIG)
    dist = i[:, None] - np.arange(2 * P)[None, :] + P
    slopes = 2.0 ** (-np.arange(1, 9))
    alibi = np.where((dist >= 0) & (dist < P), 0.0, -BIG)[:, None, :] - 8.0 * slopes[None, :, None] * dist[:, None, :]
    j, q = i[:, None], i[None, :]
    strict = same64 & (j < q)
    incl = (j % 64) <= np.arange(64)[None, :]
    rmask = np.concatenate([strict, -1.0 * strict, incl, incl], axis=1)
    lvl = []
    for n in range(6):
        s = 1 << n
        lvl.append(-1.0 * ((j // (2 * s) == q // (2 * s)) & (j % (2 * s) < s) & (q % (2 * s) >= s)))
    gla = [((j // (2 * s) == q // (2 * s)) & (j % (2 * s) < s) & (q % (2 * s) >= s)) for s in (1 << np.arange(7))]
    gla.append(j == q)
    gblock = (i[:, None] // 32 == np.arange(256)[None, :] // 64)
    t = np.arange(T1)
    inv = (f32(10000.0) ** (-np.arange(0, 64, 2, dtype=f32) / f32(64))).astype(f32)
    ang = (np.arange(T2, dtype=f32)[:, None] * inv[None, :]).astype(f32)
    return {
        "ident": eye, "bones": same64.astype(f32), 
        "causalf": causal.astype(f32),
        "alibi": alibi.astype(f32), "rmask": rmask.astype(f32), "lvlmask": np.stack(lvl, axis=1).astype(f32),
        "glamask": np.stack(gla, axis=1).astype(f32), "gblock": gblock.astype(f32),
        "reset64": np.broadcast_to((t % 64 != 0).astype(f32), (P, T1)).copy(), "reset128": np.broadcast_to((t % P != 0).astype(f32), (P, T1)).copy(),
        "cosT": np.tile(np.cos(ang).T, (4, 1)).astype(f32), "sinT": np.tile(np.sin(ang).T, (4, 1)).astype(f32),
    }


def kernel(**inputs):
    import concourse.bacc as bacc
    from concourse.bass_utils import run_bass_kernel_spmd

    arrays = {f"in_{k}": np.ascontiguousarray(v) for k, v in _layout(inputs).items()}
    nc = bacc.Bacc("TRN2", target_bir_lowering=False, num_devices=1)
    ins = {k[3:]: nc.dram_tensor(k, v.shape, mybir.dt.from_np(v.dtype), kind="ExternalInput").ap() for k, v in arrays.items()}
    out_t = nc.dram_tensor("out_t", (P, KT, T1), mybir.dt.float32, kind="ExternalOutput").ap()
    build(nc, ins, out_t)
    r = run_bass_kernel_spmd(nc, [arrays], core_ids=[0])
    got = r.results[0]["out_t"]
    return np.ascontiguousarray(got.transpose(2, 1, 0).reshape(1, T1, D))
```

```python
import math
from contextlib import ExitStack

import numpy as np

from concourse import mybir

P = 128
D = 1024
KT = D // P
T1 = 512
META = 16
T2 = T1 + META
HALF = T2 // 2
FFN = 2816
FT = FFN // P
RING = 8
RAW = 4
SPLIT = 2
BIG = 1e30
LAMBDA_INIT = 0.8 - 0.6 * math.exp(0.0)

COLUMNS = [
    ("ada_b", 24), ("norm_pre", 8), ("norm_post", 8), ("mu_rkv", 6), ("mu_w", 8), ("mu_a", 8),
    ("w0", 2), ("a0", 2), ("k_k", 2), ("k_a", 2), ("r_k", 2), ("ln_w", 2), ("ln_b", 2), ("gk_b", 1),
    ("gla_norm", 1), ("da_norm", 8), ("subln", 1), ("dsa_norm", 8), ("ffn_norm", 16), ("final_norm", 8),
    ("conv_w", 6 * FT * 2), ("conv_b", 2 * FT * 2), ("lam_q", 2), ("lam_k", 2), ("idx_norm", 2), ("sinks", 8),
]
COL = {}
_at = 0
for _name, _n in COLUMNS:
    COL[_name] = (_at, _n)
    _at += _n
NCOL = _at

N_ADA = 24
N_IN1 = 26
N_OUT = 8
N_DA = 24
N_DSA = 31
N_UP = 2 * FT
N_DOWN = 3 * KT
S_IN1 = N_ADA
S_OUT1 = S_IN1 + N_IN1
S_DA = S_OUT1 + N_OUT
S_DAO = S_DA + N_DA
S_UP0 = S_DAO + N_OUT
S_DOWN0 = S_UP0 + N_UP
S_DSA = S_DOWN0 + N_DOWN
S_DSAO = S_DSA + N_DSA
S_UP1 = S_DSAO + N_OUT
S_DOWN1 = S_UP1 + N_UP
N_SLOTS = S_DOWN1 + N_DOWN


def build(nc, ins, out_t):
    F32 = mybir.dt.float32
    BF16 = mybir.dt.bfloat16
    U8 = mybir.dt.uint8
    ALU = mybir.AluOpType
    ACT = mybir.ActivationFunctionType
    AX = mybir.AxisListType

    ctx = ExitStack()

    def sb(name, shape, dt=F32):
        return ctx.enter_context(nc.sbuf_tensor(name, shape, dt))

    def sem(name):
        return ctx.enter_context(nc.semaphore(name))

    class Steps:

        def __init__(self, eng, counter):
            self.eng, self.counter, self.n = eng, counter, 0

        def did(self, ins):
            ins.then_inc(self.counter, 1)
            self.n += 1
            return ins

        def settle(self):
            self.eng.wait_ge(self.counter, self.n)

        def link(self, ins):
            self.did(ins)
            self.settle()

    psum = ctx.enter_context(nc.psum_tensor("banks", [P, 8, 512], F32))
    h = sb("h", [P, KT, T2])
    cols = sb("cols", [P, NCOL])
    ident = sb("ident", [P, P])
    ones = sb("ones", [P, P])
    identb = sb("identb", [P, P], BF16)
    causalb = sb("causalb", [P, P], BF16)
    rs = sb("rs", [P, T2])
    ada = sb("ada", [P, 24])
    small = sb("small", [P, 64])
    stat = sb("stat", [P, 4, 8])
    stat2 = sb("stat2", [P, 8])
    nlam = stat2[:, 4:5]
    wtok = sb("wtok", [P, 4, 8])
    top8 = sb("top8", [P, 8])
    causalf = sb("causalf", [P, P])

    F32R = mybir.dt.float32r
    first = ExitStack()
    ARENA = 30500
    arena = first.enter_context(nc.sbuf_tensor("arena", [P, ARENA], F32))
    ring = first.enter_context(nc.sbuf_tensor("ring", [P, RING, KT * P], F32))
    hn_raw = first.enter_context(nc.sbuf_tensor("hn_raw", [P, KT * (T2 + 1)], F32))
    hn1 = hn_raw[:, 0:KT * T2].rearrange("p (k t) -> p k t", k=KT)
    h1 = hn_raw[:, 0:KT * (T1 + 1)].rearrange("p (k t) -> p k t", k=KT)
    norm_tmp = first.enter_context(nc.sbuf_tensor("norm_tmp", [P, T2], F32))

    class Carve:

        def __init__(self, base, size):
            self.base, self.size, self.at = base, size, 0

        def take(self, *dims):
            n = int(np.prod(dims))
            v = self.base[:, self.at:self.at + n]
            self.at += n
            assert self.at <= self.size, (self.at, self.size)
            names = "abcd"[:len(dims)]
            if len(dims) == 1:
                return v
            return v.rearrange("p (" + " ".join(names) + ") -> p " + " ".join(names), **dict(zip(names[:-1], dims[:-1])))

    def col(name, i=0, n=1):
        a = COL[name][0] + i
        return cols[:, a:a + n]

    c1 = Carve(arena, ARENA)
    bones = c1.take(P)
    agate = c1.take(4, T1)
    rgate = c1.take(2, T1)
    ggate = c1.take(2, T1)
    mix = c1.take(8, T1)
    mix_flat = mix.rearrange("p k t -> p (k t)")
    cond = mix_flat[:, 0:D]
    ada_out = mix_flat[:, D:3 * D].rearrange("p (a d) -> p a d", a=2)
    zb = c1.take(6, T1 + 1)
    sg = c1.take(2, T1)
    asig = c1.take(2, T1)
    front = c1.at
    gq = c1.take(T1)
    gk = c1.take(T1)
    gv = c1.take(2, T1)
    gz = c1.take(T1)
    low = c1.take(T1)
    glow = c1.take(T1)
    att_at = c1.at
    qz1 = c1.take(4, 2, T1)
    k1 = c1.take(T1)
    v1 = c1.take(T1)
    tail_at = c1.at
    alibi = c1.take(8, 256)
    loraW = c1.take(KT, P)
    lora2 = c1.take(5, P)
    dmix = c1.take(T1)
    mask_in = c1.take(8, P)
    ca = Carve(hn_raw, KT * (T2 + 1))
    p1 = ca.take(2, 2, 256)
    pt1 = ca.take(2, 4 * P)
    v1tok = ca.take(4, P)
    cg = Carve(arena[:, att_at:ARENA], ARENA - att_at)
    g_b = cg.take(T1)
    g_d = cg.take(2, T1)
    g_ql = cg.take(2, T1)
    g_kl = cg.take(2, T1)
    g_vz = cg.take(4, 4, P)
    g_vt = cg.take(4, 256)
    g_kt = cg.take(4, P)
    g_qe = cg.take(T1)
    g_es = cg.take(2, T1)
    ch = Carve(hn_raw, KT * (T2 + 1))
    g_at = ch.take(4, T1)
    g_kd = ch.take(T1)
    g_s = ch.take(2, 256)
    g_o = ch.take(2, T1)
    cr = Carve(arena[:, front:ARENA], ARENA - front)
    r_kk = cr.take(T1)
    r_b = cr.take(T1)
    r_e = cr.take(3, T1)
    r_rho = cr.take(T1)
    r_lt = cr.take(8, P)
    r_akt = cr.take(8, P)
    r_rbt = cr.take(8, 64)
    r_rkt = cr.take(8, 64)
    r_x = cr.take(8, 2, P)
    r_t = cr.take(8, P)
    r_n = cr.take(8, P)
    r_tok = cr.take(8, 4, P)
    r_wt = cr.take(8, P)
    r_t1 = cr.take(8, P)
    r_s = cr.take(2, P)
    r_se = cr.take(P)
    r_u = cr.take(2, P)
    ck = Carve(hn_raw, KT * (T2 + 1))
    r_z = ck.take(4, 8, P)
    y1_buf = Carve(arena[:, front:ARENA], ARENA - front).take(KT, T1)
    rmask = first.enter_context(nc.sbuf_tensor("rmask", [P, 2 * P + 128], F32))
    lvlmask = first.enter_context(nc.sbuf_tensor("lvlmask", [P, 6, P], F32))
    glamask = first.enter_context(nc.sbuf_tensor("glamask", [P, 8, P], U8))
    gblock = first.enter_context(nc.sbuf_tensor("gblock", [P, 256], F32))
    reset64 = first.enter_context(nc.sbuf_tensor("reset64", [P, T1], F32))
    reset128 = first.enter_context(nc.sbuf_tensor("reset128", [P, T1], F32))
    first.close()

    ARENA2 = 29376
    raw = sb("raw", [P, RAW, KT * P])
    w_hi = sb("w_hi", [P, SPLIT, KT * P], F32R)
    w_lo = sb("w_lo", [P, SPLIT, KT * P], F32R)
    hn_hi = sb("hn_hi", [P, KT, T2], F32R)
    hn_lo = sb("hn_lo", [P, KT, T2], F32R)
    sq = sb("sq", [P, 2, T2])
    second = ExitStack()
    arena2 = second.enter_context(nc.sbuf_tensor("arena2", [P, ARENA2], F32))
    cb = Carve(arena2, ARENA2)
    cosT = cb.take(T2)
    sinT = cb.take(T2)
    kz = cb.take(8, T2)
    rope_buf = cb.take(2, 4, T2)
    oT = rope_buf.rearrange("p a b t -> p (a b) t")
    vch = cb.take(2, T2)
    wch = vch[:, 0, :]
    pt = cb.take(2, 4 * P)
    prob_buf = cb.take(4, 2, T2)
    prob_flat = prob_buf.rearrange("p a b t -> p (a b) t")
    ki2 = prob_flat[:, 3, :]
    sel = prob_flat[:, 4:8, :]
    assert cb.at <= ARENA2 - 8 * 2 * T2 - 5 * 1024
    cb.at = ARENA2 - 8 * 2 * T2 - 5 * 1024
    vtok = cb.take(5, 1024)
    qz = cb.take(8, 2, T2)
    qiz = vtok.rearrange("p a b -> p (a b)")[:, 0:8 * T2].rearrange("p (a b t) -> p a b t", a=4, b=2)
    second.close()
    third = ExitStack()
    third.enter_context(nc.sbuf_tensor("tables_again", [P, 2 * T2], F32))
    a_hi = third.enter_context(nc.sbuf_tensor("a_hi", [P, FT, T2], F32R))
    a_lo = third.enter_context(nc.sbuf_tensor("a_lo", [P, FT, T2], F32R))
    u_in = third.enter_context(nc.sbuf_tensor("u_in", [P, 4, T2 + 2], F32))
    u_c = third.enter_context(nc.sbuf_tensor("u_c", [P, 4, T2], F32))
    third.close()

    def rope_t(i, j):
        return rope_buf[:, i % 2, j, :]

    def prob(u, c, maps=2):
        return prob_buf[:, u % 4, c, :] if maps == 2 else prob_flat[:, u % 4, :]

    def prob1(j):
        return prob_flat[:, j, :]

    w_loaded = [sem(f"w_loaded{r}") for r in range(RING)]
    raw_loaded = [sem(f"raw_loaded{r}") for r in range(RAW)]
    names = """slot_used params_in x_in consts_in meta_in out_stored dve_step act_step pool_step
        c_exp c_in c_silu norm_sq norm_sum norm_var norm_std hn_ready shift_diff lora_scaled
        lora_low lora_done in1_evac qz1_zeroed zero_cols mixed
        s1_scores s1_soft s1_sinkd s1_exp s1_prob s1_trans s1_pt s1_pv s1_out v1_trans v1_tok
        g_absz g_ln g_cum g_diff g_exp g_lvl g_score g_taken g_zero g_tr g_trc g_qk g_sc g_sd g_ops g_ost g_osq g_osum g_ovar g_ostd g_done
        r_zero r_kkraw r_kksq r_kksum r_kkstd r_decay r_exps r_ready r_bon r_bonsum r_prod r_masked r_tokps r_toksb
        r_nready r_tps r_tsb r_xps r_wps r_t1sb r_wsb r_ups r_usb r_sps r_ssb r_yps r_ysb
        r_mean r_cent r_ysq r_ysum r_yvar r_ystd r_done x_upd x1_done
            rope_in qz_zero lam_prod lam_sum lam_exp rope_read rope_done v_ch v_tr v_tok a_sc a_max a_exp a_prob a_tr a_pt a_pv a_o
            hd_sq hd_sum hd_var hd_std hd_done res_done u_zero u_evac conv_done silu_done a_ready
            w_hi_done w_split sq_used normed x_hi o_hi o_split prod_done a_hi_done final_done
            ki_sq ki_sum ki_var ki_std ki_normed ki_done wi_ch wi_tr i_sc i_relu i_acc""".split()
    scattered = [sem(f"scattered{i}") for i in range(2)]
    S = {n: sem(n) for n in names}
    block = ctx.enter_context(nc.Block())

    def bank(b, n=T1):
        return psum[:, b, 0:n]

    def pair(g, parts=P):
        return psum[0:parts, 2 * (g % 3):2 * (g % 3) + 2, 0:HALF]

    def halves(v):
        return v.rearrange("p (a b) -> p a b", a=2)

    ITEMS = 31

    def zb_d(k):
        return mix[:, k, :]

    def rz(q, u):
        return r_z[:, q, u, :]

    def rz_half(q, s):
        return r_z[64 * s:64 * s + 64, q, :, 64 * s:64 * s + 64]

    def g_e(lv):
        return g_es[:, lv % 2, :]

    def y1(g):
        return y1_buf[:, g, :]

    def g_o_sq(j):
        return g_ql[:, j, :]

    TILES = [(n, min(P, T2 - n * P)) for n in range(5)]
    EPS = 1e-6
    SELECTED = float(np.float32(-3e38))
    TOPK = 128
    LA_PE, LA_DVE, LA_ACT = 3, 2, 2

    def keys(n):
        return min((n + 1) * P, T2)

    def banks_of(b, n):
        if n < 4:
            return psum[:, b, 0:keys(n)]
        return psum[0:16, b:b + 2, 0:HALF]

    def idx_bank(i, n):
        return banks_of(2 * (i % 3), n)

    def sc_bank(maps, n, c):
        if maps == 1:
            return banks_of(n, n)
        return banks_of(2 * (n % 3) + c if n < 4 else 2 + 2 * c, n)

    def sc_sb(v, n):
        return v[:, 0:keys(n)] if n < 4 else halves(v[0:16, :])

    def hn_base(v):
        return KT * (v - 1)

    def tensor_block2(pe):
        mm = nc.tensor.matmul

        def slot(n):
            pe.wait_ge(S["w_split"], n - S_DA + 1)
            return [w[:, (n - S_DA) % SPLIT, :].rearrange("p (k m) -> p k m", k=KT) for w in (w_hi, w_lo)]

        def both(g, w, x, j, k, first, last):
            for a in range(2):
                t = slice(a * HALF, (a + 1) * HALF)
                o = psum[:, 2 * (g % 3) + a, 0:HALF]
                mm(o, w[0][:, j, :], x[0][:, k, t], start=first, stop=False)
                mm(o, w[0][:, j, :], x[1][:, k, t], start=False, stop=False)
                ins_ = mm(o, w[1][:, j, :], x[0][:, k, t], start=False, stop=last)
            return ins_

        def sums(v):
            for k in range(KT):
                pe.wait_ge(S["norm_sq"], KT * v + k + 1)
                for a in range(2):
                    last = mm(psum[:, 6 + a, 0:HALF], ones[:, :], sq[:, k % 2, a * HALF:(a + 1) * HALF], start=k == 0, stop=k == KT - 1)
                last.then_inc(S["sq_used"], 1)

        def project(s0, groups, v, free, after=None):
            for g in groups:
                w = slot(s0 + g)
                if g >= 3:
                    free(g - 3)
                for k in range(KT):
                    if g == 0:
                        pe.wait_ge(S["hn_ready"], hn_base(v) + k + 1)
                    last = both(g, w, (hn_hi, hn_lo), k, k, k == 0, k == KT - 1)
                last.then_inc(S["slot_used"], 1)
                if after:
                    after(g)

        def v_transpose(j, base):
            pe.wait_ge(S["v_ch"], base + j + 1)
            if j >= 1:
                pe.wait_ge(S["v_tok"], base + j)
            for n, w in TILES:
                dst = psum[:, 6, n * P:(n + 1) * P] if n < 4 else psum[0:16, 7, 0:P]
                last = nc.tensor.transpose(dst, vch[:, j % 2, n * P:n * P + w], ident[:, :])
            last.then_inc(S["v_tr"], 1)

        def attention(maps, heads, base_u, base_sc):
            units = [(hd, n, w) for hd in range(heads) for n, w in TILES]

            def free_scores(u, c):
                hd, n, w = units[u]
                if maps == 1:
                    if hd:
                        pe.wait_ge(S["a_max"], base_u + u - 4)
                elif n < 3:
                    if hd:
                        pe.wait_ge(S["a_exp"], base_sc + (2 * u - 2, 2 * u - 3, 2 * u - 4)[n])
                elif n == 3:
                    pe.wait_ge(S["a_exp"], base_sc + 2 * u - 4)
                else:
                    pe.wait_ge(S["a_exp"], base_sc + 2 * u - 4 + 2 * c)

            def scores(u):
                hd, n, w = units[u]
                for c in range(maps):
                    free_scores(u, c)
                    m = hd * maps + c
                    q = qz[:, m // 2, m % 2, n * P:n * P + w]
                    o = sc_bank(maps, n, c)
                    masked = maps == 2
                    if n < 4:
                        last = mm(o, q, kz[:, m // 2, 0:keys(n)], start=True, stop=not masked)
                        if masked:
                            last = mm(o[:, n * P:(n + 1) * P], identb[:, :], causalb[:, :], start=False, stop=True)
                    else:
                        mm(o[:, 0, :], q, kz[:, m // 2, 0:HALF], start=True, stop=True)
                        last = mm(o[:, 1, :], q, kz[:, m // 2, HALF:T2], start=True, stop=not masked)
                        if masked:
                            last = mm(o[:, 1, 4 * P - HALF:HALF], identb[:, 0:16], causalb[:, 0:16], start=False, stop=True)
                    last.then_inc(S["a_sc"], 1)

            def transposes(u):
                hd, n, w = units[u]
                pe.wait_ge(S["a_prob"], base_u + u + 1)
                if u >= 1:
                    pe.wait_ge(S["a_pt"], base_u + u)
                for j in range(n + 1):
                    kj = TILES[j][1]
                    last = nc.tensor.transpose(psum[0:kj, 6, j * w:(j + 1) * w], prob(u, 0, maps)[0:w, j * P:j * P + kj], ident[0:w, 0:w])
                last.then_inc(S["a_tr"], 1)

            def values(u):
                hd, n, w = units[u]
                pe.wait_ge(S["a_pt"], base_u + u + 1)
                if u >= 1:
                    pe.wait_ge(S["a_o"], base_u + u)
                e = (hd * maps // 2) * P
                for j in range(n + 1):
                    kj = TILES[j][1]
                    last = mm(psum[:, 7, 0:w], vtok[0:kj, j, e:e + P], pt[0:kj, u % 2, j * w:(j + 1) * w], start=j == 0, stop=j == n)
                last.then_inc(S["a_pv"], 1)

            for u in range(LA_PE):
                scores(u)
            for u in range(len(units)):
                if u + LA_PE < len(units):
                    scores(u + LA_PE)
                transposes(u)
                if u:
                    values(u - 1)
            values(len(units) - 1)

        def residual(s0, base, first_free):
            for g in range(KT):
                w = slot(s0 + g)
                if g >= 3:
                    pe.wait_ge(S["res_done"], base + g - 2)
                else:
                    first_free(g)
                for k in range(KT):
                    if g == 0:
                        pe.wait_ge(S["o_split"], base // 2 + k + 1)
                    last = both(g, w, (hn_hi, hn_lo), k, k, k == 0, k == KT - 1)
                last.then_inc(S["slot_used"], 1)

        def ffn(i, v, s_up, s_down, base):
            def free(g):
                pe.wait_ge(S["u_evac"], N_UP * i + g + 1)
            project(s_up, range(N_UP), v, free)
            n = s_down
            for g in range(KT):
                if g >= 3:
                    pe.wait_ge(S["res_done"], base + g - 2)
                else:
                    pe.wait_ge(S["u_evac"], N_UP * (i + 1))
                for part in range(3):
                    w = slot(n)
                    for k in range(8 * part, min(8 * part + 8, FT)):
                        if g == 0:
                            pe.wait_ge(S["a_ready"], FT * i + k + 1)
                        last = both(g, w, (a_hi, a_lo), k % 8, k, k == 0, k == FT - 1)
                    last.then_inc(S["slot_used"], 1)
                    n += 1

        sums(2)
        pe.wait_ge(S["lam_prod"], 1)
        mm(psum[:, 0, 0:2], ones[:, :], stat2[:, 0:2], start=True, stop=True).then_inc(S["lam_sum"], 1)
        pe.wait_ge(S["lam_exp"], 1)

        def da_free(g):
            if g < 16:
                pe.wait_ge(S["rope_read"], g // 2 + 1)
            else:
                pe.wait_ge(S["v_ch"], g - 16 + 1)

        def da_after(g):
            if g > 16:
                v_transpose(g - 17, 0)
        project(S_DA, range(N_DA), 2, da_free, da_after)
        v_transpose(7, 0)
        for b in range(2):
            pe.wait_ge(scattered[b], 128 * 4)
        pe.wait_ge(S["v_tok"], 8)
        attention(2, 8, 0, 0)
        for hd in range(8):
            pe.wait_ge(S["hd_sq"], hd + 1)
            if hd >= 3:
                pe.wait_ge(S["hd_var"], hd - 2)
            for a in range(2):
                last = mm(psum[:, 2 * (hd % 3) + a, 0:HALF], ones[:, :], prob(hd, 1)[:, a * HALF:(a + 1) * HALF], start=True, stop=True)
            last.then_inc(S["hd_sum"], 1)

        def da_o_free(g):
            pe.wait_ge(S["hd_var"], 8)
        residual(S_DAO, 0, da_o_free)
        sums(3)
        ffn(0, 3, S_UP0, S_DOWN0, 8)

        sums(4)

        def dsa_free(g):
            if g < 4:
                pe.wait_ge(S["rope_read"], 8 + g // 2 + 1)
            elif g < 6:
                pe.wait_ge(S["ki_normed"], 1)
            elif g == 6:
                pe.wait_ge(S["wi_ch"], 1)
            elif g < 23:
                pe.wait_ge(S["rope_read"], 10 + (g - 7) // 2 + 1)
            else:
                pe.wait_ge(S["v_ch"], 8 + g - 23 + 1)

        project(S_DSA, range(7), 4, dsa_free)
        pe.wait_ge(S["ki_sq"], 1)
        for j in range(2):
            for a in range(2):
                last = mm(psum[:, 6 + a, 0:HALF], ones[:, :], prob1(j)[:, a * HALF:(a + 1) * HALF], start=j == 0, stop=j == 1)
        last.then_inc(S["ki_sum"], 1)
        pe.wait_ge(S["ki_var"], 1)
        pe.wait_ge(S["wi_ch"], 1)
        for n, w in TILES[1:]:
            last = nc.tensor.transpose(psum[0:w, 6, (n - 1) * P:n * P], wch[:, n * P:n * P + w], ident[:, :])
        last.then_inc(S["wi_tr"], 1)
        for b in range(2):
            pe.wait_ge(scattered[b], 128 * 5)
        pe.wait_ge(S["ki_done"], 1)
        pe.wait_ge(S["wi_ch"], 1)
        for i, (n, hd) in enumerate([(n, hd) for n in range(1, 5) for hd in range(8)]):
            w = TILES[n][1]
            if i >= 3:
                pe.wait_ge(S["i_relu"], i - 2)
            q = qiz[:, hd // 2, hd % 2, n * P:n * P + w]
            if n < 4:
                last = mm(psum[:, 2 * (i % 3), 0:keys(n)], q, ki2[:, 0:keys(n)], start=True, stop=True)
            else:
                for a in range(2):
                    last = mm(psum[0:16, 2 * (i % 3) + a, 0:HALF], q, ki2[:, a * HALF:(a + 1) * HALF], start=True, stop=True)
            last.then_inc(S["i_sc"], 1)
        pe.wait_ge(S["i_relu"], 32)

        def dsa_free2(g):
            if g >= 7:
                dsa_free(g)

        def dsa_after(g):
            if g > 23:
                v_transpose(g - 24, 8)
        project(S_DSA, range(7, N_DSA), 4, dsa_free2, dsa_after)
        v_transpose(7, 8)
        for b in range(2):
            pe.wait_ge(scattered[b], 128 * 9)
        pe.wait_ge(S["v_tok"], 16)
        attention(1, 16, 40, 80)

        def dsa_o_free(g):
            pe.wait_ge(S["a_max"], 120)
        residual(S_DSAO, 16, dsa_o_free)
        sums(5)
        ffn(1, 5, S_UP1, S_DOWN1, 24)
        sums(6)

    def pool_block2(pool):
        g = nc.gpsimd

        def weight_rest(n):
            pool.wait_ge(S["w_hi_done"], n - S_DA + 1)
            w = (n - S_DA) % SPLIT
            g.tensor_tensor(w_lo[:, w, :], raw[:, (n - S_DA) % RAW, :], w_hi[:, w, :].bitcast(F32), ALU.subtract).then_inc(S["w_split"], 1)

        def output_rests(base):
            for k in range(KT):
                pool.wait_ge(S["o_hi"], base + k + 1)
                g.tensor_tensor(hn_lo[:, k, :], oT[:, k, :], hn_hi[:, k, :].bitcast(F32), ALU.subtract).then_inc(S["o_split"], 1)

        def ffn(i, s_up):
            def product_rest(m):
                pool.wait_ge(S["a_hi_done"], FT * i + m + 1)
                g.tensor_tensor(a_lo[:, m, :], u_c[:, (2 * m + 1) % 4, :], a_hi[:, m, :].bitcast(F32), ALU.subtract).then_inc(S["a_ready"], 1)

            for j in range(2, N_UP + 2):
                weight_rest(s_up + j)
                if j >= 5 and j % 2:
                    product_rest((j - 5) // 2)
            product_rest(FT - 1)
            for j in range(N_UP + 2, N_UP + N_DOWN):
                weight_rest(s_up + j)

        for n in range(S_DA, S_DA + 2):
            weight_rest(n)
        pool.wait_ge(S["x1_done"], KT)
        g.memset(qz, 0.0).then_inc(S["qz_zero"], 1)
        for n in range(S_DA + 2, S_DAO + 2):
            weight_rest(n)
        output_rests(0)
        for n in range(S_DAO + 2, S_UP0 + 2):
            weight_rest(n)
        ffn(0, S_UP0)
        for n in range(S_DSA, S_DSA + 7):
            weight_rest(n)
            if n in (S_DSA + 2, S_DSA + 3):
                half = 2 * (n - S_DSA - 2)
                for p in range(half, half + 2):
                    z = g.memset(qiz[:, p], 0.0)
                if half:
                    z.then_inc(S["qz_zero"], 1)
            elif n in (S_DSA + 4, S_DSA + 5):
                half = 4 * (n - S_DSA - 4)
                for p in range(half, half + 4):
                    z = g.memset(qz[:, p], 0.0)
                if half:
                    z.then_inc(S["qz_zero"], 1)
        for n in range(S_DSA + 7, S_DSAO + 2):
            weight_rest(n)
        output_rests(8)
        for n in range(S_DSAO + 2, S_UP1 + 2):
            weight_rest(n)
        ffn(1, S_UP1)

    def act_block2(act):
        A = nc.scalar.activation
        st = Steps(act, S["act_step"])
        st.n = 1

        act.wait_ge(S["x1_done"], KT)
        act.dma_start(cosT, ins["cosT"]).then_inc(S["rope_in"], 16)
        act.dma_start(sinT, ins["sinT"]).then_inc(S["rope_in"], 16)

        def weight_high(n):
            if n >= N_SLOTS:
                return
            if n >= S_DA + SPLIT:
                act.wait_ge(S["slot_used"], n - SPLIT + 1)
            j = n - S_DA
            act.wait_ge(raw_loaded[j % RAW], 16 * (j // RAW + 1))
            A(w_hi[:, j % SPLIT, :], raw[:, j % RAW, :], ACT.Copy).then_inc(S["w_hi_done"], 1)

        def ahead(n):
            weight_high(n + SPLIT)

        def squares(v, ready):
            for k in range(KT):
                ready(k)
                if KT * (v - 2) + k >= 2:
                    act.wait_ge(S["sq_used"], KT * (v - 2) + k - 1)
                if k < 2 and v > 2:
                    act.wait_ge(S["hn_ready"], hn_base(v - 1) + KT)
                A(sq[:, k % 2, :], h[:, k, :], ACT.Square).then_inc(S["norm_sq"], 1)
            act.wait_ge(S["norm_var"], v + 1)
            A(rs[:, :], rs[:, :], ACT.Sqrt).then_inc(S["norm_std"], 1)

        def norm_highs(v):
            for k in range(KT):
                act.wait_ge(S["normed"], KT * (v - 2) + k + 1)
                A(hn_hi[:, k, :], sq[:, k % 2, :], ACT.Copy).then_inc(S["x_hi"], 1)

        def scatter(i, p, dst):
            act.wait_ge(S["rope_done"], i + 1)
            for r in range(4):
                m = 4 * p + r
                for half, src in enumerate((rope_t(i, 0), rope_t(i, 3))):
                    at = 64 * (m % 2) + 32 * half
                    act.dma_start(dst(m)[at:at + 32], src[32 * r:32 * r + 32, :]).then_inc(scattered[i % 2], 16)

        def values(s0, g0, base):
            for j in range(8):
                act.wait_ge(S["slot_used"], s0 + g0 + j + 1)
                if j >= 2:
                    act.wait_ge(S["v_tr"], base + j - 1)
                A(halves(vch[:, j % 2, :]), pair(g0 + j), ACT.Copy).then_inc(S["v_ch"], 1)
                ahead(s0 + g0 + j)

        def attention(maps, heads, base_u, base_sc):
            units = [(hd, n, w) for hd in range(heads) for n, w in TILES]

            def exps(u):
                hd, n, w = units[u]
                act.wait_ge(S["a_max"], base_u + u + 1)
                if u >= 4:
                    act.wait_ge(S["a_tr"], base_u + u - 3)
                s = stat[0:w, u % 4, :]
                for c in range(maps):
                    p = sc_sb(prob(u, c, maps), n)
                    A(p, sc_bank(maps, n, c) if maps == 2 else p, ACT.Exp, bias=s[:, 2 + c:3 + c], scale=0.125 if maps == 2 else 1.0,
                      accum_out=s[:, 4 + c:5 + c]).then_inc(S["a_exp"], 1)

            def copy_pt(u):
                hd, n, w = units[u]
                act.wait_ge(S["a_tr"], base_u + u + 1)
                if u >= 2:
                    act.wait_ge(S["a_pv"], base_u + u - 1)
                if n < 4:
                    A(pt[:, u % 2, 0:w * (n + 1)], psum[:, 6, 0:w * (n + 1)], ACT.Copy).then_inc(S["a_pt"], 1)
                else:
                    A(pt[:, u % 2, 0:64], psum[:, 6, 0:64], ACT.Copy)
                    A(pt[0:16, u % 2, 64:80], psum[0:16, 6, 64:80], ACT.Copy).then_inc(S["a_pt"], 1)

            def out(u):
                hd, n, w = units[u]
                act.wait_ge(S["a_pv"], base_u + u + 1)
                r = slice(0, P) if maps == 2 else slice(64 * (hd % 2), 64 * (hd % 2) + 64)
                A(oT[r, hd * maps // 2, n * P:n * P + w], psum[r, 7, 0:w], ACT.Copy).then_inc(S["a_o"], 1)
                if maps == 1 and u % 10 == 9:
                    act.wait_ge(S["a_o"], base_u + u + 1)
                    A(hn_hi[:, u // 10, :], oT[:, u // 10, :], ACT.Copy).then_inc(S["o_hi"], 1)

            for u in range(LA_ACT):
                exps(u)
            for u in range(len(units)):
                if u + LA_ACT < len(units):
                    exps(u + LA_ACT)
                copy_pt(u)
                if u:
                    out(u - 1)
            out(len(units) - 1)

        def ffn(i, s_up):
            def product_high(m):
                act.wait_ge(S["prod_done"], FT * i + m + 1)
                A(a_hi[:, m, :], u_c[:, (2 * m + 1) % 4, :], ACT.Copy).then_inc(S["a_hi_done"], 1)

            for g in range(N_UP):
                act.wait_ge(S["slot_used"], s_up + g + 1)
                if g == 0:
                    act.wait_ge(S["u_zero"], i + 1)
                if g >= 4:
                    act.wait_ge(S["conv_done"], N_UP * i + g - 3)
                A(halves(u_in[:, g % 4, 2:T2 + 2]), pair(g), ACT.Copy).then_inc(S["u_evac"], 1)
                ahead(s_up + g)
                if g % 2:
                    act.wait_ge(S["conv_done"], N_UP * i + g)
                    A(u_c[:, (g - 1) % 4, :], u_c[:, (g - 1) % 4, :], ACT.Silu).then_inc(S["silu_done"], 1)
                elif g:
                    product_high(g // 2 - 1)
            product_high(FT - 1)
            for j in range(N_DOWN):
                ahead(s_up + N_UP + j)

        def x1_ready(k):
            act.wait_ge(S["x1_done"], k + 1)
            act.wait_ge(S["meta_in"], 16)

        for n in range(S_DA, S_DA + SPLIT):
            act.wait_ge(S["slot_used"], S_DA)
            weight_high(n)
        squares(2, x1_ready)
        act.wait_ge(S["lam_sum"], 1)
        A(stat2[:, 2:4], psum[:, 0, 0:2], ACT.Exp).then_inc(S["lam_exp"], 1)
        norm_highs(2)

        def to_q(m):
            return qz[:, m // 2, m % 2, :]

        def to_k(m):
            return kz[:, m // 2, :]

        for i in range(8):
            ahead(S_DA + 2 * i)
            if i == 1:
                act.wait_ge(S["qz_zero"], 1)
            if i:
                scatter(i - 1, (i - 1) % 4, to_q if i <= 4 else to_k)
            ahead(S_DA + 2 * i + 1)
        scatter(7, 3, to_k)
        values(S_DA, 16, 0)
        attention(2, 8, 0, 0)
        act.wait_ge(S["a_prob"], 40)

        def head_high(hd):
            act.wait_ge(S["hd_done"], hd + 1)
            A(hn_hi[:, hd, :], oT[:, hd, :], ACT.Copy).then_inc(S["o_hi"], 1)

        for hd in range(8):
            if hd >= 2:
                act.wait_ge(S["hd_sum"], hd - 1)
            A(prob(hd, 1), oT[:, hd, :], ACT.Square).then_inc(S["hd_sq"], 1)
            if hd:
                act.wait_ge(S["hd_var"], hd)
                A(prob(hd - 1, 0), prob(hd - 1, 0), ACT.Sqrt).then_inc(S["hd_std"], 1)
            if hd >= 2:
                head_high(hd - 2)
        act.wait_ge(S["hd_var"], 8)
        A(prob(7, 0), prob(7, 0), ACT.Sqrt).then_inc(S["hd_std"], 1)
        head_high(6)
        head_high(7)
        for g in range(N_OUT):
            ahead(S_DAO + g)
        squares(3, lambda k: act.wait_ge(S["res_done"], k + 1))
        norm_highs(3)
        ffn(0, S_UP0)
        squares(4, lambda k: act.wait_ge(S["res_done"], 8 + k + 1))
        norm_highs(4)
        for i in range(8, 10):
            ahead(S_DSA + 2 * i - 16)
            ahead(S_DSA + 2 * i - 15)
            act.wait_ge(S["qz_zero"], 2)
            scatter(i, i - 8, lambda m: qiz[:, m // 2, m % 2, :])
        ahead(S_DSA + 4)
        ahead(S_DSA + 5)
        act.wait_ge(S["slot_used"], S_DSA + 6)
        A(halves(prob1(0)), pair(4), ACT.Square)
        A(halves(prob1(1)), pair(5), ACT.Square).then_inc(S["ki_sq"], 1)
        act.wait_ge(S["slot_used"], S_DSA + 7)
        A(halves(wch), pair(6), ACT.Copy).then_inc(S["wi_ch"], 1)
        ahead(S_DSA + 6)
        act.wait_ge(S["ki_var"], 1)
        A(rope_t(1, 0), rope_t(1, 0), ACT.Sqrt).then_inc(S["ki_std"], 1)
        for i, (n, hd) in enumerate([(n, hd) for n in range(1, 5) for hd in range(8)]):
            act.wait_ge(S["i_sc"], i + 1)
            if i >= 2:
                act.wait_ge(S["i_acc"], i - 1)
            A(sc_sb(prob1(i % 2), n), idx_bank(i, n), ACT.Relu, scale=0.125).then_inc(S["i_relu"], 1)
        act.wait_ge(S["qz_zero"], 3)
        for i in range(10, 18):
            ahead(S_DSA + 7 + 2 * (i - 10))
            if i > 10:
                scatter(i - 1, (i - 11) % 4, to_q if i <= 14 else to_k)
            ahead(S_DSA + 8 + 2 * (i - 10))
        scatter(17, 3, to_k)
        values(S_DSA, 23, 8)
        attention(1, 16, 40, 80)
        for g in range(N_OUT):
            ahead(S_DSAO + g)
        squares(5, lambda k: act.wait_ge(S["res_done"], 16 + k + 1))
        norm_highs(5)
        ffn(1, S_UP1)
        squares(6, lambda k: act.wait_ge(S["res_done"], 24 + k + 1))

    def vector_block2(ve, st):
        V = nc.vector

        def norm_scale(v):
            ve.wait_ge(S["sq_used"], KT * (v - 1))
            V.tensor_scalar(halves(rs[:, :]), psum[:, 6:8, 0:HALF], 1.0 / D, EPS, ALU.mult, ALU.add).then_inc(S["norm_var"], 1)
            ve.wait_ge(S["norm_std"], v + 1)
            st.link(V.reciprocal(rs[:, :], rs[:, :]))

        def norm(v, gain):
            norm_scale(v)
            for k in range(KT + 1):
                if k < KT:
                    if k >= 2:
                        ve.wait_ge(S["hn_ready"], hn_base(v) + k - 1)
                    V.scalar_tensor_tensor(out=sq[:, k % 2, :], in0=h[:, k, :], scalar=gain(k), in1=rs[:, :], op0=ALU.mult, op1=ALU.mult).then_inc(S["normed"], 1)
                if k:
                    ve.wait_ge(S["x_hi"], KT * (v - 2) + k)
                    V.tensor_tensor(hn_lo[:, k - 1, :], sq[:, (k - 1) % 2, :], hn_hi[:, k - 1, :].bitcast(F32), ALU.subtract).then_inc(S["hn_ready"], 1)

        cos2, sin2 = halves(cosT), halves(sinT)

        def rope(i, s0, g):
            ve.wait_ge(S["slot_used"], s0 + g + 2)
            if i >= 2:
                ve.wait_ge(scattered[i % 2], 128 * (i // 2))
            a, b = pair(g), pair(g + 1)
            V.tensor_tensor(halves(rope_t(i, 0)), a, cos2, ALU.mult)
            V.tensor_tensor(halves(rope_t(i, 1)), b, sin2, ALU.mult)
            V.tensor_tensor(halves(rope_t(i, 2)), a, sin2, ALU.mult)
            V.tensor_tensor(halves(rope_t(i, 3)), b, cos2, ALU.mult).then_inc(S["rope_read"], 1)
            ve.wait_ge(S["rope_read"], i + 1)
            V.tensor_tensor(rope_t(i, 0), rope_t(i, 0), rope_t(i, 1), ALU.subtract)
            V.tensor_tensor(rope_t(i, 3), rope_t(i, 3), rope_t(i, 2), ALU.add).then_inc(S["rope_done"], 1)

        def values(base):
            for j in range(8):
                ve.wait_ge(S["v_tr"], base + j + 1)
                V.tensor_copy(vtok[:, 0:4, j * P:(j + 1) * P], psum[:, 6, :].rearrange("p (n m) -> p n m", n=4))
                V.tensor_copy(vtok[0:16, 4, j * P:(j + 1) * P], psum[0:16, 7, 0:P]).then_inc(S["v_tok"], 1)

        def attention(maps, heads, base_u, base_sc):
            units = [(hd, n, w) for hd in range(heads) for n, w in TILES]

            def soft(u):
                hd, n, w = units[u]
                s = stat[0:w, u % 4, :]
                for c in range(maps):
                    ve.wait_ge(S["a_sc"], base_sc + u * maps + c + 1)
                    if maps == 2:
                        axis = AX.X if n < 4 else AX.XY
                        st.did(V.tensor_reduce(s[:, c:c + 1], sc_bank(2, n, c), axis, ALU.max))
                    else:
                        if u >= 4:
                            ve.wait_ge(S["a_tr"], base_u + u - 3)
                        bias = sc_sb(sel[:, n - 1, :], n) if n else causalf[:, :]
                        st.did(V.tensor_tensor_reduce(out=sc_sb(prob(u, 0, 1), n), in0=sc_bank(1, n, 0), in1=bias, scale=0.125, scalar=-BIG,
                                                      op0=ALU.add, op1=ALU.max, accum_out=s[:, c:c + 1]))
                st.settle()
                V.tensor_scalar(s[:, 2:2 + maps], s[:, 0:maps], -0.125 if maps == 2 else -1.0, None, ALU.mult).then_inc(S["a_max"], 1)

            def normalise(u):
                hd, n, w = units[u]
                s = stat[0:w, u % 4, :]
                ve.wait_ge(S["a_exp"], base_sc + (u + 1) * maps)
                st.link(V.reciprocal(s[:, 6:6 + maps], s[:, 4:4 + maps]))
                p0 = prob(u, 0, maps)[0:w, 0:keys(n)]
                if maps == 2:
                    st.did(V.tensor_scalar(s[:, 7:8], s[:, 7:8], nlam[0:w], None, ALU.mult))
                    st.link(V.tensor_scalar(p0, p0, s[:, 6:7], None, ALU.mult))
                    V.scalar_tensor_tensor(out=p0, in0=prob(u, 1)[0:w, 0:keys(n)], scalar=s[:, 7:8], in1=p0, op0=ALU.mult, op1=ALU.add).then_inc(S["a_prob"], 1)
                else:
                    V.tensor_scalar(p0, p0, s[:, 6:7], None, ALU.mult).then_inc(S["a_prob"], 1)

            for u in range(LA_DVE):
                soft(u)
            for u in range(len(units)):
                if u + LA_DVE < len(units):
                    soft(u + LA_DVE)
                normalise(u)

        def residual(ready, base):
            for g in range(KT):
                ve.wait_ge(S["slot_used"], ready(g))
                V.tensor_tensor(halves(h[:, g, :]), halves(h[:, g, :]), pair(g), ALU.add).then_inc(S["res_done"], 1)

        def ffn(i, s_up, s_down, base):
            V.memset(u_in[:, :, 0:2], 0.0).then_inc(S["u_zero"], 1)
            for g in range(N_UP):
                n = N_UP * i + g
                ve.wait_ge(S["u_evac"], n + 1)
                if g >= 5 and g % 2:
                    ve.wait_ge(S["a_ready"], FT * i + (g - 3) // 2)
                w = [col("conv_w", 3 * N_UP * i + N_UP * j + g) for j in range(3)]
                c = u_c[:, g % 4, :]
                u = u_in[:, g % 4, :]
                st.link(V.tensor_scalar(c, u[:, 2:T2 + 2], w[2], col("conv_b", n), ALU.mult, ALU.add))
                st.link(V.scalar_tensor_tensor(out=c, in0=u[:, 1:T2 + 1], scalar=w[1], in1=c, op0=ALU.mult, op1=ALU.add))
                V.scalar_tensor_tensor(out=c, in0=u[:, 0:T2], scalar=w[0], in1=c, op0=ALU.mult, op1=ALU.add).then_inc(S["conv_done"], 1)
                if g % 2:
                    ve.wait_ge(S["silu_done"], (n + 1) // 2)
                    ve.wait_ge(S["conv_done"], n + 1)
                    V.tensor_tensor(c, u_c[:, (g - 1) % 4, :], c, ALU.mult).then_inc(S["prod_done"], 1)
                    ve.wait_ge(S["prod_done"], (n + 1) // 2)
            residual(lambda g: s_down + 3 * (g + 1), base)

        V.tensor_tensor(stat2[:, 0:2], col("lam_q", 0, 2), col("lam_k", 0, 2), ALU.mult).then_inc(S["lam_prod"], 1)
        norm(2, lambda k: col("da_norm", k))
        ve.wait_ge(S["lam_exp"], 1)
        st.link(V.tensor_tensor(stat2[:, 4:5], stat2[:, 3:4], stat2[:, 2:3], ALU.subtract))
        st.did(V.tensor_scalar(stat2[:, 4:5], stat2[:, 4:5], -LAMBDA_INIT, None, ALU.add))
        st.link(V.tensor_scalar(stat2[:, 5:6], col("subln"), 1.0 - LAMBDA_INIT, None, ALU.mult))
        ve.wait_ge(S["rope_in"], 32)
        for i in range(8):
            rope(i, S_DA, 2 * i)
        values(0)
        attention(2, 8, 0, 0)
        for hd in range(8):
            ve.wait_ge(S["hd_sum"], hd + 1)
            V.tensor_scalar(halves(prob(hd, 0)), pair(hd), 1.0 / P, EPS, ALU.mult, ALU.add).then_inc(S["hd_var"], 1)
            ve.wait_ge(S["hd_std"], hd + 1)
            st.link(V.reciprocal(prob(hd, 0), prob(hd, 0)))
            V.scalar_tensor_tensor(out=oT[:, hd, :], in0=oT[:, hd, :], scalar=stat2[:, 5:6], in1=prob(hd, 0), op0=ALU.mult, op1=ALU.mult).then_inc(S["hd_done"], 1)
            ve.wait_ge(S["hd_done"], hd + 1)
        residual(lambda g: S_DAO + g + 1, 0)
        norm(3, lambda k: col("ffn_norm", k))
        ffn(0, S_UP0, S_DOWN0, 8)

        norm(4, lambda k: col("dsa_norm", k))
        for i in range(2):
            rope(8 + i, S_DSA, 2 * i)
        ve.wait_ge(S["ki_sum"], 1)
        ve.wait_ge(scattered[1], 128 * 5)
        V.tensor_scalar(halves(rope_t(1, 0)), psum[:, 6:8, 0:HALF], 1.0 / 256, EPS, ALU.mult, ALU.add).then_inc(S["ki_var"], 1)
        ve.wait_ge(S["ki_std"], 1)
        st.link(V.reciprocal(rope_t(1, 0), rope_t(1, 0)))
        ve.wait_ge(S["wi_ch"], 1)
        ve.wait_ge(scattered[0], 128 * 5)
        for j in range(2):
            V.scalar_tensor_tensor(out=halves(rope_t(1, 2 + j)), in0=pair(4 + j), scalar=col("idx_norm", j), in1=halves(rope_t(1, 0)),
                                   op0=ALU.mult, op1=ALU.mult).then_inc(S["ki_normed"], 1)
        ve.wait_ge(S["ki_normed"], 2)
        ka, kb = rope_t(1, 2), rope_t(1, 3)
        for q in range(4):
            r = slice(32 * q, 32 * q + 32)
            own, other = (ka, kb) if q % 2 == 0 else (kb, ka)
            st.did(V.tensor_tensor(rope_t(0, 0)[r], own[r], cosT[r], ALU.mult))
            st.did(V.tensor_tensor(rope_t(0, 1)[r], other[r], sinT[r], ALU.mult))
        st.settle()
        for q in range(4):
            r = slice(32 * q, 32 * q + 32)
            last = V.tensor_tensor(ki2[r], rope_t(0, 0)[r], rope_t(0, 1)[r], ALU.subtract if q % 2 == 0 else ALU.add)
        last.then_inc(S["ki_done"], 1)
        ve.wait_ge(S["wi_tr"], 1)
        for n, w in TILES[1:]:
            st.did(V.tensor_scalar(wtok[0:w, n - 1, :], psum[0:w, 6, (n - 1) * P:(n - 1) * P + 8], 8.0 ** -0.5, None, ALU.mult))
        st.settle()
        for i, (n, hd) in enumerate([(n, hd) for n in range(1, 5) for hd in range(8)]):
            w = TILES[n][1]
            ve.wait_ge(S["i_relu"], i + 1)
            s = sel[0:w, n - 1, 0:keys(n)]
            r = prob1(i % 2)[0:w, 0:keys(n)]
            if hd == 0:
                V.tensor_scalar(s, r, wtok[0:w, n - 1, 0:1], None, ALU.mult).then_inc(S["i_acc"], 1)
            else:
                V.scalar_tensor_tensor(out=s, in0=r, scalar=wtok[0:w, n - 1, hd:hd + 1], in1=s, op0=ALU.mult, op1=ALU.add).then_inc(S["i_acc"], 1)
            ve.wait_ge(S["i_acc"], i + 1)
            if hd == 7:
                d = sel[0:w, n - 1, n * P:n * P + w]
                st.did(V.tensor_tensor(d, d, causalf[0:w, 0:w], ALU.add))
                st.link(V.memset(sel[0:w, n - 1, 0:META], BIG))

        def take_eight(r):
            n, w = TILES[1 + r // 16]
            s = sel[0:w, n - 1, 0:keys(n)]
            st.link(V.max(top8[0:w, :], s))
            st.link(V.match_replace(out=s, in_to_replace=top8[0:w, :], in_values=s, imm_value=SELECTED))
            if r % 16 == 15:
                st.link(V.tensor_scalar(s, s, SELECTED, -BIG, ALU.not_equal, ALU.mult))

        for i in range(8):
            rope(10 + i, S_DSA, 7 + 2 * i)
            for r in range(8):
                take_eight(8 * i + r)
        values(8)
        attention(1, 16, 40, 80)
        residual(lambda g: S_DSAO + g + 1, 16)
        norm(5, lambda k: col("ffn_norm", 8 + k))
        ffn(1, S_UP1, S_DOWN1, 24)
        norm_scale(6)
        for k in range(KT):
            V.scalar_tensor_tensor(out=h[:, k, :], in0=h[:, k, :], scalar=col("final_norm", k), in1=rs[:, :], op0=ALU.mult, op1=ALU.mult).then_inc(S["final_done"], 1)

    @block.sync
    def _(sp):
        sp.dma_start(cond, ins["cond"]).then_inc(S["c_in"], 16)
        sp.dma_start(cols[:, :], ins["columns"]).then_inc(S["params_in"], 16)
        for r in range(RING):
            sp.dma_start(ring[:, r, :], ins["weights"][r]).then_inc(w_loaded[r], 16)
            if r in (1, 3):
                k = 2 * (r - 1)
                sp.dma_start(h[:, k:k + 4, META:T2], ins["xT"][:, k:k + 4, :]).then_inc(S["x_in"], 16)
        sp.dma_start(h[:, :, 0:META], ins["metaT"]).then_inc(S["meta_in"], 16)
        for dst, name in ((loraW, "lora1"), (lora2, "lora2"), (ident[:, :], "ident"), (bones, "bones"),
                          (causalf[:, :], "causalf"), (alibi, "alibi"), (rmask[:, :], "rmask"),
                          (lvlmask[:, :, :], "lvlmask"), (mask_in, "glamask"), (gblock[:, :], "gblock"),
                          (reset64[:, :], "reset64"), (reset128[:, :], "reset128")):
            sp.dma_start(dst, ins[name]).then_inc(S["consts_in"], 16)
        with sp.Fori(1, S_DA // RING) as turn:
            for r in range(RING):
                sp.wait_ge(S["slot_used"], turn * RING + (r - RING + 1))
                sp.dma_start(ring[:, r, :], ins["weights"][turn * RING + r]).then_inc(w_loaded[r], 16)
        for n in range(S_DA // RING * RING, S_DA):
            sp.wait_ge(S["slot_used"], n - RING + 1)
            sp.dma_start(ring[:, n % RING, :], ins["weights"][n]).then_inc(w_loaded[n % RING], 16)
        sp.wait_ge(S["slot_used"], S_OUT1 + 1)
        for r in range(RAW):
            sp.dma_start(raw[:, r, :], ins["weights"][S_DA + r]).then_inc(raw_loaded[r], 16)
        turns = (N_SLOTS - S_DA) // RAW
        with sp.Fori(1, turns) as turn:
            for r in range(RAW):
                sp.wait_ge(S["w_split"], turn * RAW + (r - RAW + 1))
                sp.dma_start(raw[:, r, :], ins["weights"][turn * RAW + (S_DA + r)]).then_inc(raw_loaded[r], 16)
        for j in range(turns * RAW, N_SLOTS - S_DA):
            sp.wait_ge(S["w_split"], j - RAW + 1)
            sp.dma_start(raw[:, j % RAW, :], ins["weights"][S_DA + j]).then_inc(raw_loaded[j % RAW], 16)
        for k in range(0, KT, 2):
            sp.wait_ge(S["final_done"], k + 2)
            sp.dma_start(out_t[:, k:k + 2, :], h[:, k:k + 2, META:T2]).then_inc(S["out_stored"], 16)
        sp.wait_ge(S["out_stored"], 16 * (KT // 2))

    @block.tensor
    def _(pe):
        mm = nc.tensor.matmul

        def slot(n):
            pe.wait_ge(w_loaded[n % RING], 16 * (n // RING + 1))
            return ring[:, n % RING, :].rearrange("p (k m) -> p k m", k=KT)

        def norm_sums1(v):
            for k in range(KT):
                pe.wait_ge(S["norm_sq"], KT * v + k + 1)
                last = mm(bank(1), ones[:, :], hn1[:, k, 0:T1], start=k == 0, stop=k == KT - 1)
            last.then_inc(S["norm_sum"], 1)

        pe.wait_ge(S["zero_cols"], 1)
        norm_sums1(0)

        def free_bank(n):
            if n >= 8:
                pe.wait_ge(S["in1_evac"], n - 7)

        def in1(item, g, rhs=lambda k: h1[:, k, 1:T1 + 1]):
            w = slot(S_IN1 + g)
            free_bank(item)
            for k in range(KT):
                if g == 0:
                    pe.wait_ge(S["hn_ready"], k + 1)
                last = mm(bank(item % 8), w[:, k, :], rhs(k), start=k == 0, stop=k == KT - 1 and g > 0)
            last.then_inc(S["slot_used"], 1)

        in1(0, 0)
        pe.wait_ge(S["shift_diff"], KT)
        pe.wait_ge(S["lora_scaled"], KT)
        for k in range(KT):
            last = mm(bank(0), loraW[:, k, :], zb_d(k), start=False, stop=k == KT - 1)
        last.then_inc(S["lora_done"], 1)
        for g in range(1, 8):
            in1(g, g)
        pe.wait_ge(S["in1_evac"], 2)
        for j in range(5):
            free_bank(8 + j)
            mm(bank((8 + j) % 8), lora2[:, j, :], (low if j < 4 else glow), start=True, stop=True).then_inc(S["lora_done"], 1)
        for g in range(8, N_IN1):
            in1(g + 5, g)

        def v1_transposes():
            pe.wait_ge(S["in1_evac"], ITEMS)
            for t in range(4):
                last = nc.tensor.transpose(psum[:, 7, t * P:(t + 1) * P], v1[:, t * P:(t + 1) * P], ident[:, :])
            last.then_inc(S["v1_trans"], 1)

        v1_transposes()
        units = [(n, g) for n in range(4) for g in range(4)]

        def s1_scores(u):
            n, g = units[u]
            lo = max(0, n - 1) * P
            w = (n + 1) * P - lo
            if u >= 3:
                pe.wait_ge(S["s1_soft"], u - 2)
            for s in range(2):
                last = mm(psum[:, u % 3, s * w:(s + 1) * w], qz1[:, g, s, n * P:(n + 1) * P], k1[:, lo:lo + w], start=True, stop=True)
            last.then_inc(S["s1_scores"], 1)

        def s1_transposes(u):
            n, g = units[u]
            blocks = 2 if n else 1
            pe.wait_ge(S["s1_prob"], u + 1)
            if u >= 1:
                pe.wait_ge(S["s1_pt"], u)
            for s in range(2):
                for b in range(blocks):
                    j = s * blocks + b
                    last = nc.tensor.transpose(psum[:, 6, j * P:(j + 1) * P], p1[:, u % 2, s, b * P:(b + 1) * P], ident[:, :])
            last.then_inc(S["s1_trans"], 1)

        def s1_values(u):
            n, g = units[u]
            blocks = 2 if n else 1
            pe.wait_ge(S["s1_pt"], u + 1)
            if u == 0:
                pe.wait_ge(S["v1_tok"], 1)
            if u >= 1:
                pe.wait_ge(S["s1_out"], u)
            for s in range(2):
                for b in range(blocks):
                    last = mm(psum[:, 7, s * P:(s + 1) * P], v1tok[:, max(0, n - 1) + b, :],
                              pt1[:, u % 2, (s * blocks + b) * P:(s * blocks + b + 1) * P], start=b == 0, stop=b == blocks - 1)
            last.then_inc(S["s1_pv"], 1)

        s1_scores(0)
        for u in range(16):
            if u + 1 < 16:
                s1_scores(u + 1)
            s1_transposes(u)
            if u >= 1:
                s1_values(u - 1)
        s1_values(15)

        for lv in range(8):
            if lv < 7:
                pe.wait_ge(S["g_lvl"], lv + 1)
            if lv == 0:
                pe.wait_ge(S["s1_out"], 16)
            else:
                pe.wait_ge(S["g_taken"], 4 * lv)
            for hd in range(4):
                r = slice(32 * hd, 32 * hd + 32)
                for c in range(4):
                    t = slice(c * P, (c + 1) * P)
                    kl, ql = (g_kl[r, lv % 2, t], g_ql[r, lv % 2, t]) if lv < 7 else (gk[r, t], gq[r, t])
                    last = mm(psum[:, hd, c * P:(c + 1) * P], kl, ql, start=True, stop=True)
                last.then_inc(S["g_score"], 1)
        for j in range(2):
            for c in range(4):
                last = nc.tensor.transpose(psum[:, 4 + j, c * P:(c + 1) * P], gv[:, j, c * P:(c + 1) * P], ident[:, :])
            last.then_inc(S["g_tr"], 1)
        pe.wait_ge(S["g_qk"], 1)
        for c in range(4):
            last = nc.tensor.transpose(psum[:, 6, c * P:(c + 1) * P], g_kd[:, c * P:(c + 1) * P], ident[:, :])
        last.then_inc(S["g_tr"], 1)
        pe.wait_ge(S["g_trc"], 7)
        pe.wait_ge(S["g_taken"], 32)
        for c in range(4):
            t = slice(c * P, (c + 1) * P)
            if c >= 1:
                pe.wait_ge(S["g_sc"], c)
            for j in range(2):
                o = psum[:, j, t]
                if c >= 1:
                    mm(o, g_s[:, c % 2, j * P:(j + 1) * P], g_qe[:, t], start=True, stop=False)
                for s in range(2):
                    last = mm(o, g_vz[:, c, 2 * j + s, :], g_at[:, 2 * j + s, t], start=c == 0 and s == 0, stop=s == 1)
            last.then_inc(S["g_ops"], 1)
            if c < 3:
                mm(psum[:, 7, 0:256], g_kt[:, c, :], g_vt[:, c, :], start=True, stop=True).then_inc(S["g_sd"], 1)
        for j in range(2):
            pe.wait_ge(S["g_osq"], j + 1)
            mm(bank(2 + j), bones, g_o_sq(j), start=True, stop=True).then_inc(S["g_osum"], 1)

        for i in range(2):
            pe.wait_ge(S["r_kksq"], i + 1)
            mm(bank(0), bones, r_e[:, 0, :], start=True, stop=True).then_inc(S["r_kksum"], 1)
            pe.wait_ge(S["r_bon"], i + 1)
            mm(bank(1), bones, r_rho, start=True, stop=True).then_inc(S["r_bonsum"], 1)
            pe.wait_ge(S["r_ready"], i + 1)
            for u in range(8):
                if u >= 4:
                    pe.wait_ge(S["r_masked"], 8 * i + u - 3)
                t = slice(u * 64, (u + 1) * 64)
                b = u % 4
                mm(psum[:, b, 0:P], rz(1, u), rz(0, u), start=True, stop=True)
                mm(psum[:, b, P:2 * P], rz(2, u), rz(0, u), start=True, stop=True)
                mm(psum[:, b, 2 * P:2 * P + 64], rz(1, u), r_rho[:, t], start=True, stop=True)
                mm(psum[:, b, 2 * P + 64:3 * P], rz(2, u), r_rho[:, t], start=True, stop=True).then_inc(S["r_prod"], 1)
                if u >= 2:
                    pe.wait_ge(S["r_toksb"], 8 * i + u - 1)
                for q in range(4):
                    last = nc.tensor.transpose(psum[:, 6 + u % 2, q * P:(q + 1) * P], rz(q, u), ident[:, :])
                last.then_inc(S["r_tokps"], 1)
            for lv in range(6):
                for u in range(8):
                    if u % 2 == 0:
                        pe.wait_ge(S["r_nready"], 24 * i + 4 * lv + u // 2 + 1)
                    last = mm(psum[:, 4 + u // 4, (u % 4) * P:(u % 4 + 1) * P], r_n[:, u, :], r_x[:, u, 0, :], start=True, stop=True)
                    if u % 4 == 3:
                        last.then_inc(S["r_tps"], 1)
                for u in range(8):
                    if u % 4 == 0:
                        pe.wait_ge(S["r_tsb"], 12 * i + 2 * lv + u // 4 + 1)
                    o = (u % 2) * 256
                    mm(psum[:, u // 2, o:o + P], r_x[:, u, 1, :], r_t[:, u, :], start=True, stop=True)
                    last = mm(psum[:, u // 2, o + P:o + 2 * P], r_t[:, u, :], r_x[:, u, 1, :], start=True, stop=True)
                    if u % 2:
                        last.then_inc(S["r_xps"], 1)
            pe.wait_ge(S["r_toksb"], 8 * (i + 1))
            pe.wait_ge(S["x_upd"], 4 * (i + 1))
            for u in range(8):
                o = (u % 4) * P
                mm(psum[:, 4 + u // 4, o:o + P], r_akt[:, u, :], r_tok[:, u, 3, :], start=True, stop=True)
                mm(psum[:, u // 4, o:o + P], r_tok[:, u, 0, :], r_x[:, u, 1, :], start=True, stop=True).then_inc(S["r_wps"], 1)
            pe.wait_ge(S["r_t1sb"], i + 1)
            pe.wait_ge(S["r_wsb"], i + 1)
            for c in range(8):
                n = 8 * i + c
                if c >= 1:
                    pe.wait_ge(S["r_ssb"], 7 * i + c)
                last = mm(psum[:, 6 + c % 2, 0:P], r_x[:, c, 1, :], r_t1[:, c, :], start=True, stop=c == 0)
                if c:
                    last = mm(psum[:, 6 + c % 2, 0:P], r_wt[:, c, :], r_s[:, c % 2, :], start=False, stop=True)
                last.then_inc(S["r_ups"], 1)
                pe.wait_ge(S["r_usb"], n + 1)
                if c < 7:
                    mm(psum[:, 2 + c % 2, 0:P], r_tok[:, c, 1, :], r_u[:, c % 2, :], start=True, stop=False)
                    mm(psum[:, 2 + c % 2, 0:P], r_tok[:, c, 2, :], r_tok[:, c, 3, :], start=False, stop=True).then_inc(S["r_sps"], 1)
                t = slice(c * 64, (c + 1) * 64)
                if c >= 2:
                    pe.wait_ge(S["r_ysb"], n - 1)
                y = psum[:, 4 + c % 2, 0:64]
                if c:
                    mm(y, r_s[:, c % 2, :], r_rho[:, t], start=True, stop=False)
                mm(y, r_u[:, c % 2, :], r_rbt[:, c, :], start=c == 0, stop=False)
                mm(y, r_tok[:, c, 3, :], r_rkt[:, c, :], start=False, stop=True).then_inc(S["r_yps"], 1)
            pe.wait_ge(S["r_ysb"], 8 * (i + 1))
            mm(bank(0), bones, sg[:, i, :], start=True, stop=True).then_inc(S["r_mean"], 1)
            pe.wait_ge(S["r_ysq"], i + 1)
            mm(bank(1), bones, r_e[:, 0, :], start=True, stop=True).then_inc(S["r_ysum"], 1)

        pe.wait_ge(S["r_done"], 2)
        pe.wait_ge(S["g_done"], 2)
        pe.wait_ge(S["s1_out"], 16)
        for g in range(N_OUT):
            w = slot(S_OUT1 + g)
            for k in range(KT):
                last = mm(bank(g), w[:, k, :], mix[:, k, :], start=k == 0, stop=k == KT - 1)
            last.then_inc(S["slot_used"], 1)
        pe.wait_ge(S["norm_sq"], KT + 2)
        norm_sums1(1)
        tensor_block2(pe)

    @block.gpsimd
    def _(pool):
        g = nc.gpsimd
        st = Steps(pool, S["pool_step"])
        g.memset(zb[:, :, 0:1], 0.0).then_inc(S["qz1_zeroed"], 1)
        g.memset(qz1, 0.0).then_inc(S["qz1_zeroed"], 1)
        pool.wait_ge(S["s1_out"], 16)
        pool.wait_ge(S["s1_pv"], 16)
        g.memset(g_at, 0.0).then_inc(S["g_zero"], 1)
        g.memset(g_vz, 0.0).then_inc(S["g_zero"], 1)
        pool.wait_ge(S["g_done"], 2)
        g.memset(r_z, 0.0).then_inc(S["r_zero"], 1)
        pool_block2(pool)

    @block.scalar
    def _(act):
        A = nc.scalar.activation
        st = Steps(act, S["act_step"])
        act.wait_ge(S["c_in"], 16)
        A(cond, cond, ACT.Silu).then_inc(S["c_silu"], 1)
        act.wait_ge(S["x_in"], 32)
        for k in range(KT):
            A(hn1[:, k, 0:T1], h[:, k, META:T2], ACT.Square).then_inc(S["norm_sq"], 1)
        act.wait_ge(S["norm_var"], 1)
        A(rs[:, 0:T1], rs[:, 0:T1], ACT.Sqrt).then_inc(S["norm_std"], 1)

        def take(item):
            if item < 8 and item != 0:
                act.wait_ge(S["slot_used"], S_IN1 + item + 1)
            elif item == 0:
                act.wait_ge(S["lora_done"], 1)
            elif item < 13:
                act.wait_ge(S["lora_done"], 2 + item - 8)
            else:
                act.wait_ge(S["slot_used"], S_IN1 + item - 5 + 1)
            return bank(item % 8)

        def evac(dst, item, func=ACT.Copy, part=slice(0, P), **kw):
            return A(dst, psum[part, item % 8, 0:T1], func, **kw)

        done = S["in1_evac"]
        take(0)
        evac(low[0:64, :], 0, ACT.Tanh, slice(0, 64))
        evac(low[64:P, :], 0, part=slice(64, P)).then_inc(done, 1)
        take(1)
        evac(glow, 1).then_inc(done, 1)
        for j in range(6):
            take(2 + j)
            evac(zb[:, j, 1:T1 + 1], 2 + j).then_inc(done, 1)
        for j in range(2):
            take(8 + j)
            evac(sg[:, j, :], 8 + j, ACT.Sigmoid, bias=col("w0", j)).then_inc(done, 1)
        for j in range(2):
            take(10 + j)
            evac(asig[:, j, :], 10 + j, ACT.Sigmoid, bias=col("a0", j)).then_inc(done, 1)
        take(12)
        evac(gz, 12, ACT.Identity, bias=col("gk_b")).then_inc(done, 1)
        take(13)
        evac(gq, 13, scale=32.0 ** -0.5).then_inc(done, 1)
        take(14)
        evac(gk, 14).then_inc(done, 1)
        for j in range(2):
            take(15 + j)
            evac(gv[:, j, :], 15 + j).then_inc(done, 1)
        act.wait_ge(S["qz1_zeroed"], 2)
        for j in range(4):
            take(17 + j)
            evac(qz1[0:64, j, 0, :], 17 + j, part=slice(0, 64))
            evac(qz1[64:P, j, 1, :], 17 + j, part=slice(64, P)).then_inc(done, 1)
        take(21)
        evac(k1, 21).then_inc(done, 1)
        take(22)
        evac(v1, 22).then_inc(done, 1)
        for j in range(4):
            take(23 + j)
            evac(agate[:, j, :], 23 + j, ACT.Silu).then_inc(done, 1)
        for j in range(2):
            take(27 + j)
            evac(rgate[:, j, :], 27 + j, ACT.Silu).then_inc(done, 1)
        for j in range(2):
            take(29 + j)
            evac(ggate[:, j, :], 29 + j, ACT.Silu).then_inc(done, 1)

        act.wait_ge(S["g_absz"], 1)
        st.link(A(norm_tmp[:, 0:T1], norm_tmp[:, 0:T1], ACT.Exp))
        A(norm_tmp[:, 0:T1], norm_tmp[:, 0:T1], ACT.Ln, bias=1.0).then_inc(S["g_ln"], 1)

        act.wait_ge(S["v1_trans"], 1)
        A(v1tok, psum[:, 7, 0:512].rearrange("p (a b) -> p a b", a=4), ACT.Copy).then_inc(S["v1_tok"], 1)

        def s1_exp(u):
            n, g = divmod(u, 4)
            w = 256 if n else P
            act.wait_ge(S["s1_soft"], u + 1)
            o = 24 + 8 * (u % 2)
            for s in range(2):
                A(p1[:, u % 2, s, 0:w], p1[:, u % 2, s, 0:w], ACT.Exp, bias=small[:, o + 2 + s:o + 3 + s],
                  accum_out=small[:, o + 4 + s:o + 5 + s])
            A(small[:, o + 6:o + 8], small[:, o + 6:o + 8], ACT.Exp).then_inc(S["s1_exp"], 1)

        def s1_copy(u):
            n, g = divmod(u, 4)
            w = 4 * P if n else 2 * P
            act.wait_ge(S["s1_trans"], u + 1)
            if u >= 2:
                act.wait_ge(S["s1_pv"], u - 1)
            A(pt1[:, u % 2, 0:w], psum[:, 6, 0:w], ACT.Copy).then_inc(S["s1_pt"], 1)

        s1_exp(0)
        for u in range(16):
            if u + 1 < 16:
                s1_exp(u + 1)
            s1_copy(u)

        act.wait_ge(S["g_cum"], 1)
        A(g_d[:, 0, :], g_b, ACT.Exp, scale=1.0 / 16).then_inc(S["g_exp"], 1)
        A(g_d[:, 1, :], g_d[:, 1, :], ACT.Exp, scale=1.0 / 16).then_inc(S["g_exp"], 1)
        for lv in range(7):
            act.wait_ge(S["g_diff"], lv + 1)
            A(g_e(lv), g_e(lv), ACT.Exp, scale=1.0 / 16).then_inc(S["g_exp"], 1)
        act.wait_ge(S["g_zero"], 2)
        for j in range(2):
            act.wait_ge(S["g_tr"], j + 1)
            src = psum[:, 4 + j, 0:512].rearrange("p (c m) -> p c m", c=4)
            A(g_vt[:, :, j * P:(j + 1) * P], src, ACT.Copy).then_inc(S["g_trc"], 1)
            for s in range(2):
                A(g_vz[:, :, 2 * j + s, 64 * s:64 * s + 64], src[:, :, 64 * s:64 * s + 64], ACT.Copy).then_inc(S["g_trc"], 1)
        act.wait_ge(S["g_tr"], 3)
        A(g_kt, psum[:, 6, 0:512].rearrange("p (c m) -> p c m", c=4), ACT.Copy).then_inc(S["g_trc"], 1)
        act.wait_ge(S["g_ost"], 4)
        for j in range(2):
            A(g_o_sq(j), g_o[:, j, :], ACT.Square).then_inc(S["g_osq"], 1)
        for j in range(2):
            act.wait_ge(S["g_ovar"], j + 1)
            A(g_kl[:, j, :], g_kl[:, j, :], ACT.Sqrt).then_inc(S["g_ostd"], 1)

        for i in range(2):
            act.wait_ge(S["r_kkraw"], i + 1)
            A(r_e[:, 0, :], r_kk, ACT.Square).then_inc(S["r_kksq"], 1)
            act.wait_ge(S["r_kksum"], i + 1)
            A(norm_tmp[:, 0:T1], bank(0), ACT.Sqrt).then_inc(S["r_kkstd"], 1)
            act.wait_ge(S["r_decay"], i + 1)
            A(r_e[:, 0, :], r_e[:, 0, :], ACT.Exp)
            A(r_e[:, 1, :], r_b, ACT.Exp, scale=-1.0)
            A(r_e[:, 2, :], r_b, ACT.Exp).then_inc(S["r_exps"], 1)
            for u in range(8):
                act.wait_ge(S["r_tokps"], 8 * i + u + 1)
                A(r_tok[:, u, :, :], psum[:, 6 + u % 2, 0:512].rearrange("p (q m) -> p q m", q=4), ACT.Copy).then_inc(S["r_toksb"], 1)
            for lv in range(6):
                for q in range(2):
                    act.wait_ge(S["r_tps"], 12 * i + 2 * lv + q + 1)
                    A(r_t[:, 4 * q:4 * q + 4, :], psum[:, 4 + q, :].rearrange("p (u m) -> p u m", u=4), ACT.Copy).then_inc(S["r_tsb"], 1)
            act.wait_ge(S["r_wps"], 8 * (i + 1))
            A(r_t1[:, 0:4, :], psum[:, 4, :].rearrange("p (u m) -> p u m", u=4), ACT.Copy)
            A(r_t1[:, 4:8, :], psum[:, 5, :].rearrange("p (u m) -> p u m", u=4), ACT.Copy).then_inc(S["r_t1sb"], 1)
            for c in range(8):
                n = 8 * i + c
                act.wait_ge(S["r_ups"], n + 1)
                if c >= 2:
                    act.wait_ge(S["r_yps"], n - 1)
                A(r_u[:, c % 2, :], psum[:, 6 + c % 2, 0:P], ACT.Copy).then_inc(S["r_usb"], 1)
                act.wait_ge(S["r_yps"], n + 1)
                A(sg[:, i, c * 64:(c + 1) * 64], psum[:, 4 + c % 2, 0:64], ACT.Copy).then_inc(S["r_ysb"], 1)
            act.wait_ge(S["r_cent"], i + 1)
            A(r_e[:, 0, :], sg[:, i, :], ACT.Square).then_inc(S["r_ysq"], 1)
            act.wait_ge(S["r_yvar"], i + 1)
            A(r_e[:, 1, :], r_e[:, 1, :], ACT.Sqrt).then_inc(S["r_ystd"], 1)

        for g in range(N_OUT):
            act.wait_ge(S["slot_used"], S_OUT1 + g + 1)
            A(y1(g), bank(g), ACT.Copy)
            A(hn1[:, g, 0:T1], bank(g), ACT.Square).then_inc(S["norm_sq"], 1)
        act.wait_ge(S["norm_var"], 2)
        A(rs[:, 0:T1], rs[:, 0:T1], ACT.Sqrt).then_inc(S["norm_std"], 1)
        act_block2(act)

    @block.vector
    def _(ve):
        V = nc.vector
        st = Steps(ve, S["dve_step"])
        V.memset(ones[:, :], 1.0).then_inc(S["zero_cols"], 1)

        def modulation(m):
            ve.wait_ge(w_loaded[m % RING], 16 * (m // RING + 1))
            if m >= 2:
                ve.wait_ge(S["slot_used"], m - 1)
            V.tensor_tensor_reduce(out=ada_out[:, m % 2, :], in0=ring[:, m % RING, :], in1=cond, scale=1.0, scalar=0.0,
                                   op0=ALU.mult, op1=ALU.add, accum_out=ada[:, m:m + 1]).then_inc(S["slot_used"], 1)

        ve.wait_ge(S["c_silu"], 1)
        for m in range(RING):
            modulation(m)
        ve.wait_ge(S["norm_sum"], 1)
        V.tensor_scalar(rs[:, 0:T1], bank(1), 1.0 / D, 1e-6, ALU.mult, ALU.add).then_inc(S["norm_var"], 1)
        for m in range(RING, N_ADA):
            modulation(m)
        ve.wait_ge(S["consts_in"], 16 * 12)
        V.tensor_copy(identb[:, :], ident[:, :])
        V.tensor_copy(causalb[:, :], causalf[:, :])
        V.tensor_copy(glamask[:, :, :], mask_in)
        ve.wait_ge(S["norm_std"], 1)
        V.memset(h1[:, :, 0:1], 0.0)
        st.link(V.reciprocal(rs[:, 0:T1], rs[:, 0:T1]))
        ve.wait_ge(S["params_in"], 16)
        ve.wait_ge(S["slot_used"], N_ADA)
        st.link(V.tensor_tensor(ada[:, :], ada[:, :], col("ada_b", 0, 24), ALU.add))
        V.scalar_tensor_tensor(out=small[:, 8:16], in0=ada[:, 8:16], scalar=1.0, in1=col("norm_pre", 0, 8), op0=ALU.add, op1=ALU.mult)
        st.link(V.tensor_tensor(small[:, 16:24], ada[:, 16:24], col("norm_post", 0, 8), ALU.mult))
        for k in range(KT):
            st.did(V.scalar_tensor_tensor(out=h1[:, k, 1:T1 + 1], in0=h[:, k, META:T2], scalar=small[:, 8 + k:9 + k],
                                          in1=rs[:, 0:T1], op0=ALU.mult, op1=ALU.mult))
        st.settle()
        for k in range(KT):
            V.tensor_scalar(h1[:, k, 1:T1 + 1], h1[:, k, 1:T1 + 1], ada[:, k:k + 1], None, ALU.add).then_inc(S["hn_ready"], 1)
        for k in range(KT):
            ve.wait_ge(S["hn_ready"], k + 1)
            V.tensor_tensor(zb_d(k), h1[:, k, 0:T1], h1[:, k, 1:T1 + 1], ALU.subtract).then_inc(S["shift_diff"], 1)
            V.tensor_scalar(loraW[:, k, 0:64], loraW[:, k, 0:64], col("mu_w", k), None, ALU.mult)
            V.tensor_scalar(loraW[:, k, 64:P], loraW[:, k, 64:P], col("mu_a", k), None, ALU.mult).then_inc(S["lora_scaled"], 1)
        ve.wait_ge(S["qz1_zeroed"], 1)
        for j in range(6):
            ve.wait_ge(S["in1_evac"], 3 + j)
            st.link(V.tensor_tensor(dmix, zb[:, j, 0:T1], zb[:, j, 1:T1 + 1], ALU.subtract))
            st.link(V.scalar_tensor_tensor(out=zb[:, j, 1:T1 + 1], in0=dmix, scalar=col("mu_rkv", j), in1=zb[:, j, 1:T1 + 1],
                                           op0=ALU.mult, op1=ALU.add))
        ve.wait_ge(S["in1_evac"], 13)
        V.scalar_tensor_tensor(out=norm_tmp[:, 0:T1], in0=gz, scalar=-1.0, in1=gz, op0=ALU.mult, op1=ALU.min).then_inc(S["g_absz"], 1)
        ve.wait_ge(S["g_ln"], 1)
        st.link(V.scalar_tensor_tensor(out=gz, in0=gz, scalar=0.0, in1=norm_tmp[:, 0:T1], op0=ALU.min, op1=ALU.subtract))

        ve.wait_ge(S["in1_evac"], ITEMS)

        def s1_max(u):
            n, g = divmod(u, 4)
            w = 256 if n else P
            o = 24 + 8 * (u % 2)
            ve.wait_ge(S["s1_scores"], u + 1)
            if u >= 2:
                ve.wait_ge(S["s1_trans"], u - 1)
            for s in range(2):
                st.did(V.tensor_tensor_reduce(out=p1[:, u % 2, s, 0:w], in0=psum[:, u % 3, s * w:(s + 1) * w],
                                              in1=alibi[:, g + 4 * s, 256 - w:256], scale=0.125, scalar=-BIG, op0=ALU.add, op1=ALU.max,
                                              accum_out=small[:, o + s:o + s + 1]))
            st.settle()
            sinks = cols[:, COL["sinks"][0] + g:COL["sinks"][0] + g + 5:4]
            st.link(V.tensor_tensor(small[:, o:o + 2], small[:, o:o + 2], sinks, ALU.max))
            V.tensor_tensor(small[:, o + 6:o + 8], sinks, small[:, o:o + 2], ALU.subtract)
            V.tensor_scalar(small[:, o + 2:o + 4], small[:, o:o + 2], -1.0, None, ALU.mult).then_inc(S["s1_soft"], 1)

        def s1_normalise(u):
            n, g = divmod(u, 4)
            w = 256 if n else P
            o = 24 + 8 * (u % 2)
            ve.wait_ge(S["s1_exp"], u + 1)
            st.link(V.tensor_tensor(small[:, o + 4:o + 6], small[:, o + 4:o + 6], small[:, o + 6:o + 8], ALU.add))
            st.link(V.reciprocal(small[:, o + 4:o + 6], small[:, o + 4:o + 6]))
            V.tensor_scalar(p1[:, u % 2, 0, 0:w], p1[:, u % 2, 0, 0:w], small[:, o + 4:o + 5], None, ALU.mult)
            V.tensor_scalar(p1[:, u % 2, 1, 0:w], p1[:, u % 2, 1, 0:w], small[:, o + 5:o + 6], None, ALU.mult).then_inc(S["s1_prob"], 1)

        def s1_gate(u):
            n, g = divmod(u, 4)
            t = slice(n * P, (n + 1) * P)
            ve.wait_ge(S["s1_pv"], u + 1)
            V.tensor_tensor(mix[0:64, g, t], psum[0:64, 7, 0:P], agate[0:64, g, t], ALU.mult)
            V.tensor_tensor(mix[64:P, g, t], psum[64:P, 7, P:2 * P], agate[64:P, g, t], ALU.mult).then_inc(S["s1_out"], 1)

        s1_max(0)
        for u in range(16):
            if u + 1 < 16:
                s1_max(u + 1)
            s1_normalise(u)
            if u >= 1:
                s1_gate(u - 1)
        s1_gate(15)

        ve.wait_ge(S["s1_out"], 16)
        st.link(V.tensor_tensor_scan(g_b, reset128[:, :], gz, 0.0, ALU.mult, ALU.add))
        b128 = g_b.rearrange("p (n w) -> p n w", w=P)
        V.tensor_tensor(g_d[:, 1, :].rearrange("p (n w) -> p n w", w=P), b128[:, :, P - 1:P].to_broadcast([P, 4, P]), b128, ALU.subtract).then_inc(S["g_cum"], 1)
        ve.wait_ge(S["g_exp"], 2)
        V.tensor_tensor(g_qe, gq, g_d[:, 0, :], ALU.mult)
        V.tensor_tensor(g_kd, gk, g_d[:, 1, :], ALU.mult).then_inc(S["g_qk"], 1)

        def g_distance(lv):
            s = 1 << lv
            bb = g_b.rearrange("p (n w) -> p n w", w=2 * s)
            e = g_e(lv)
            st.link(V.tensor_tensor(e.rearrange("p (n w) -> p n w", w=2 * s), bb, bb[:, :, s - 1:s].to_broadcast([P, T1 // (2 * s), 2 * s]), ALU.subtract))
            V.scalar_tensor_tensor(out=e, in0=e, scalar=-1.0, in1=e, op0=ALU.mult, op1=ALU.min).then_inc(S["g_diff"], 1)

        def g_take(lv):
            if lv == 0:
                ve.wait_ge(S["g_zero"], 1)
            for hd in range(4):
                ve.wait_ge(S["g_score"], 4 * lv + hd + 1)
                V.copy_predicated(g_at[:, hd, :].rearrange("p (c m) -> p c m", c=4),
                                  glamask[:, lv:lv + 1, :].to_broadcast([P, 4, P]),
                                  psum[:, hd, :].rearrange("p (c m) -> p c m", c=4)).then_inc(S["g_taken"], 1)

        for lv in range(7):
            g_distance(lv)
            if lv >= 1:
                g_take(lv - 1)
            ve.wait_ge(S["g_exp"], 2 + lv + 1)
            V.tensor_tensor(g_ql[:, lv % 2, :], gq, g_e(lv), ALU.mult)
            V.tensor_tensor(g_kl[:, lv % 2, :], gk, g_e(lv), ALU.mult).then_inc(S["g_lvl"], 1)
        g_take(6)
        g_take(7)
        for c in range(4):
            t = slice(c * P, (c + 1) * P)
            ve.wait_ge(S["g_ops"], c + 1)
            V.tensor_copy(g_o[:, 0:2, t], psum[:, 0:2, t]).then_inc(S["g_ost"], 1)
            if c < 3:
                ve.wait_ge(S["g_sd"], c + 1)
                nxt = g_s[:, (c + 1) % 2, :]
                if c == 0:
                    V.tensor_tensor(nxt, psum[:, 7, 0:256], gblock[:, :], ALU.mult).then_inc(S["g_sc"], 1)
                else:
                    st.link(V.tensor_tensor(nxt, psum[:, 7, 0:256], gblock[:, :], ALU.mult))
                    V.scalar_tensor_tensor(out=nxt, in0=g_s[:, c % 2, :], scalar=g_d[:, 0, (c + 1) * P - 1:(c + 1) * P], in1=nxt,
                                           op0=ALU.mult, op1=ALU.add).then_inc(S["g_sc"], 1)
        for j in range(2):
            ve.wait_ge(S["g_osum"], j + 1)
            V.tensor_scalar(g_kl[:, j, :], bank(2 + j), 1.0 / 64, 1e-5, ALU.mult, ALU.add).then_inc(S["g_ovar"], 1)
        for j in range(2):
            ve.wait_ge(S["g_ostd"], j + 1)
            st.link(V.reciprocal(g_kl[:, j, :], g_kl[:, j, :]))
            st.link(V.scalar_tensor_tensor(out=g_kl[:, j, :], in0=g_kl[:, j, :], scalar=col("gla_norm"), in1=g_o[:, j, :], op0=ALU.mult, op1=ALU.mult))
            V.tensor_tensor(mix[:, 6 + j, :], g_kl[:, j, :], ggate[:, j, :], ALU.mult).then_inc(S["g_done"], 1)

        ve.wait_ge(S["r_zero"], 1)
        for i in range(2):
            if i:
                ve.wait_ge(S["r_done"], i)
            zr, zk, zv = (zb[:, 2 * q + i, 1:T1 + 1] for q in range(3))
            V.tensor_scalar(r_kk, zk, col("k_k", i), None, ALU.mult).then_inc(S["r_kkraw"], 1)
            st.link(V.tensor_scalar(r_e[:, 1, :], sg[:, i, :], -math.exp(-0.5), None, ALU.mult))
            st.link(V.tensor_tensor_scan(r_b, reset64[:, :], r_e[:, 1, :], 0.0, ALU.mult, ALU.add))
            st.link(V.tensor_scalar(small[:, 40:41], col("k_a", i), -1.0, 1.0, ALU.mult, ALU.add))
            st.link(V.tensor_scalar(r_rho, asig[:, i, :], col("k_a", i), small[:, 40:41], ALU.mult, ALU.add))
            st.link(V.tensor_tensor(zk, zk, r_rho, ALU.mult))
            V.scalar_tensor_tensor(out=r_rho, in0=zr, scalar=col("r_k", i), in1=zk, op0=ALU.mult, op1=ALU.mult).then_inc(S["r_bon"], 1)
            ve.wait_ge(S["r_kkstd"], i + 1)
            V.tensor_tensor(r_e[:, 0, :], r_b, r_e[:, 1, :], ALU.subtract).then_inc(S["r_decay"], 1)
            st.link(V.tensor_scalar(norm_tmp[:, 0:T1], norm_tmp[:, 0:T1], 1e-12, None, ALU.max))
            st.link(V.reciprocal(norm_tmp[:, 0:T1], norm_tmp[:, 0:T1]))
            st.link(V.tensor_tensor(r_kk, r_kk, norm_tmp[:, 0:T1], ALU.mult))
            ve.wait_ge(S["r_bonsum"], i + 1)
            V.tensor_tensor(mix[:, 4 + i, :], bank(1), zv, ALU.mult)
            ve.wait_ge(S["r_exps"], i + 1)

            def chunks(v, s):
                return v[64 * s:64 * s + 64].rearrange("p (c t) -> p c t", c=8)

            for s in range(2):
                st.did(V.tensor_tensor(rz_half(0, s), chunks(r_kk, s), chunks(r_e[:, 0, :], s), ALU.mult))
                st.did(V.tensor_tensor(rz_half(2, s), chunks(zk, s), chunks(r_e[:, 1, :], s), ALU.mult))
                st.did(V.tensor_copy(rz_half(3, s), chunks(zv, s)))
            st.did(V.tensor_tensor(r_rho, zr, r_e[:, 2, :], ALU.mult))
            st.settle()
            st.link(V.tensor_tensor(r_kk, r_kk, asig[:, i, :], ALU.mult))
            V.tensor_tensor(rz_half(1, 0), chunks(r_kk, 0), chunks(r_e[:, 1, :], 0), ALU.mult)
            V.tensor_tensor(rz_half(1, 1), chunks(r_kk, 1), chunks(r_e[:, 1, :], 1), ALU.mult).then_inc(S["r_ready"], 1)
            for u in range(8):
                ve.wait_ge(S["r_prod"], 8 * i + u + 1)
                b = u % 4
                V.tensor_tensor(r_lt[:, u, :], psum[:, b, 0:P], rmask[:, 0:P], ALU.mult)
                V.tensor_tensor(r_akt[:, u, :], psum[:, b, P:2 * P], rmask[:, P:2 * P], ALU.mult)
                V.tensor_tensor(r_rbt[:, u, :], psum[:, b, 2 * P:2 * P + 64], rmask[:, 2 * P:2 * P + 64], ALU.mult)
                V.tensor_tensor(r_rkt[:, u, :], psum[:, b, 2 * P + 64:3 * P], rmask[:, 2 * P + 64:3 * P], ALU.mult).then_inc(S["r_masked"], 1)
                st.did(V.tensor_copy(r_x[:, u, :, :], ident[:, :].rearrange("p (a m) -> p a m", a=1).to_broadcast([P, 2, P])))
            st.settle()
            ve.wait_ge(S["r_masked"], 8 * (i + 1))
            for q in range(4):
                two = slice(2 * q, 2 * q + 2)
                V.tensor_tensor(r_n[:, two, :], r_lt[:, two, :], lvlmask[:, 0:1, :].to_broadcast([P, 2, P]), ALU.mult).then_inc(S["r_nready"], 1)
            for lv in range(6):
                for q in range(4):
                    two = slice(2 * q, 2 * q + 2)
                    ve.wait_ge(S["r_xps"], 24 * i + 4 * lv + q + 1)
                    upd = V.tensor_tensor(r_x[:, two, :, :], r_x[:, two, :, :], psum[:, q, :].rearrange("p (u a m) -> p u a m", u=2, a=2), ALU.add)
                    if lv < 5:
                        V.tensor_tensor(r_n[:, two, :], r_lt[:, two, :], lvlmask[:, lv + 1:lv + 2, :].to_broadcast([P, 2, P]), ALU.mult).then_inc(S["r_nready"], 1)
                    else:
                        upd.then_inc(S["x_upd"], 1)
            ve.wait_ge(S["r_wps"], 8 * (i + 1))
            V.tensor_scalar(r_wt[:, 0:4, :], psum[:, 0, :].rearrange("p (u m) -> p u m", u=4), -1.0, None, ALU.mult)
            V.tensor_scalar(r_wt[:, 4:8, :], psum[:, 1, :].rearrange("p (u m) -> p u m", u=4), -1.0, None, ALU.mult).then_inc(S["r_wsb"], 1)
            for c in range(7):
                nxt = r_s[:, (c + 1) % 2, :]
                e = r_e[:, 2, 64 * c + 63:64 * c + 64]
                if c:
                    st.link(V.tensor_scalar(r_se, r_s[:, c % 2, :], e, None, ALU.mult))
                ve.wait_ge(S["r_sps"], 7 * i + c + 1)
                if c >= 1:
                    ve.wait_ge(S["r_yps"], 8 * i + c)
                if c:
                    V.scalar_tensor_tensor(out=nxt, in0=psum[:, 2 + c % 2, 0:P], scalar=e, in1=r_se, op0=ALU.mult, op1=ALU.add).then_inc(S["r_ssb"], 1)
                else:
                    V.tensor_scalar(nxt, psum[:, 2 + c % 2, 0:P], e, None, ALU.mult).then_inc(S["r_ssb"], 1)
                ve.wait_ge(S["r_ssb"], 7 * i + c + 1)
            ve.wait_ge(S["r_mean"], i + 1)
            V.scalar_tensor_tensor(out=sg[:, i, :], in0=bank(0), scalar=-1.0 / 64, in1=sg[:, i, :], op0=ALU.mult, op1=ALU.add).then_inc(S["r_cent"], 1)
            ve.wait_ge(S["r_ysum"], i + 1)
            V.tensor_scalar(r_e[:, 1, :], bank(1), 1.0 / 64, 64e-5, ALU.mult, ALU.add).then_inc(S["r_yvar"], 1)
            ve.wait_ge(S["r_ystd"], i + 1)
            st.link(V.reciprocal(r_e[:, 1, :], r_e[:, 1, :]))
            st.link(V.scalar_tensor_tensor(out=r_e[:, 1, :], in0=sg[:, i, :], scalar=col("ln_w", i), in1=r_e[:, 1, :], op0=ALU.mult, op1=ALU.mult))
            st.link(V.scalar_tensor_tensor(out=r_e[:, 1, :], in0=r_e[:, 1, :], scalar=col("ln_b", i), in1=mix[:, 4 + i, :], op0=ALU.add, op1=ALU.add))
            V.tensor_tensor(mix[:, 4 + i, :], r_e[:, 1, :], rgate[:, i, :], ALU.mult).then_inc(S["r_done"], 1)

        ve.wait_ge(S["norm_sum"], 2)
        V.tensor_scalar(rs[:, 0:T1], bank(1), 1.0 / D, 1e-6, ALU.mult, ALU.add).then_inc(S["norm_var"], 1)
        ve.wait_ge(S["norm_std"], 2)
        st.link(V.reciprocal(rs[:, 0:T1], rs[:, 0:T1]))
        for g in range(KT):
            st.did(V.scalar_tensor_tensor(out=y1(g), in0=y1(g), scalar=small[:, 16 + g:17 + g], in1=rs[:, 0:T1], op0=ALU.mult, op1=ALU.mult))
        st.settle()
        for g in range(KT):
            V.tensor_tensor(h[:, g, META:T2], h[:, g, META:T2], y1(g), ALU.add).then_inc(S["x1_done"], 1)
        vector_block2(ve, st)
    ctx.close()


def _groups(w):
    k, m = w.shape
    return w.reshape(k // P, P, m // P, P).transpose(2, 1, 0, 3).reshape(m // P, P, k)


def _down(w):
    g = _groups(w)
    out = np.zeros((g.shape[0], 3, P, KT * P), w.dtype)
    for j in range(3):
        n = min(KT * P, FFN - j * KT * P)
        out[:, j, :, :n] = g[:, :, j * KT * P:j * KT * P + n]
    return out.reshape(-1, P, KT * P)


def _pad_cols(w, n):
    return np.concatenate([w, np.zeros((w.shape[0], n - w.shape[1]), w.dtype)], axis=1)


def _rope_split(w, heads):
    k = w.shape[0]
    return w.reshape(k, heads // 4, 4, 2, 32).transpose(0, 1, 3, 2, 4).reshape(k, heads * 64)


def _vec(v):
    return v.reshape(-1, P).T


def _layout(a):
    f = {k: np.asarray(v) for k, v in a.items()}
    one = {k: (v[0] if v.ndim and v.shape[0] == 1 else v) for k, v in f.items()}
    w_in = one["w_in"]
    cut = np.cumsum([512, 128, 128, 512, 768, 256, 128, 128, 256, 256])
    aq, ak, av, ag, rkv, rg, gq, gk, gv, gg = np.split(w_in, cut[:-1], axis=1)
    pairs = np.arange(8).reshape(2, 4).T.reshape(-1)

    def by_pair(w):
        return w.reshape(w.shape[0], 8, 64)[:, pairs].reshape(w.shape[0], 512)

    lora1 = np.concatenate([one["rwkv_w1"], one["rwkv_a1"]], axis=1)
    w_out = one["w_out"]
    w_out = np.concatenate([w_out[:512].reshape(8, 64, D)[pairs].reshape(512, D), w_out[512:]], axis=0)
    dsa = one["dsa_w_in_2"]
    dq, dk, dv, qi, ki, wi = np.split(dsa, np.cumsum([1024, 1024, 1024, 512, 64]), axis=1)
    qkv = one["da_w_qkv_2"]
    up, down = f["ffn_w_up_2"], f["ffn_w_down_2"]

    def mixed_up(w):
        return w.reshape(D, 2, FT, P).transpose(0, 2, 1, 3).reshape(D, 2 * FFN)

    streams = [
        one["ada_w"].T.reshape(N_ADA, P, D),
        _groups(lora1), _groups(_pad_cols(one["gla_gk1"], P)), _groups(rkv), _groups(gq), _groups(gk), _groups(gv),
        _groups(by_pair(aq)), _groups(ak), _groups(av), _groups(by_pair(ag)), _groups(rg), _groups(gg),
        _groups(w_out),
        _groups(_rope_split(qkv[:, :1024], 16)), _groups(_rope_split(qkv[:, 1024:2048], 16)), _groups(qkv[:, 2048:]),
        _groups(one["da_w_o_2"]),
        _groups(mixed_up(up[0])), _down(down[0]),
        _groups(_rope_split(qi, 8)), _groups(np.tile(ki[:, :32], (1, 4))), _groups(np.tile(ki[:, 32:], (1, 4))),
        _groups(_pad_cols(wi, P)),
        _groups(_rope_split(dq, 16)), _groups(_rope_split(dk, 16)), _groups(dv),
        _groups(one["dsa_w_o_2"]),
        _groups(mixed_up(up[1])), _down(down[1]),
    ]
    weights = np.concatenate(streams, axis=0)
    assert weights.shape[0] == N_SLOTS, (weights.shape, N_SLOTS)

    def block_cols(v):
        return v.reshape(2, FT, P).transpose(1, 0, 2).reshape(-1, P).T

    zero64 = np.zeros((64,), w_in.dtype)
    w2, a2, gk2 = one["rwkv_w2"], one["rwkv_a2"], one["gla_gk2"]
    lora2 = np.zeros((P, 5, P), w_in.dtype)
    for j in range(2):
        lora2[0:64, j] = w2[:, j * P:(j + 1) * P]
        lora2[64:P, 2 + j] = a2[:, j * P:(j + 1) * P]
    lora2[0:16, 4] = gk2
    parts = {
        "ada_b": _vec(one["ada_b"]), "norm_pre": _vec(one["norm_pre"]), "norm_post": _vec(one["norm_post"]),
        "mu_rkv": _vec(one["rwkv_mu_rkv"]), "mu_w": _vec(one["rwkv_mu_w"]), "mu_a": _vec(one["rwkv_mu_a"]),
        "w0": _vec(one["rwkv_w0"]), "a0": _vec(one["rwkv_a0"]), "k_k": _vec(one["rwkv_k_k"]), "k_a": _vec(one["rwkv_k_a"]),
        "r_k": _vec(one["rwkv_r_k"].reshape(-1)), "ln_w": _vec(one["rwkv_ln_w"]), "ln_b": _vec(one["rwkv_ln_b"]),
        "gk_b": _vec(one["gla_gk_b"]), "gla_norm": _vec(np.tile(one["gla_norm_w"], 2)),
        "da_norm": _vec(one["da_norm_2"]), "subln": _vec(one["da_subln_2"]), "dsa_norm": _vec(one["dsa_norm_2"]),
        "ffn_norm": np.concatenate([_vec(v) for v in f["ffn_norm_2"]], axis=1), "final_norm": _vec(f["final_norm_2"]),
        "conv_w": np.concatenate([block_cols(f["ffn_conv_w_2"][i, j]) for i in range(2) for j in range(3)], axis=1),
        "conv_b": np.concatenate([block_cols(f["ffn_conv_b_2"][i]) for i in range(2)], axis=1),
        "lam_q": np.stack([np.concatenate([one[f"da_lambda_q{i}_2"], zero64]) for i in (1, 2)], axis=1),
        "lam_k": np.stack([np.concatenate([one[f"da_lambda_k{i}_2"], zero64]) for i in (1, 2)], axis=1),
        "idx_norm": np.stack([np.tile(one["dsa_idx_k_norm_2"][:32], 4), np.tile(one["dsa_idx_k_norm_2"][32:], 4)], axis=1),
        "sinks": np.broadcast_to(one["attn_sinks"][None, :], (P, 8)),
    }
    columns = np.concatenate([parts[n] for n, _ in COLUMNS], axis=1)

    def tokens_last(x):
        return np.ascontiguousarray(x.T.reshape(KT, P, -1).transpose(1, 0, 2))

    return {
        "weights": weights, "cond": np.broadcast_to(f["c"][0], (P, D)), "columns": np.ascontiguousarray(columns), "xT": tokens_last(f["x"][0]), "metaT": tokens_last(f["meta_tokens_2"]),
        "lora1": np.ascontiguousarray(lora1.reshape(KT, P, P).transpose(1, 0, 2)), "lora2": lora2,
        **_constants(),
    }


def _constants():
    f32 = np.float32
    i = np.arange(P)
    eye = np.eye(P, dtype=f32)
    same64 = i[:, None] // 64 == i[None, :] // 64
    causal = np.where(i[None, :] <= i[:, None], 0.0, -BIG)
    dist = i[:, None] - np.arange(2 * P)[None, :] + P
    slopes = 2.0 ** (-np.arange(1, 9))
    alibi = np.where((dist >= 0) & (dist < P), 0.0, -BIG)[:, None, :] - 8.0 * slopes[None, :, None] * dist[:, None, :]
    j, q = i[:, None], i[None, :]
    strict = same64 & (j < q)
    incl = (j % 64) <= np.arange(64)[None, :]
    rmask = np.concatenate([strict, -1.0 * strict, incl, incl], axis=1)
    lvl = []
    for n in range(6):
        s = 1 << n
        lvl.append(-1.0 * ((j // (2 * s) == q // (2 * s)) & (j % (2 * s) < s) & (q % (2 * s) >= s)))
    gla = [((j // (2 * s) == q // (2 * s)) & (j % (2 * s) < s) & (q % (2 * s) >= s)) for s in (1 << np.arange(7))]
    gla.append(j == q)
    gblock = (i[:, None] // 32 == np.arange(256)[None, :] // 64)
    t = np.arange(T1)
    inv = (f32(10000.0) ** (-np.arange(0, 64, 2, dtype=f32) / f32(64))).astype(f32)
    ang = (np.arange(T2, dtype=f32)[:, None] * inv[None, :]).astype(f32)
    return {
        "ident": eye, "bones": same64.astype(f32), 
        "causalf": causal.astype(f32),
        "alibi": alibi.astype(f32), "rmask": rmask.astype(f32), "lvlmask": np.stack(lvl, axis=1).astype(f32),
        "glamask": np.stack(gla, axis=1).astype(f32), "gblock": gblock.astype(f32),
        "reset64": np.broadcast_to((t % 64 != 0).astype(f32), (P, T1)).copy(), "reset128": np.broadcast_to((t % P != 0).astype(f32), (P, T1)).copy(),
        "cosT": np.tile(np.cos(ang).T, (4, 1)).astype(f32), "sinT": np.tile(np.sin(ang).T, (4, 1)).astype(f32),
    }


def kernel(**inputs):
    import concourse.bacc as bacc
    from concourse.bass_utils import run_bass_kernel_spmd

    arrays = {f"in_{k}": np.ascontiguousarray(v) for k, v in _layout(inputs).items()}
    nc = bacc.Bacc("TRN2", target_bir_lowering=False, num_devices=1)
    ins = {k[3:]: nc.dram_tensor(k, v.shape, mybir.dt.from_np(v.dtype), kind="ExternalInput").ap() for k, v in arrays.items()}
    out_t = nc.dram_tensor("out_t", (P, KT, T1), mybir.dt.float32, kind="ExternalOutput").ap()
    build(nc, ins, out_t)
    r = run_bass_kernel_spmd(nc, [arrays], core_ids=[0])
    got = r.results[0]["out_t"]
    return np.ascontiguousarray(got.transpose(2, 1, 0).reshape(1, T1, D))
```
